# Optimizing a Trainium2 kernel written in Bass

```python
import math, functools
import jax, jax.numpy as jnp
from jax import lax
import numpy as np

D_MODEL = 1024
BATCH = 1
SEQ = 1024
DEPTH = 1
DEC_BATCH = 8
DEC_SEQ = 8
PAST_LEN = 512
PAGE_SIZE = 128

DA_HEADS = 4
DA_HD = 64
DA_VD = 2 * DA_HD
DA_WIDTH = DA_HEADS * DA_VD
DA_QK = DA_HEADS * 2 * DA_HD
RW_HEADS = 8
RW_HD = 64
RW_WIDTH = RW_HEADS * RW_HD
RW_W_RANK = 64
RW_A_RANK = 64
RW_G_RANK = 128
RW_PROJ = 3 * RW_WIDTH + RW_W_RANK + RW_A_RANK + RW_G_RANK
RW_GN_EPS = 64e-5
MIX_WIDTH = DA_WIDTH + RW_WIDTH
IN_PROJ = 2 * DA_QK + DA_WIDTH + RW_PROJ
PEER_HEADS = 8
PEER_NKEYS = 128
PEER_EXPERTS = PEER_NKEYS * PEER_NKEYS
PEER_KD = 128
PEER_TOPK = 16
PEER_CHUNK = 128
ROPE_THETA = 10000.0
Q_BLOCK = 128
NORM_EPS = 1e-6
NEG_INF = -1e30

kernel_name = 'hybrid_diffattn_rwkv7_peer_step'

def rms_norm(x, g):
    xf = x.astype(jnp.float32)
    y = xf * lax.rsqrt(jnp.mean(xf * xf, axis=-1, keepdims=True) + NORM_EPS)
    return (y * g.astype(jnp.float32)).astype(x.dtype)

def rope(x, pos):
    half = DA_HD // 2
    inv = ROPE_THETA ** (-jnp.arange(half, dtype=jnp.float32) / half)
    ang = pos.astype(jnp.float32)[:, None] * inv[None, :]
    cos = jnp.cos(ang)[None, :, None, None, :]
    sin = jnp.sin(ang)[None, :, None, None, :]
    xf = x.astype(jnp.float32)
    x1, x2 = xf[..., :half], xf[..., half:]
    return jnp.concatenate([x1 * cos - x2 * sin, x1 * sin + x2 * cos], axis=-1).astype(x.dtype)

def diff_attend(q, k, v, q_pos, k_pos, lam):
    s = jnp.einsum('bqhcd,bkhcd->bhcqk', q.astype(jnp.float32), k.astype(jnp.float32)) * (DA_HD ** -0.5)
    mask = k_pos[None, :] <= q_pos[:, None]
    p = jax.nn.softmax(jnp.where(mask, s, NEG_INF), axis=-1)
    a = p[:, :, 0] - lam * p[:, :, 1]
    return jnp.einsum('bhqk,bkhe->bqhe', a, v.astype(jnp.float32))

def attend_prompt(q, k, v, lam, pos):
    B, T = q.shape[0], q.shape[1]
    nb = T // Q_BLOCK
    qb = jnp.moveaxis(q.reshape(B, nb, Q_BLOCK, DA_HEADS, 2, DA_HD), 1, 0)
    pb = pos.reshape(nb, Q_BLOCK)
    ob = lax.map(lambda a: diff_attend(a[0], k, v, a[1], pos, lam), (qb, pb))
    return jnp.moveaxis(ob, 0, 1).reshape(B, T, DA_HEADS, DA_VD)

def attend_sample(q, k, v, lam, pos, k_cache, v_cache, page_table):
    Bd, T = q.shape[0], q.shape[1]
    past = page_table.shape[1] * PAGE_SIZE
    kp = k_cache[page_table].reshape(Bd, past, DA_HEADS, 2, DA_HD)
    vp = v_cache[page_table].reshape(Bd, past, DA_HEADS, DA_VD)
    k_all = jnp.concatenate([kp, k.astype(kp.dtype)], axis=1)
    v_all = jnp.concatenate([vp, v.astype(vp.dtype)], axis=1)
    k_pos = jnp.arange(past + T, dtype=jnp.int32)
    return diff_attend(q, k_all, v_all, pos, k_pos, lam)

def rwkv_time_mix(p, shift0, S0, mu, w0, w_up, a0, a_up, g_up, k_k, k_a, r_k, ln_w, ln_b):
    B, T, _ = p.shape
    W = RW_WIDTH
    p_prev = jnp.concatenate([shift0[:, None].astype(p.dtype), p[:, :-1]], axis=1)
    ps = p + (p_prev - p) * mu
    r, k, v = ps[..., :W], ps[..., W:2 * W], ps[..., 2 * W:3 * W]
    o = 3 * W
    xw = ps[..., o:o + RW_W_RANK]
    o += RW_W_RANK
    xa = ps[..., o:o + RW_A_RANK]
    o += RW_A_RANK
    xg = ps[..., o:o + RW_G_RANK]
    w = -jax.nn.softplus(-(w0 + jnp.tanh(xw) @ w_up)) - 0.5
    decay = jnp.exp(-jnp.exp(w.astype(jnp.float32)))
    a = jax.nn.sigmoid(a0 + xa @ a_up)
    g = jax.nn.sigmoid(xg) @ g_up
    heads = lambda t: t.reshape(B, T, RW_HEADS, RW_HD).astype(jnp.float32)
    r, k, v, a, decay = heads(r), heads(k), heads(v), heads(a), heads(decay)
    kk = k * k_k.reshape(RW_HEADS, RW_HD).astype(jnp.float32)
    kk = kk / jnp.maximum(jnp.sqrt(jnp.sum(kk * kk, axis=-1, keepdims=True)), 1e-12)
    k = k * (1.0 + (a - 1.0) * k_a.reshape(RW_HEADS, RW_HD).astype(jnp.float32))

    def step(S, inp):
        r_t, w_t, k_t, v_t, kk_t, b_t = inp
        sa = jnp.einsum('bhij,bhj->bhi', S, -kk_t)
        S = S * w_t[:, :, None, :] + sa[..., None] * b_t[:, :, None, :] + v_t[..., None] * k_t[:, :, None, :]
        return S, jnp.einsum('bhij,bhj->bhi', S, r_t)

    tm = lambda t: jnp.moveaxis(t, 1, 0)
    S, y = lax.scan(step, S0.astype(jnp.float32), (tm(r), tm(decay), tm(k), tm(v), tm(kk), tm(kk * a)))
    y = jnp.moveaxis(y, 0, 1)
    mean = jnp.mean(y, axis=-1, keepdims=True)
    var = jnp.mean(jnp.square(y - mean), axis=-1, keepdims=True)
    y = ((y - mean) * lax.rsqrt(var + RW_GN_EPS)).reshape(B, T, W)
    y = y * ln_w.astype(jnp.float32) + ln_b.astype(jnp.float32)
    bonus = jnp.sum(r * k * r_k.astype(jnp.float32), axis=-1, keepdims=True) * v
    y = (y + bonus.reshape(B, T, W)) * g.astype(jnp.float32)
    return y.astype(p.dtype), S, p[:, -1]

def peer_ffn(h, wq, sub_keys, u_tab, v_tab):
    B, T, D = h.shape
    n = B * T
    xt = h.reshape(n, D)
    n_pad = (-n) % PEER_CHUNK
    xc = jnp.pad(xt, ((0, n_pad), (0, 0))).reshape(-1, PEER_CHUNK, D)

    def chunk(xb):
        q = (xb @ wq).reshape(PEER_CHUNK, PEER_HEADS, 2, PEER_KD)
        s = jnp.einsum('thcd,hcnd->thcn', q.astype(jnp.float32), sub_keys.astype(jnp.float32))
        sv, si = lax.top_k(s, PEER_TOPK)
        cand = (sv[:, :, 0, :, None] + sv[:, :, 1, None, :]).reshape(PEER_CHUNK, PEER_HEADS, -1)
        cidx = (si[:, :, 0, :, None] * PEER_NKEYS + si[:, :, 1, None, :]).reshape(PEER_CHUNK, PEER_HEADS, -1)
        bv, bi = lax.top_k(cand, PEER_TOPK)
        eidx = jnp.take_along_axis(cidx, bi, axis=-1)
        gate = jax.nn.softmax(bv, axis=-1)
        u = u_tab[eidx]
        v = v_tab[eidx]
        act = jax.nn.gelu(jnp.einsum('thkd,td->thk', u, xb))
        return jnp.einsum('thk,thkd->td', (gate * act.astype(jnp.float32)).astype(xb.dtype), v)

    out = lax.map(chunk, xc).reshape(-1, D)[:n]
    return out.reshape(B, T, D)

def trunk_layer(x, pos, attend, wkv0, shift0, lam, lam_init, attn_norm, w_in, w_out, da_subln,
                rw_mu, rw_w0, rw_w_up, rw_a0, rw_a_up, rw_g_up, rw_k_k, rw_k_a, rw_r_k, rw_ln_w, rw_ln_b,
                ffn_norm, peer_wq, peer_sub_keys, peer_u, peer_v):
    B, T, _ = x.shape
    xn = rms_norm(x, attn_norm)
    proj = xn @ w_in
    q = rope(proj[..., :DA_QK].reshape(B, T, DA_HEADS, 2, DA_HD), pos)
    k = rope(proj[..., DA_QK:2 * DA_QK].reshape(B, T, DA_HEADS, 2, DA_HD), pos)
    v = proj[..., 2 * DA_QK:2 * DA_QK + DA_WIDTH].reshape(B, T, DA_HEADS, DA_VD)
    p_rw = proj[..., 2 * DA_QK + DA_WIDTH:]
    o_da = attend(q, k, v, lam)
    o_da = rms_norm(o_da, da_subln) * (1.0 - lam_init)
    o_rw, wkv, shift = rwkv_time_mix(p_rw, shift0, wkv0, rw_mu, rw_w0, rw_w_up, rw_a0, rw_a_up, rw_g_up,
                                     rw_k_k, rw_k_a, rw_r_k, rw_ln_w, rw_ln_b)
    mixed = jnp.concatenate([o_da.reshape(B, T, DA_WIDTH).astype(x.dtype), o_rw], axis=-1)
    h = x + mixed @ w_out
    h = h + peer_ffn(rms_norm(h, ffn_norm), peer_wq, peer_sub_keys, peer_u, peer_v)
    return h, k.reshape(B, T, DA_HEADS, 2 * DA_HD), v, wkv, shift

def setup_inputs(seed: int = 0) -> dict:
    key = jax.random.key(seed)
    ks = jax.random.split(key, 40)
    f32 = jnp.float32
    nrm = lambda kk, shape, s: jax.random.normal(kk, shape, f32) * s
    n_pages = PAST_LEN // PAGE_SIZE
    n_used = DEC_BATCH * n_pages
    n_pool = n_used + max(1, n_used // 4)
    page_table = jax.random.permutation(ks[0], n_pool)[:n_used].reshape(DEC_BATCH, n_pages).astype(jnp.int32)
    L = DEPTH
    return {
        'x_prompt': nrm(ks[1], (BATCH, SEQ, D_MODEL), 1.0),
        'x_sample': nrm(ks[2], (DEC_BATCH, DEC_SEQ, D_MODEL), 1.0),
        'cache_k': nrm(ks[3], (L, n_pool, PAGE_SIZE, DA_HEADS, 2 * DA_HD), 1.0),
        'cache_v': nrm(ks[4], (L, n_pool, PAGE_SIZE, DA_HEADS, DA_VD), 1.0),
        'state_wkv': nrm(ks[5], (L, DEC_BATCH, RW_HEADS, RW_HD, RW_HD), 0.5),
        'state_shift': nrm(ks[6], (L, DEC_BATCH, RW_PROJ), 1.0),
        'page_table': page_table,
        'attn_norm': 1.0 + nrm(ks[7], (L, D_MODEL), 0.01),
        'w_in': nrm(ks[8], (L, D_MODEL, IN_PROJ), D_MODEL ** -0.5),
        'w_out': nrm(ks[9], (L, MIX_WIDTH, D_MODEL), MIX_WIDTH ** -0.5),
        'da_lambda_q1': nrm(ks[10], (L, DA_HD), 0.1),
        'da_lambda_k1': nrm(ks[11], (L, DA_HD), 0.1),
        'da_lambda_q2': nrm(ks[12], (L, DA_HD), 0.1),
        'da_lambda_k2': nrm(ks[13], (L, DA_HD), 0.1),
        'da_subln': 1.0 + nrm(ks[14], (L, DA_VD), 0.01),
        'rw_mu': jax.random.uniform(ks[15], (L, RW_PROJ), f32, 0.0, 1.0),
        'rw_w0': jax.random.uniform(ks[16], (L, RW_WIDTH), f32, -6.0, 0.0),
        'rw_w_up': nrm(ks[17], (L, RW_W_RANK, RW_WIDTH), 0.5 * RW_W_RANK ** -0.5),
        'rw_a0': nrm(ks[18], (L, RW_WIDTH), 0.5),
        'rw_a_up': nrm(ks[19], (L, RW_A_RANK, RW_WIDTH), 0.5 * RW_A_RANK ** -0.5),
        'rw_g_up': nrm(ks[20], (L, RW_G_RANK, RW_WIDTH), RW_G_RANK ** -0.5),
        'rw_k_k': 0.85 + nrm(ks[21], (L, RW_WIDTH), 0.05),
        'rw_k_a': 1.0 + nrm(ks[22], (L, RW_WIDTH), 0.05),
        'rw_r_k': nrm(ks[23], (L, RW_HEADS, RW_HD), 0.1),
        'rw_ln_w': 1.0 + nrm(ks[24], (L, RW_WIDTH), 0.01),
        'rw_ln_b': nrm(ks[25], (L, RW_WIDTH), 0.01),
        'ffn_norm': 1.0 + nrm(ks[26], (L, D_MODEL), 0.01),
        'peer_wq': nrm(ks[27], (L, D_MODEL, PEER_HEADS * 2 * PEER_KD), D_MODEL ** -0.5),
        'peer_sub_keys': nrm(ks[28], (L, PEER_HEADS, 2, PEER_NKEYS, PEER_KD), PEER_KD ** -0.5),
        'peer_u': nrm(ks[29], (L, PEER_EXPERTS, D_MODEL), D_MODEL ** -0.5),
        'peer_v': nrm(ks[30], (L, PEER_EXPERTS, D_MODEL), PEER_HEADS ** -0.5),
        'final_norm': 1.0 + nrm(ks[31], (D_MODEL,), 0.01),
    }

def reference(x_prompt, x_sample, cache_k, cache_v, state_wkv, state_shift, page_table,
              attn_norm, w_in, w_out, da_lambda_q1, da_lambda_k1, da_lambda_q2, da_lambda_k2, da_subln,
              rw_mu, rw_w0, rw_w_up, rw_a0, rw_a_up, rw_g_up, rw_k_k, rw_k_a, rw_r_k, rw_ln_w, rw_ln_b,
              ffn_norm, peer_wq, peer_sub_keys, peer_u, peer_v, final_norm):
    B, T_p = x_prompt.shape[0], x_prompt.shape[1]
    T_s = x_sample.shape[1]
    past = page_table.shape[1] * PAGE_SIZE
    pos_p = jnp.arange(T_p, dtype=jnp.int32)
    pos_s = past + jnp.arange(T_s, dtype=jnp.int32)
    yp, ys = x_prompt, x_sample
    kp_l, vp_l, wp_l, sp_l, ks_l, vs_l, ws_l, ss_l = [], [], [], [], [], [], [], []
    for l in range(DEPTH):
        lam_init = 0.8 - 0.6 * math.exp(-0.3 * l)
        f = lambda t: t.astype(jnp.float32)
        lam = (jnp.exp(jnp.sum(f(da_lambda_q1[l]) * f(da_lambda_k1[l])))
               - jnp.exp(jnp.sum(f(da_lambda_q2[l]) * f(da_lambda_k2[l]))) + lam_init)
        shared = (attn_norm[l], w_in[l], w_out[l], da_subln[l], rw_mu[l], rw_w0[l], rw_w_up[l], rw_a0[l],
                  rw_a_up[l], rw_g_up[l], rw_k_k[l], rw_k_a[l], rw_r_k[l], rw_ln_w[l], rw_ln_b[l],
                  ffn_norm[l], peer_wq[l], peer_sub_keys[l], peer_u[l], peer_v[l])
        att_p = functools.partial(attend_prompt, pos=pos_p)
        att_s = functools.partial(attend_sample, pos=pos_s, k_cache=cache_k[l], v_cache=cache_v[l],
                                  page_table=page_table)
        wkv0_p = jnp.zeros((B, RW_HEADS, RW_HD, RW_HD), jnp.float32)
        shift0_p = jnp.zeros((B, RW_PROJ), x_prompt.dtype)
        yp, kp, vp, wp, sp = trunk_layer(yp, pos_p, att_p, wkv0_p, shift0_p, lam, lam_init, *shared)
        ys, ks_, vs, ws, ss = trunk_layer(ys, pos_s, att_s, state_wkv[l], state_shift[l], lam, lam_init, *shared)
        kp_l.append(kp)
        vp_l.append(vp)
        wp_l.append(wp.astype(x_prompt.dtype))
        sp_l.append(sp)
        ks_l.append(ks_.astype(cache_k.dtype))
        vs_l.append(vs.astype(cache_v.dtype))
        ws_l.append(ws.astype(state_wkv.dtype))
        ss_l.append(ss.astype(state_shift.dtype))
    y_prompt = rms_norm(yp, final_norm)
    y_sample = rms_norm(ys, final_norm)
    k_prompt = jnp.stack(kp_l)
    v_prompt = jnp.stack(vp_l)
    wkv_prompt = jnp.stack(wp_l)
    shift_prompt = jnp.stack(sp_l)
    k_sample = jnp.stack(ks_l)
    v_sample = jnp.stack(vs_l)
    wkv_sample = jnp.stack(ws_l)
    shift_sample = jnp.stack(ss_l)
    return (y_prompt, y_sample, k_prompt, v_prompt, wkv_prompt, shift_prompt, k_sample, v_sample, wkv_sample, shift_sample)


_drawn_inputs = setup_inputs


def setup_inputs(seed=0):
    import zlib

    import numpy as np

    out = dict(_drawn_inputs(seed))
    spreads = {}
    factors = {'attn_norm': 2.896,
     'da_lambda_q1': 6.027,
     'da_subln': 27.966,
     'rw_ln_w': 34.733,
     'rw_ln_b': 34.478,
     'ffn_norm': 20.401,
     'final_norm': 33.55}
    for name, (base, spread) in spreads.items():
        noise = np.random.default_rng([zlib.crc32(name.encode()), seed]).standard_normal(out[name].shape)
        drawn = base * np.exp(spread * noise) if base else spread * noise
        out[name] = __import__('jax').numpy.asarray(drawn.astype(out[name].dtype))
    for name, factor in factors.items():
        out[name] = (out[name] * factor).astype(out[name].dtype)
    return out
```

```python
from contextlib import ExitStack

import numpy as np

import concourse.bass as bass
from concourse import mybir

F32 = mybir.dt.float32
U32 = mybir.dt.uint32
I32 = mybir.dt.int32
ALU = mybir.AluOpType
ACT = mybir.ActivationFunctionType
AX_X = mybir.AxisListType.X

P = 128
D = 1024
KD = D // P
SEQ = 1024
PT = SEQ // P
NT = PT + 1
ROWS = NT * P
SB, ST = 8, 8
SROWS = SB * ST
PAST = 512
PAGE = 128
NPAGE = PAST // PAGE
H = 4
HD = 64
VD = 128
QK = H * 2 * HD
RH = 8
RD = 64
RW = RH * RD
RP = 3 * RW + 64 + 64 + 128
IN = 2 * QK + H * VD + RP
CH = 64
GN_EPS = 64e-5
EPS = 1e-6
NEG = -1e30
LAM0 = 0.2
PH = 8
NK = 128
TOPK = 16


ONE = 1


class Chain:

    def __init__(self, eng, sem, start=0, carrier=None, first=0):
        self.eng, self.sem, self.n, self.carrier = eng, sem, start + first, carrier

    def __call__(self, ins):
        ins.then_inc(self.sem, 1)
        self.n = self.n + 1
        self.eng.wait_ge(self.sem, self.n)
        if self.carrier is not None:
            carry(self.eng, self.carrier)


class Mem:

    def __init__(self, nc, ctx, tag):
        self.nc, self.ctx, self.tag, self.sems = nc, ctx, tag, []

    def sb(self, name, shape, dt=F32):
        return self.ctx.enter_context(self.nc.sbuf_tensor(f"{self.tag}_{name}", shape, dt))

    def ps(self, name, shape, dt=F32):
        return self.ctx.enter_context(self.nc.psum_tensor(f"{self.tag}_{name}", shape, dt))

    def sem(self, name, from_zero=False):
        sem = self.nc.alloc_semaphore(f"{self.tag}_{name}")
        if not from_zero:
            self.sems.append(sem)
        return sem

    def prime(self):
        engines = (self.nc.sync, self.nc.gpsimd, self.nc.tensor, self.nc.scalar, self.nc.vector)
        for n, s in enumerate(self.sems):
            engines[n % 5].sem_inc(s, ONE)
        self.nc.all_engine_barrier()


def carry(eng, carrier):
    eng.sem_inc(carrier, 1)


def rows(t, n=P):
    return bass.ds(t * P, n)


def in_projection(nc, T):
    NG = (IN + 511) // 512
    cols = [(n * 512, min(512, IN - n * 512)) for n in range(NG)]
    NB = 6
    with ExitStack() as ctx:
        m = Mem(nc, ctx, "ip")
        w = m.sb("w", [P, KD, IN])
        x = m.sb("x", [P, D])
        sq = m.sb("sq", [P, D])
        xs = m.sb("xs", [P, D])
        xT = m.sb("xT", [P, KD, P])
        g = m.sb("g", [P, KD])
        ident = m.sb("ident", [P, P])
        stat = m.sb("stat", [P, 4])
        rope = m.sb("rope", [P, 4, 32])
        prod = m.sb("prod", [P, 2, QK])
        swap = m.sb("swap", [P, 2, QK])
        qk = m.sb("qk", [P, 2, QK])
        v = m.sb("v", [P, QK])
        rw = m.sb("rw", [P, RP])
        psT = m.ps("psT", [P, KD, P])
        psG = m.ps("psG", [P, NB, 512])

        const_in = m.sem("const_in")
        w_in = [m.sem(f"w_in{n}") for n in range(NG)]
        x_in = m.sem("x_in")
        eps_set = m.sem("eps_set")
        summed = m.sem("summed")
        squared = m.sem("squared")
        scaled = m.sem("scaled")
        turned = m.sem("turned")
        xT_ready = m.sem("xT_ready")
        group_done = m.sem("group_done")
        rotated = m.sem("rotated")
        copied = m.sem("copied")
        stored = m.sem("stored")
        dve_chain = m.sem("dve_chain")
        m.prime()
        block = ctx.enter_context(nc.Block())

        def store(sp, t):
            sp.wait_ge(rotated, ONE + 2 * t + 2)
            sp.dma_start(T["q"][rows(t), :], qk[:, 0, :]).then_inc(stored, 16)
            sp.dma_start(T["k_all"][rows(t), :], qk[:, 1, :]).then_inc(stored, 16)
            sp.wait_ge(copied, ONE + (NG - 2) * (t + 1))
            sp.dma_start(T["v_all"][rows(t), :], v[:]).then_inc(stored, 16)
            sp.dma_start(T["p_all"][rows(t), :], rw[:]).then_inc(stored, 16)

        @block.sync
        def _(sp):
            sp.dma_start(x[:], T["x"][0:P, :]).then_inc(x_in, 16)
            sp.dma_start(rope[:], T["rope"][0:P, :, :]).then_inc(x_in, 16)
            sp.dma_start(g[:], T["attn_norm"]).then_inc(const_in, 16)
            sp.dma_start(ident[:], T["ident"]).then_inc(const_in, 16)
            for n, (c0, cn) in enumerate(cols):
                sp.dma_start(w[:, :, c0:c0 + cn],
                             T["w_in"].rearrange("(k p) n -> p k n", p=P)[:, :, c0:c0 + cn]).then_inc(w_in[n], 16)
            with sp.Fori(0, NT - 1) as t:
                sp.wait_ge(scaled, ONE + t + 1)
                sp.dma_start(x[:], T["x"][rows(t + 1), :]).then_inc(x_in, 16)
                sp.wait_ge(rotated, ONE + 2 * t + 2)
                sp.dma_start(rope[:], T["rope"][rows(t + 1), :, :]).then_inc(x_in, 16)
                store(sp, t)
            store(sp, NT - 1)
            sp.wait_ge(stored, ONE + 64 * NT)

        @block.scalar
        def _(act):
            act.wait_ge(eps_set, ONE + 1)
            with act.Fori(0, NT) as t:
                act.wait_ge(x_in, ONE + 32 * t + 32)
                act.wait_ge(scaled, ONE + t)
                nc.scalar.activation(sq[:], x[:], ACT.Square, accum_out=stat[:, 0:1]).then_inc(summed, 1)
                act.wait_ge(summed, ONE + t + 1)
                nc.scalar.activation(stat[:, 1:2], stat[:, 0:1], ACT.Sqrt, bias=stat[:, 3:4],
                                     scale=1.0 / D).then_inc(squared, 1)
                act.wait_ge(stored, ONE + 64 * t)
                for n in range(2, NG):
                    c0, cn = cols[n]
                    act.wait_ge(group_done, ONE + NG * t + n + 1)
                    dst = v[:] if n == 2 else rw[:, c0 - 3 * QK:c0 - 3 * QK + cn]
                    nc.scalar.activation(dst, psG[:, n % NB, 0:cn], ACT.Copy).then_inc(copied, 1)

        @block.vector
        def _(dve):
            nc.vector.memset(stat[:, 3:4], EPS).then_inc(eps_set, 1)
            K = 3
            with dve.Fori(0, NT) as t:
                chain = Chain(dve, dve_chain, K * t, first=ONE)
                dve.wait_ge(squared, ONE + t + 1)
                chain(nc.vector.reciprocal(stat[:, 2:3], stat[:, 1:2]))
                dve.wait_ge(turned, ONE + t)
                nc.vector.tensor_scalar(xs[:], x[:], stat[:, 2:3], None, ALU.mult).then_inc(scaled, 1)
                dve.wait_ge(group_done, ONE + NG * t)
                dve.wait_ge(const_in, ONE + 32)
                dve.wait_ge(turned, ONE + t + 1)
                nc.vector.tensor_tensor(xT[:], psT[:], g[:].unsqueeze(2).broadcast_to([P, KD, P]),
                                        ALU.mult).then_inc(xT_ready, 1)
                cos = rope[:, 0:2, :].unsqueeze(1).broadcast_to([P, 2 * H, 2, 32])
                for n in range(2):
                    dve.wait_ge(group_done, ONE + NG * t + n + 1)
                    src = psG[:, n, :].rearrange("p (h s d) -> p h s d", h=2 * H, s=2)
                    pr = prod[:, n, :].rearrange("p (h s d) -> p h s d", h=2 * H, s=2)
                    sw = swap[:, n, :].rearrange("p (h s d) -> p h s d", h=2 * H, s=2)
                    nc.vector.tensor_tensor(pr, src, cos, ALU.mult)
                    for s in range(2):
                        sin = rope[:, 2 + s, :].unsqueeze(1).broadcast_to([P, 2 * H, 32])
                        last = nc.vector.tensor_tensor(sw[:, :, s, :], src[:, :, 1 - s, :], sin, ALU.mult)
                    chain(last)
                    dve.wait_ge(stored, ONE + 64 * t)
                    nc.vector.tensor_tensor(qk[:, n, :], prod[:, n, :], swap[:, n, :], ALU.add).then_inc(rotated, 1)
                dve.wait_ge(rotated, ONE + 2 * t + 2)

        @block.tensor
        def _(pe):
            pe.wait_ge(const_in, ONE + 32)
            with pe.Fori(0, NT) as t:
                pe.wait_ge(scaled, ONE + t + 1)
                pe.wait_ge(xT_ready, ONE + t)
                for k in range(KD):
                    last = nc.tensor.transpose(psT[:, k, :], xs[:, k * P:(k + 1) * P], ident[:])
                last.then_inc(turned, 1)
                pe.wait_ge(xT_ready, ONE + t + 1)
                for n, (c0, cn) in enumerate(cols):
                    if n < 2:
                        pe.wait_ge(rotated, ONE + 2 * t)
                        pe.wait_ge(copied, ONE + (NG - 2) * t)
                    elif n >= NB:
                        pe.wait_ge(rotated, ONE + 2 * t + n - NB + 1)
                    else:
                        pe.wait_ge(copied, ONE + (NG - 2) * t)
                    pe.wait_ge(w_in[n], ONE + 16)
                    for k in range(KD):
                        last = nc.tensor.matmul(psG[:, n % NB, 0:cn], xT[:, k, :], w[:, k, c0:c0 + cn],
                                                start=(k == 0), stop=(k == KD - 1))
                    last.then_inc(group_done, 1)

def attention(nc, T):
    SC = HD ** -0.5
    NU = PT * H
    KEYS = PAST + ST
    with ExitStack() as ctx:
        m = Mem(nc, ctx, "at")
        ident = m.sb("ident", [P, P])
        causal = m.sb("causal", [P, P])
        lam_in = m.sb("lam_in", [P, 4, HD])
        lam_pr = m.sb("lam_pr", [P, 2, HD])
        lam = m.sb("lam", [P, 4])
        subln = m.sb("subln", [P, VD])
        stat = m.sb("stat", [P, 1])
        qs = m.sb("q", [P, QK])
        ks = m.sb("k", [P, QK])
        qT = m.sb("qT", [P, H, P])
        kT = m.sb("kT", [P, H, SEQ])
        vs = m.sb("v", [P, PT, H * VD])
        prob = m.sb("prob", [P, 2, SEQ])
        A = m.sb("A", [P, SEQ])
        AT = m.sb("AT", [P, SEQ])
        mx = m.sb("mx", [P, 2])
        sums = m.sb("sums", [P, 2])
        inv = m.sb("inv", [P, 4])
        sq = m.sb("sq", [P, H, VD])
        hst = m.sb("hst", [P, 4, H])
        o = m.sb("o", [P, H, VD])
        pages = m.sb("pages", [P, SB * NPAGE], I32)
        pagef = m.sb("pagef", [P, SB * NPAGE])
        prow = m.sb("prow", [P, 1])
        pidx = m.sb("pidx", [P, SB * NPAGE], U32)
        kp = [m.sb(f"kp{i}", [P, NPAGE, QK]) for i in range(2)]
        vp = [m.sb(f"vp{i}", [P, NPAGE, H * VD]) for i in range(2)]
        vnew = m.sb("vnew", [ST, SB, H * VD])
        QB = m.sb("QB", [P, SB, H, 4, ST])
        kpT = m.sb("kpT", [P, H, PAST])
        knT = m.sb("knT", [P, H, SROWS])
        new_mask = m.sb("new_mask", [P, ST])
        coef = m.sb("coef", [P, 2])
        pick = m.sb("pick", [P, 4 * ST])
        pickw = m.sb("pickw", [P, 4 * ST])
        ATs = m.sb("ATs", [P, NPAGE + 1, 4 * ST])
        wrow = m.sb("wrow", [P, 2])
        coefl = m.sb("coefl", [P, 1])
        oT = m.sb("oT", [P, H, SROWS])
        psA = m.ps("psA", [P, 2, SEQ])
        psX = m.ps("psX", [P, SEQ])
        psO = m.ps("psO", [P, H, VD])
        psK = m.ps("psK", [P, H, P])

        const_in = m.sem("const_in")
        page_in = m.sem("page_in")
        pidx_ready = m.sem("pidx_ready")
        q_in = m.sem("q_in")
        k_in = m.sem("k_in")
        v_in = [m.sem(f"v_in{i}") for i in range(PT + 1)]
        kp_in = [m.sem(f"kp_in{i}") for i in range(2)]
        vp_in = [m.sem(f"vp_in{i}") for i in range(2)]
        lam_chain = m.sem("lam_chain")
        lam_exp = m.sem("lam_exp")
        lam_ready = m.sem("lam_ready")
        turned = m.sem("turned")
        turn_copied = m.sem("turn_copied")
        scored = m.sem("scored")
        chain_s = m.sem("chain")
        max_ready = m.sem("max_ready")
        exp_done = m.sem("exp_done")
        A_ready = m.sem("A_ready")
        A_turned = m.sem("A_turned")
        AT_ready = m.sem("AT_ready")
        pv_done = m.sem("pv_done")
        o_squared = m.sem("o_squared")
        o_sums = m.sem("o_sums")
        o_root = m.sem("o_root")
        o_ready = m.sem("o_ready")
        o_stored = m.sem("o_stored")
        QB_zero = m.sem("QB_zero")
        kp_turned = m.sem("kp_turned")
        kp_copied = m.sem("kp_copied")
        pickw_ready = m.sem("pickw_ready")
        pages_used = m.sem("pages_used")
        ATs_done = m.sem("ATs_done")
        ATs_copied = m.sem("ATs_copied")
        oT_copied = m.sem("oT_copied")
        block = ctx.enter_context(nc.Block())
        NCONST = 11

        def store(sp, t):
            n = P if t < PT else SROWS
            sp.wait_ge(o_ready, t + 1)
            sp.dma_start(T["mixed"][t * P:t * P + n, 0:H * VD], o[0:n].rearrange("p h d -> p (h d)")
                         ).then_inc(o_stored, 16)

        @block.sync
        def _(sp):
            for n, name in enumerate(("da_lambda_q1", "da_lambda_k1", "da_lambda_q2", "da_lambda_k2")):
                sp.dma_start(lam_in[:, n, :], T[name].partition_broadcast(P)).then_inc(const_in, 16)
            for dst, name in ((ident, "ident"), (causal, "causal"), (new_mask, "new_mask"), (coef, "coef"),
                              (pick, "pick"), (prow, "prow")):
                sp.dma_start(dst[:], T[name]).then_inc(const_in, 16)
            sp.dma_start(subln[:], T["da_subln"].partition_broadcast(P)).then_inc(const_in, 16)
            sp.dma_start(pages[:], T["page_table"].broadcast_to([P, SB * NPAGE])).then_inc(page_in, 16)
            for t in range(NT):
                if t:
                    sp.wait_ge(turned, 2 * t)
                sp.dma_start(ks[:], T["k_all"][t * P:(t + 1) * P, :]).then_inc(k_in, 16)
                sp.dma_start(qs[:], T["q"][t * P:(t + 1) * P, :]).then_inc(q_in, 16)
                if t < PT:
                    sp.dma_start(vs[:, t, :], T["v_all"][t * P:(t + 1) * P, :]).then_inc(v_in[t], 16)
                else:
                    sp.dma_start(vnew[:], T["v_all"][SEQ:SEQ + SROWS, :].rearrange("(b s) n -> s b n", s=ST)
                                 ).then_inc(v_in[t], 16)
                if t:
                    store(sp, t - 1)
            store(sp, PT)
            sp.wait_ge(o_stored, 16 * NT)

        @block.gpsimd
        def _(pool):
            nc.gpsimd.memset(QB[:], 0.0).then_inc(QB_zero, 1)
            pool.wait_ge(pidx_ready, 1)
            for b in range(SB):
                if b >= 2:
                    pool.wait_ge(pages_used, b - 1)
                for dst, src, s in ((kp, "cache_k", kp_in), (vp, "cache_v", vp_in)):
                    for g in range(NPAGE):
                        pool.indirect_dma_start(dst[b % 2][:, g, :], None, T[src], bass.IndirectOffsetOnAxis(
                            ap=pidx[:, b * NPAGE + g:b * NPAGE + g + 1], axis=0)).then_inc(s[b % 2], 16)

        @block.tensor
        def _(pe):
            pe.wait_ge(const_in, 16 * NCONST)

            def turn(t):
                for n, (src, s) in enumerate(((ks, k_in), (qs, q_in))):
                    pe.wait_ge(s, 16 * (t + 1))
                    pe.wait_ge(turn_copied, 2 * t + n)
                    for h in range(H):
                        last = nc.tensor.transpose(psK[:, h, :], src[:, h * P:(h + 1) * P], ident[:])
                    last.then_inc(turned, 1)

            def score(u):
                t, h = u // H, u % H
                pe.wait_ge(turn_copied, 2 * t + 2)
                if u:
                    pe.wait_ge(exp_done, 2 * u)
                n = (t + 1) * P
                for c in range(2):
                    for k0 in range(0, n, 512):
                        kn = min(512, n - k0)
                        last = nc.tensor.matmul(psA[:, c, k0:k0 + kn], qT[c * HD:(c + 1) * HD, h, :],
                                                kT[c * HD:(c + 1) * HD, h, k0:k0 + kn], start=True, stop=True)
                    last.then_inc(scored, 1)

            def value(u):
                t, h = u // H, u % H
                pe.wait_ge(A_ready, u + 1)
                if u:
                    pe.wait_ge(AT_ready, u)
                for b in range(t + 1):
                    last = nc.tensor.transpose(psX[:, b * P:(b + 1) * P], A[:, b * P:(b + 1) * P], ident[:])
                last.then_inc(A_turned, 1)
                pe.wait_ge(AT_ready, u + 1)
                if h == 0 and t:
                    pe.wait_ge(o_ready, t)
                if h == 0:
                    pe.wait_ge(v_in[t], 16)
                for b in range(t + 1):
                    last = nc.tensor.matmul(psO[:, h, :], AT[:, b * P:(b + 1) * P], vs[:, b, h * VD:(h + 1) * VD],
                                            start=(b == 0), stop=(b == t))
                last.then_inc(pv_done, 1)

            turn(0)
            score(0)
            for u in range(NU):
                if (u + 1) % H == 0 and u + 1 <= NU:
                    turn((u + 1) // H)
                if u + 1 < NU:
                    score(u + 1)
                value(u)
            pe.wait_ge(turn_copied, 2 * NT)
            pe.wait_ge(v_in[PT], 16)
            for b in range(SB):
                pe.wait_ge(kp_in[b % 2], 16 * NPAGE * (b // 2 + 1))
                for hp in range(2):
                    pe.wait_ge(kp_copied, 2 * b + hp)
                    if b == 0 and hp == 0:
                        pe.wait_ge(AT_ready, NU)
                    for h in range(2):
                        for g in range(NPAGE):
                            hh = 2 * hp + h
                            last = nc.tensor.transpose(psX[:, (h * NPAGE + g) * P:(h * NPAGE + g + 1) * P],
                                                       kp[b % 2][:, g, hh * P:(hh + 1) * P], ident[:])
                    last.then_inc(kp_turned, 1)
                pe.wait_ge(kp_copied, 2 * b + 2)
                pe.wait_ge(exp_done, 2 * NU + b)
                for h in range(H):
                    lhs = QB[:, b, h, :, :].rearrange("p c t -> p (c t)")
                    nc.tensor.matmul(psA[32 * h:32 * h + 32, 0, 0:PAST], lhs, kpT[:, h, :], start=True, stop=True)
                for h in range(H):
                    lhs = QB[:, b, h, :, :].rearrange("p c t -> p (c t)")
                    last = nc.tensor.matmul(psA[32 * h:32 * h + 32, 0, PAST:KEYS], lhs,
                                            knT[:, h, b * ST:(b + 1) * ST], start=True, stop=True)
                last.then_inc(scored, 1)
                pe.wait_ge(pickw_ready, b + 1)
                pe.wait_ge(ATs_copied, b)
                for g in range(NPAGE):
                    nc.tensor.matmul(psK[:, 0, g * 32:(g + 1) * 32], prob[:, 0, g * P:(g + 1) * P], pickw[:],
                                     start=True, stop=True)
                nc.tensor.matmul(psK[0:ST, 1, 0:32], prob[:, 0, PAST:KEYS], pickw[:],
                                 start=True, stop=True).then_inc(ATs_done, 1)
                pe.wait_ge(ATs_copied, b + 1)
                pe.wait_ge(vp_in[b % 2], 16 * NPAGE * (b // 2 + 1))
                if b == 0:
                    pe.wait_ge(o_ready, PT)
                for h in range(H):
                    out = psO[:, h, b * ST:(b + 1) * ST]
                    for g in range(NPAGE):
                        nc.tensor.matmul(out, vp[b % 2][:, g, h * VD:(h + 1) * VD], ATs[:, g, h * ST:(h + 1) * ST],
                                         start=(g == 0), stop=False)
                    last = nc.tensor.matmul(out, vnew[:, b, h * VD:(h + 1) * VD],
                                            ATs[0:ST, NPAGE, h * ST:(h + 1) * ST], start=False, stop=True)
                last.then_inc(pages_used, 1)
            pe.wait_ge(oT_copied, 1)
            for h in range(H):
                last = nc.tensor.transpose(psK[0:SROWS, h, :], oT[:, h, :], ident[:])
            last.then_inc(pv_done, 1)

        @block.scalar
        def _(act):
            act.wait_ge(lam_chain, 1)
            nc.scalar.activation(lam[:, 0:2], lam[:, 2:4], ACT.Exp).then_inc(lam_exp, 1)

            def expo(u):
                n = (u // H + 1) * P
                for c in range(2):
                    act.wait_ge(max_ready, 2 * u + c + 1)
                    if u:
                        act.wait_ge(A_ready, u)
                    nc.scalar.activation(prob[:, c, 0:n], psA[:, c, 0:n], ACT.Exp, bias=mx[:, c:c + 1],
                                         accum_out=sums[:, c:c + 1]).then_inc(exp_done, 1)

            def copy_AT(u):
                n = (u // H + 1) * P
                act.wait_ge(A_turned, u + 1)
                if u:
                    act.wait_ge(pv_done, u)
                nc.scalar.activation(AT[:, 0:n], psX[:, 0:n], ACT.Copy).then_inc(AT_ready, 1)

            def square(t, src, R):
                nc.scalar.activation(sq[0:R], src, ACT.Square).then_inc(o_squared, 1)
                act.wait_ge(o_sums, t + 1)
                nc.scalar.activation(hst[0:R, 1, :], hst[0:R, 0, :], ACT.Sqrt, bias=stat[0:R],
                                     scale=1.0 / VD).then_inc(o_root, 1)

            for u in range(NU):
                expo(u)
                copy_AT(u)
                if u % H == H - 1:
                    act.wait_ge(pv_done, u + 1)
                    square(u // H, psO[:], P)
            for b in range(SB):
                for hp in range(2):
                    act.wait_ge(kp_turned, 2 * b + hp + 1)
                    if b:
                        act.wait_ge(scored, 2 * NU + b)
                    nc.scalar.activation(kpT[:, 2 * hp:2 * hp + 2, :].rearrange("p h k -> p (h k)"), psX[:],
                                         ACT.Copy).then_inc(kp_copied, 1)
                act.wait_ge(max_ready, 2 * NU + b + 1)
                act.wait_ge(ATs_done, b)
                act.wait_ge(A_ready, NU)
                nc.scalar.activation(prob[:, 0, 0:KEYS], psA[:, 0, 0:KEYS], ACT.Exp, bias=mx[:, 0:1],
                                     accum_out=sums[:, 0:1]).then_inc(exp_done, 1)
            act.wait_ge(pv_done, NU + 1)
            square(PT, psK[0:SROWS], SROWS)

        @block.vector
        def _(dve):
            chain = Chain(dve, chain_s)
            chain(nc.vector.memset(stat[:], EPS))
            dve.wait_ge(const_in, 16 * NCONST)
            for n in range(2):
                nc.vector.tensor_tensor_reduce(lam_pr[:, n, :], lam_in[:, 2 * n, :], lam_in[:, 2 * n + 1, :], 1.0, 0.0,
                                               ALU.mult, ALU.add, lam[:, 2 + n:3 + n])
            nc.vector.memset(hst[:], 0.0).then_inc(lam_chain, 1)
            dve.wait_ge(lam_exp, 1)
            chain(nc.vector.tensor_tensor(lam[:, 2:3], lam[:, 1:2], lam[:, 0:1], ALU.subtract))
            chain(nc.vector.tensor_scalar(lam[:, 3:4], lam[:, 2:3], LAM0, None, ALU.subtract))
            nc.vector.scalar_tensor_tensor(coefl[:], coef[:, 1:2], lam[:, 3:4], coef[:, 0:1], ALU.mult,
                                           ALU.add).then_inc(lam_ready, 1)
            dve.wait_ge(page_in, 16)
            chain(nc.vector.tensor_copy(pagef[:], pages[:]))
            nc.vector.tensor_scalar(pidx[:], pagef[:], float(PAGE), prow[:, 0:1], ALU.mult,
                                    ALU.add).then_inc(pidx_ready, 1)

            def copy_turn(t):
                dve.wait_ge(turned, 2 * t + 1)
                if t < PT:
                    nc.vector.tensor_copy(kT[:, :, t * P:(t + 1) * P], psK[:]).then_inc(turn_copied, 1)
                    dve.wait_ge(turned, 2 * t + 2)
                    if t:
                        dve.wait_ge(scored, 2 * H * t)
                    nc.vector.tensor_scalar(qT[:], psK[:], SC, None, ALU.mult).then_inc(turn_copied, 1)
                else:
                    nc.vector.tensor_copy(knT[:], psK[:, :, 0:SROWS]).then_inc(turn_copied, 1)
                    dve.wait_ge(turned, 2 * t + 2)
                    dve.wait_ge(QB_zero, 1)
                    for c in range(2):
                        for h in range(H):
                            part = slice(c * HD, (c + 1) * HD)
                            last = nc.vector.tensor_scalar(
                                QB[part, :, h, c, :], psK[part, h, 0:SROWS].rearrange("p (b t) -> p b t", t=ST), SC, None,
                                ALU.mult)
                    last.then_inc(turn_copied, 1)

            def maxima(u):
                n = (u // H + 1) * P
                for c in range(2):
                    dve.wait_ge(scored, 2 * u + c + 1)
                    chain(nc.vector.tensor_tensor(psA[:, c, n - P:n], psA[:, c, n - P:n], causal[:], ALU.add))
                    dve.wait_ge(exp_done, 2 * u)
                    chain(nc.vector.reduce_max(inv[:, 2:3], psA[:, c, 0:n], axis=AX_X))
                    nc.vector.tensor_scalar(mx[:, c:c + 1], inv[:, 2:3], -1.0, None, ALU.mult).then_inc(max_ready, 1)
                    dve.wait_ge(max_ready, 2 * u + c + 1)

            def combine(u):
                n = (u // H + 1) * P
                dve.wait_ge(exp_done, 2 * u + 2)
                chain(nc.vector.reciprocal(inv[:, 0:2], sums[:]))
                chain(nc.vector.tensor_tensor(inv[:, 3:4], inv[:, 1:2], lam[:, 3:4], ALU.mult))
                chain(nc.vector.tensor_scalar(prob[:, 1, 0:n], prob[:, 1, 0:n], inv[:, 3:4], None, ALU.mult))
                if u:
                    dve.wait_ge(A_turned, u)
                nc.vector.scalar_tensor_tensor(A[:, 0:n], prob[:, 0, 0:n], inv[:, 0:1], prob[:, 1, 0:n], ALU.mult,
                                               ALU.add).then_inc(A_ready, 1)

            def norm(t, src, R):
                dve.wait_ge(o_squared, t + 1)
                nc.vector.reduce_sum(hst[0:R, 0, :], sq[0:R], axis=AX_X).then_inc(o_sums, 1)
                dve.wait_ge(o_root, t + 1)
                chain(nc.vector.reciprocal(hst[0:R, 2, :], hst[0:R, 1, :]))
                dve.wait_ge(o_stored, 16 * t)
                chain(nc.vector.tensor_tensor(o[0:R], src, hst[0:R, 2, :].unsqueeze(2).broadcast_to([R, H, VD]),
                                              ALU.mult))
                nc.vector.scalar_tensor_tensor(o[0:R], o[0:R], 1.0 - LAM0,
                                               subln[0:R].unsqueeze(1).broadcast_to([R, H, VD]), ALU.mult,
                                               ALU.mult).then_inc(o_ready, 1)

            dve.wait_ge(lam_ready, 1)
            copy_turn(0)
            maxima(0)
            for u in range(NU):
                combine(u)
                if (u + 1) % H == 0:
                    copy_turn((u + 1) // H)
                if u + 1 < NU:
                    maxima(u + 1)
                if u % H == H - 1:
                    norm(u // H, psO[:], P)
            for b in range(SB):
                dve.wait_ge(scored, 2 * NU + b + 1)
                chain(nc.vector.tensor_tensor(psA[:, 0, PAST:KEYS], psA[:, 0, PAST:KEYS], new_mask[:], ALU.add))
                dve.wait_ge(exp_done, 2 * NU + b)
                chain(nc.vector.reduce_max(inv[:, 2:3], psA[:, 0, 0:KEYS], axis=AX_X))
                nc.vector.tensor_scalar(mx[:, 0:1], inv[:, 2:3], -1.0, None, ALU.mult).then_inc(max_ready, 1)
                dve.wait_ge(exp_done, 2 * NU + b + 1)
                chain(nc.vector.reciprocal(wrow[:, 0:1], sums[:, 0:1]))
                chain(nc.vector.tensor_tensor(wrow[:, 1:2], wrow[:, 0:1], coefl[:], ALU.mult))
                dve.wait_ge(ATs_done, b)
                nc.vector.tensor_scalar(pickw[:], pick[:], wrow[:, 1:2], None, ALU.mult).then_inc(pickw_ready, 1)
                dve.wait_ge(ATs_done, b + 1)
                dve.wait_ge(pages_used, b)
                nc.vector.tensor_copy(ATs[:, 0:NPAGE, :], psK[:, 0, :].rearrange("p (g t) -> p g t", g=NPAGE))
                nc.vector.tensor_copy(ATs[0:ST, NPAGE, :], psK[0:ST, 1, 0:32]).then_inc(ATs_copied, 1)
            dve.wait_ge(pages_used, SB)
            nc.vector.tensor_copy(oT[:], psO[:, :, 0:SROWS]).then_inc(oT_copied, 1)
            norm(PT, psK[0:SROWS], SROWS)

class CountedChain(Chain):

    def __init__(self, eng, sem, times, per):
        super().__init__(eng, sem, times * per, first=ONE)
        self.per, self.calls = per, 0

    def __call__(self, ins):
        super().__call__(ins)
        self.calls += 1

    def end(self, last=False):
        if not last and self.calls != self.per:
            raise ValueError(f"the chain has {self.calls} instructions a turn, not {self.per}")


def time_mixing(nc, T):
    W = RW
    LEVELS = 6
    SLEVELS = 3
    NPAIR = RH // 2
    with ExitStack() as ctx:
        m = Mem(nc, ctx, "tm")
        ident = m.sb("ident", [P, P])
        eye = m.sb("eye", [P, CH])
        vec = {n: m.sb(n, [P, W]) for n in ("w0", "a0", "k_k", "k_a", "r_k", "ln_w", "ln_b")}
        mu = m.sb("mu", [P, RP])
        wa_up = m.sb("wa_up", [P, W])
        g_up = m.sb("g_up", [P, W])
        cum_l = [m.sb("cum_p", [P, P]), m.sb("cum_s", [P, P])]
        tot = [m.sb("tot_p", [P, 4]), m.sb("tot_s", [P, SB])]
        tri = [m.sb("tri_p", [P, 2, CH]), m.sb("tri_s", [P, 2, CH])]
        lev = m.sb("lev", [P, LEVELS, CH])
        seq_of = m.sb("seq_of", [P, SB, CH])
        seq_row = m.sb("seq_row", [P, SB])
        stat = m.sb("stat", [P, 1])
        p = m.sb("p", [P, RP])
        prev = m.sb("prev", [P, RP])
        ps = m.sb("ps", [P, RP])
        lo = m.sb("lo", [P, 2 * P])
        loT = m.sb("loT", [P, 2, P])
        z = m.sb("z", [P, W])
        lw = m.sb("lw", [P, W])
        a = m.sb("a", [P, W])
        g = m.sb("g", [P, W])
        kk = m.sb("kk", [P, W])
        k2 = m.sb("k2", [P, W])
        bb = m.sb("bb", [P, W])
        e_in = m.sb("e_in", [P, W])
        e_out = m.sb("e_out", [P, W])
        e_bef = m.sb("e_bef", [P, W])
        sq = m.sb("sq", [P, W])
        rt = m.sb("rt", [P, W])
        kq = m.sb("kq", [P, W])
        bt = m.sb("bt", [P, W])
        kt = m.sb("kt", [P, W])
        ep = m.sb("ep", [P, NPAIR, SB])
        hs = m.sb("hs", [P, 8, RH])
        qrT = m.sb("qrT", [P, 2, NPAIR, P])
        bkT = m.sb("bkT", [P, 2, NPAIR, P])
        AB = m.sb("AB", [P, RH, 2, CH])
        AK = m.sb("AK", [P, RH, 2, CH])
        ML = m.sb("ML", [P, LEVELS, RH * CH])
        Tn = m.sb("Tn", [P, RH, CH])
        Tt = m.sb("Tt", [P, RH, CH])
        X = m.sb("X", [P, RH, CH])
        state = m.sb("state", [P, NPAIR, RD])
        Sp = m.sb("Sp", [P, NPAIR, 2, RD])
        R_ = m.sb("R", [P, W])
        SA = m.sb("SA", [P, W])
        yc = m.sb("yc", [P, W])
        bon = m.sb("bon", [P, W])
        out = m.sb("out", [P, W])
        sstate = m.sb("sstate", [P, NPAIR, SB, RD])
        sdiag = m.sb("sdiag", [P, NPAIR, SB, 2, RD])
        big = m.sb("big", [P, 2 * NPAIR, SB, CH])
        PS = m.ps("PS", [P, 8, 512])

        names = """const_in p_in prev_in sstate_in eps_set prev_set mixed kk_scaled lo_ready lo_sig lo_turned lo_copied
            lora_done z_ready z_exp lw_ready za_ready a_tanh g_copied cum_done e_ready bef_ready bef_exp
            kk_squared kk_sum kk_root scaled_ready turned_ready turned_copied pair_done masked level_masks
            x_done x_copied y_done t_ready sp_ready r_done r_copied sa_done sa_copied yy_done st_done
            state_ready y_centered y_squared y_sum y_root y_scaled bonus_in out_ready out_stored state_stored chain pool_chain
            big_ready rk_ready carrier""".split()
        s = {n: m.sem(n) for n in names}
        NCONST = 1 + len(vec) + 3 + 11
        m.prime()
        block = ctx.enter_context(nc.Block())

        SBANK = (0, 1, 2, 7)

        def heads(ap, n=RH):
            return ap.rearrange("p (h d) -> p h d", h=n)

        @block.sync
        def _(sp):
            sp.dma_start(p[:], T["p_all"][0:P, :]).then_inc(s["p_in"], 16)
            sp.wait_ge(s["prev_set"], ONE + 1)
            sp.dma_start(prev[1:P, :], T["p_all"][0:P - 1, :]).then_inc(s["prev_in"], 16)
            sp.dma_start(mu[:], T["rw_mu"].partition_broadcast(P)).then_inc(s["const_in"], 16)
            for n in vec:
                sp.dma_start(vec[n][:], T["rw_" + n].partition_broadcast(P)).then_inc(s["const_in"], 16)
            sp.dma_start(wa_up[0:64, :], T["rw_w_up"]).then_inc(s["const_in"], 16)
            sp.dma_start(wa_up[64:128, :], T["rw_a_up"]).then_inc(s["const_in"], 16)
            sp.dma_start(g_up[:], T["rw_g_up"]).then_inc(s["const_in"], 16)
            for dst, n in ((ident, "ident"), (eye, "eye"), (cum_l[0], "cum_p"), (cum_l[1], "cum_s"), (tot[0], "tot_p"),
                           (tot[1], "tot_s"), (tri[0], "tri_p"), (tri[1], "tri_s"), (lev, "levels"),
                           (seq_of, "seq_of"), (seq_row, "seq_row")):
                sp.dma_start(dst[:], T[n]).then_inc(s["const_in"], 16)
            sp.dma_start(sstate[:], T["state"]).then_inc(s["sstate_in"], 16)
            sp.dma_start(sdiag[:], T["state_diag"]).then_inc(s["sstate_in"], 16)

            def store(t, n):
                sp.wait_ge(s["out_ready"], ONE + t + 1)
                sp.dma_start(T["mixed"][rows(t, n), RW:2 * RW], out[0:n, :]).then_inc(s["out_stored"], 16)

            with sp.Fori(0, PT - 1) as t:
                sp.wait_ge(s["mixed"], ONE + t + 1)
                sp.dma_start(p[:], T["p_all"][rows(t + 1), :]).then_inc(s["p_in"], 16)
                sp.dma_start(prev[:], T["p_all"][bass.ds((t + 1) * P - 1, P), :]).then_inc(s["prev_in"], 16)
                store(t, P)
            sp.wait_ge(s["mixed"], ONE + PT)
            sp.dma_start(p[0:SROWS], T["p_all"][SEQ:SEQ + SROWS, :]).then_inc(s["p_in"], 16)
            sp.dma_start(prev[0:SROWS], T["p_all"][SEQ - 1:SEQ + SROWS - 1, :]).then_inc(s["prev_in"], 16)
            sp.wait_ge(s["prev_in"], ONE + 16 * NT)
            sp.dma_start(prev[0:SROWS:ST, :], T["shift"]).then_inc(s["prev_in"], 16)
            store(PT - 1, P)
            sp.wait_ge(s["state_ready"], ONE + 2 * PT)
            sp.dma_start(T["wkv_p"], state[:]).then_inc(s["state_stored"], 16)
            store(PT, SROWS)
            sp.wait_ge(s["state_ready"], ONE + 2 * PT + 1)
            sp.dma_start(T["wkv_s"], sstate[:]).then_inc(s["state_stored"], 16)
            sp.wait_ge(s["out_stored"], ONE + 16 * NT)
            sp.wait_ge(s["state_stored"], ONE + 32)

        def times(body):
            def run(eng):
                with eng.Fori(0, PT) as t:
                    body(t, P, 0)
                body(PT, SROWS, 1)
            return run

        @block.gpsimd
        def _(pool):
            nc.gpsimd.memset(prev[0:1, :], 0.0).then_inc(s["prev_set"], 1)
            nc.gpsimd.memset(stat[:], EPS).then_inc(s["eps_set"], 1)
            pool.wait_ge(s["const_in"], ONE + 16 * NCONST)

            def body(t, R, smp):
                chain = CountedChain(pool, s["pool_chain"], t, 3)
                pool.wait_ge(s["p_in"], ONE + 16 * (t + 1))
                pool.wait_ge(s["prev_in"], ONE + 16 * (t + 1) + 16 * smp)
                chain(nc.gpsimd.tensor_tensor(prev[0:R], prev[0:R], p[0:R], ALU.subtract))
                chain(nc.gpsimd.tensor_tensor(prev[0:R], prev[0:R], mu[0:R], ALU.mult))
                pool.wait_ge(s["out_ready"], ONE + t)
                nc.gpsimd.tensor_tensor(ps[0:R], prev[0:R], p[0:R], ALU.add).then_inc(s["mixed"], 1)
                pool.wait_ge(s["mixed"], ONE + t + 1)
                nc.gpsimd.tensor_tensor(kk[0:R], ps[0:R, W:2 * W], vec["k_k"][0:R], ALU.mult).then_inc(s["kk_scaled"], 1)
                pool.wait_ge(s["masked"], ONE + 2 * t + 1)
                for n in range(SLEVELS if smp else LEVELS):
                    last = nc.gpsimd.tensor_tensor(
                        heads(ML[0:R, n, :]), AB[0:R, :, 0, :],
                        lev[0:R, n, :].unsqueeze(1).broadcast_to([R, RH, CH]), ALU.mult)
                    if n == 0:
                        last.then_inc(s["level_masks"], 1)
                last.then_inc(s["level_masks"], 1)
                pool.wait_ge(s["rk_ready"], ONE + t + 1)
                chain(nc.gpsimd.tensor_tensor(bon[0:R], ps[0:R, 0:W], k2[0:R], ALU.mult))
                nc.gpsimd.tensor_tensor(bon[0:R], bon[0:R], vec["r_k"][0:R], ALU.mult).then_inc(s["bonus_in"], 1)
                chain.end()

            times(body)(pool)

        @block.tensor
        def _(pe):
            pe.wait_ge(s["const_in"], ONE + 16 * NCONST)

            def body(t, R, smp):
                G = 1 if smp else 2
                pe.wait_ge(s["state_ready"], ONE + 2 * t)
                pe.wait_ge(s["y_centered"], ONE + t)
                pe.wait_ge(s["lo_sig"], ONE + t + 1)
                for n in range(2):
                    last = nc.tensor.transpose(PS[:, 4, n * P:n * P + R], lo[0:R, n * P:(n + 1) * P], ident[0:R, 0:R])
                last.then_inc(s["lo_turned"], 1)
                pe.wait_ge(s["lo_copied"], ONE + t + 1)
                nc.tensor.matmul(PS[0:R, 0, :], loT[0:64, 0, 0:R], wa_up[0:64, :], start=True, stop=True)
                nc.tensor.matmul(PS[0:R, 1, :], loT[64:128, 0, 0:R], wa_up[64:128, :], start=True, stop=True)
                nc.tensor.matmul(PS[0:R, 2, :], loT[:, 1, 0:R], g_up[:], start=True, stop=True).then_inc(s["lora_done"], 1)
                pe.wait_ge(s["lw_ready"], ONE + t + 1)
                nc.tensor.matmul(PS[0:R, 3, :], cum_l[smp][0:R, 0:R], lw[0:R, :], start=True, stop=True)
                NS = SB if smp else 4
                for n in range(NPAIR):
                    last = nc.tensor.matmul(PS[:, 4, 256 + n * NS:256 + (n + 1) * NS], lw[0:R, n * P:(n + 1) * P],
                                            tot[smp][0:R, :], start=True, stop=True)
                last.then_inc(s["cum_done"], 1)
                pe.wait_ge(s["scaled_ready"], ONE + t + 1)
                pe.wait_ge(s["bef_exp"], ONE + t + 1)
                pe.wait_ge(s["za_ready"], ONE + t + 1)
                pe.wait_ge(s["g_copied"], ONE + t + 1)
                for n, src in enumerate((kq, rt, bt, kt)):
                    for pr in range(NPAIR):
                        last = nc.tensor.transpose(PS[:, n, pr * P:pr * P + R], src[0:R, pr * P:(pr + 1) * P],
                                                   ident[0:R, 0:R])
                    last.then_inc(s["turned_ready"], 1)
                pe.wait_ge(s["turned_copied"], ONE + 4 * t + 4)
                carry(pe, s["carrier"])
                for n in range(2):
                    for h in range(RH):
                        hp = slice(64 * (h % 2), 64 * (h % 2) + 64)
                        for c in range(G):
                            tok = slice(c * CH, (c + 1) * CH)
                            dst = PS[c * CH:(c + 1) * CH, 4 + 2 * n + h % 2, (h // 2) * P:(h // 2 + 1) * P]
                            last = nc.tensor.matmul(dst.rearrange("p (k t) -> p k t", k=2), bkT[hp, n, h // 2, tok],
                                                    qrT[hp, :, h // 2, tok], start=True, stop=True)
                    last.then_inc(s["pair_done"], 1)
                NL = SLEVELS if smp else LEVELS
                tl = t * (LEVELS)
                for n in range(NL):
                    if n == 0:
                        pe.wait_ge(s["level_masks"], ONE + 2 * t + 1)
                    else:
                        pe.wait_ge(s["level_masks"], ONE + 2 * t + 2)
                        pe.wait_ge(s["t_ready"], ONE + tl + n)
                    carry(pe, s["carrier"])
                    for h in range(RH):
                        for c in range(G):
                            cp = slice(c * CH, (c + 1) * CH)
                            rhs = eye[cp, :] if n == 0 else Tn[cp, h, :]
                            last = nc.tensor.matmul(PS[cp, 0, h * CH:(h + 1) * CH], heads(ML[:, n, :])[cp, h, :], rhs,
                                                    start=True, stop=True)
                    last.then_inc(s["x_done"], 1)
                    if n == 0:
                        continue
                    pe.wait_ge(s["x_copied"], ONE + t * (LEVELS - 1) + n)
                    carry(pe, s["carrier"])
                    for h in range(RH):
                        for c in range(G):
                            cp = slice(c * CH, (c + 1) * CH)
                            if n < NL - 1:
                                nc.tensor.matmul(PS[cp, 1, h * CH:(h + 1) * CH], Tt[cp, h, :], X[cp, h, :],
                                                 start=True, stop=True)
                            last = nc.tensor.matmul(PS[cp, 2, h * CH:(h + 1) * CH], X[cp, h, :], Tt[cp, h, :],
                                                    start=True, stop=True)
                    last.then_inc(s["y_done"], 1)
                pe.wait_ge(s["t_ready"], ONE + tl + NL)
                pe.wait_ge(s["masked"], ONE + 2 * t + 2)
                for c in range(G):
                    u = 2 * t + c
                    cp = slice(c * CH, (c + 1) * CH)
                    pe.wait_ge(s["sp_ready"], ONE + u + 1)
                    for h in range(RH):
                        hc = slice(h * CH, (h + 1) * CH)
                        if h % 2 == 0:
                            from_state(0, h // 2, cp, PS[cp, 3, h * CH:(h + 2) * CH], smp)
                        last = nc.tensor.matmul(PS[cp, 3, hc], AK[cp, h, 0, :], ps[cp, 2 * W + h * RD:2 * W + (h + 1) * RD],
                                                start=False, stop=True, skip_group_check=True)
                    last.then_inc(s["r_done"], 1)
                    for h in range(RH):
                        hc = slice(h * CH, (h + 1) * CH)
                        vh = ps[cp, 2 * W + h * RD:2 * W + (h + 1) * RD]
                        if h == 0:
                            pe.wait_ge(s["r_copied"], ONE + u + 1)
                            carry(pe, s["carrier"])
                            for i in range(RH):
                                last = nc.tensor.matmul(PS[cp, 4, i * CH:(i + 1) * CH], Tt[cp, i, :],
                                                        R_[cp, i * CH:(i + 1) * CH], start=True, stop=True)
                            last.then_inc(s["sa_done"], 1)
                            pe.wait_ge(s["sa_copied"], ONE + u + 1)
                        if h % 2 == 0:
                            from_state(1, h // 2, cp, PS[cp, 5, h * CH:(h + 2) * CH], smp)
                        nc.tensor.matmul(PS[cp, 5, hc], AK[cp, h, 1, :], vh, start=False, stop=False,
                                         skip_group_check=True)
                        last = nc.tensor.matmul(PS[cp, 5, hc], AB[cp, h, 1, :], SA[cp, hc], start=False, stop=True,
                                                skip_group_check=True)
                    last.then_inc(s["yy_done"], 1)
                    if not smp:
                        for h in range(RH):
                            hp = slice(64 * (h % 2), 64 * (h % 2) + 64)
                            hc = slice(h * CH, (h + 1) * CH)
                            dst = PS[hp, 6, (h // 2) * RD:(h // 2 + 1) * RD]
                            nc.tensor.matmul(dst, bt[cp, hc], SA[cp, hc], start=True, stop=False)
                            last = nc.tensor.matmul(dst, kt[cp, hc], ps[cp, 2 * W + h * RD:2 * W + (h + 1) * RD],
                                                    start=False, stop=True)
                        last.then_inc(s["st_done"], 1)
                        continue
                    for n, src in enumerate((bt, kt)):
                        pe.wait_ge(s["big_ready"], ONE + 1 + n)
                        for h in range(RH):
                            hp = slice(64 * (h % 2), 64 * (h % 2) + 64)
                            last = nc.tensor.matmul(PS[hp, SBANK[h // 2], :], src[cp, h * RD:(h + 1) * RD],
                                                    big[cp, h, :, :].rearrange("p b i -> p (b i)"),
                                                    start=(n == 0), stop=(n == 1), skip_group_check=True)
                        last.then_inc(s["st_done"], 1)

            def from_state(n, pr, cp, dst, smp):
                if not smp:
                    nc.tensor.matmul(dst, qrT[:, n, pr, cp], Sp[:, pr].rearrange("p k i -> p (k i)"), start=True,
                                     stop=False, skip_group_check=True)
                    return
                for b in range(SB):
                    nc.tensor.matmul(dst, big[:, n * NPAIR + pr, b, :], sdiag[:, pr, b].rearrange("p k i -> p (k i)"),
                                     start=(b == 0), stop=False, skip_group_check=True)

            times(body)(pe)

        @block.scalar
        def _(act):
            act.wait_ge(s["eps_set"], ONE + 1)
            gn_eps = hs[:, 7, 0:1]
            act.wait_ge(s["chain"], ONE + 1)

            def body(t, R, smp):
                G = 1 if smp else 2
                act.wait_ge(s["mixed"], ONE + t + 1)
                nc.scalar.activation(lo[0:R, 0:64], ps[0:R, 3 * W:3 * W + 64], ACT.Tanh)
                nc.scalar.activation(lo[0:R, 64:128], ps[0:R, 3 * W + 64:3 * W + 128], ACT.Copy)
                nc.scalar.activation(lo[0:R, 128:256], ps[0:R, 3 * W + 128:3 * W + 256], ACT.Tanh,
                                     scale=0.5).then_inc(s["lo_ready"], 1)
                act.wait_ge(s["kk_scaled"], ONE + t + 1)
                nc.scalar.activation(sq[0:R], kk[0:R], ACT.Square).then_inc(s["kk_squared"], 1)
                act.wait_ge(s["lo_turned"], ONE + t + 1)
                nc.scalar.activation(loT[:, :, 0:R], PS[:, 4, 0:256].rearrange("p (n t) -> p n t", n=2)[:, :, 0:R],
                                     ACT.Copy).then_inc(s["lo_copied"], 1)
                act.wait_ge(s["z_ready"], ONE + t + 1)
                nc.scalar.activation(z[0:R], z[0:R], ACT.Exp, scale=-1.0).then_inc(s["z_exp"], 1)
                act.wait_ge(s["za_ready"], ONE + t + 1)
                nc.scalar.activation(a[0:R], a[0:R], ACT.Tanh, scale=0.5).then_inc(s["a_tanh"], 1)
                nc.scalar.activation(g[0:R], PS[0:R, 2, :], ACT.Copy).then_inc(s["g_copied"], 1)
                act.wait_ge(s["cum_done"], ONE + t + 1)
                nc.scalar.activation(e_in[0:R], PS[0:R, 3, :], ACT.Exp)
                nc.scalar.activation(e_out[0:R], PS[0:R, 3, :], ACT.Exp, scale=-1.0)
                NS = SB if smp else 4
                nc.scalar.activation(ep[:, :, 0:NS], PS[:, 4, 256:256 + NPAIR * NS].rearrange("p (n k) -> p n k", n=NPAIR),
                                     ACT.Exp).then_inc(s["e_ready"], 1)
                act.wait_ge(s["bef_ready"], ONE + t + 1)
                nc.scalar.activation(e_bef[0:R], e_bef[0:R], ACT.Exp).then_inc(s["bef_exp"], 1)
                act.wait_ge(s["kk_sum"], ONE + t + 1)
                nc.scalar.activation(hs[0:R, 1, :], hs[0:R, 0, :], ACT.Sqrt).then_inc(s["kk_root"], 1)
                for n in range(4):
                    dst = (qrT, bkT)[n // 2][:, n % 2, :, 0:R]
                    act.wait_ge(s["turned_ready"], ONE + 4 * t + n + 1)
                    nc.scalar.activation(dst, PS[:, n, :].rearrange("p (n t) -> p n t", n=NPAIR)[:, :, 0:R],
                                         ACT.Copy).then_inc(s["turned_copied"], 1)
                for n in range(1, SLEVELS if smp else LEVELS):
                    act.wait_ge(s["x_done"], ONE + t * LEVELS + n + 1)
                    nc.scalar.activation(X[0:R], heads(PS[0:R, 0, :]), ACT.Copy).then_inc(s["x_copied"], 1)
                for c in range(G):
                    u = 2 * t + c
                    cp = slice(c * CH, (c + 1) * CH)
                    act.wait_ge(s["r_done"], ONE + u + 1)
                    nc.scalar.activation(R_[cp], PS[cp, 3, :], ACT.Copy, scale=-1.0).then_inc(s["r_copied"], 1)
                    act.wait_ge(s["sa_done"], ONE + u + 1)
                    nc.scalar.activation(SA[cp], PS[cp, 4, :], ACT.Copy).then_inc(s["sa_copied"], 1)
                act.wait_ge(s["y_centered"], ONE + t + 1)
                nc.scalar.activation(sq[0:R], yc[0:R], ACT.Square).then_inc(s["y_squared"], 1)
                act.wait_ge(s["y_sum"], ONE + t + 1)
                nc.scalar.activation(hs[0:R, 4, :], hs[0:R, 3, :], ACT.Sqrt, bias=gn_eps[0:R],
                                     scale=1.0 / RD).then_inc(s["y_root"], 1)

            times(body)(act)

        @block.vector
        def _(dve):
            nc.vector.memset(hs[:, 7, :], GN_EPS).then_inc(s["chain"], 1)
            nc.vector.memset(Sp[:], 0.0)
            nc.vector.memset(state[:], 0.0).then_inc(s["chain"], 1)
            dve.wait_ge(s["chain"], ONE + 2)
            dve.wait_ge(s["const_in"], ONE + 16 * NCONST)
            K = 19

            def spread(ap, R):
                return ap.unsqueeze(2).broadcast_to([R, RH, RD])

            def body(t, R, smp):
                G = 1 if smp else 2
                chain = CountedChain(dve, s["chain"], t, K)
                chain.n = chain.n + 2
                v = ps[0:R, 2 * W:3 * W]
                dve.wait_ge(s["lo_ready"], ONE + t + 1)
                nc.vector.tensor_scalar(lo[0:R, 128:256], lo[0:R, 128:256], 0.5, 0.5, ALU.mult,
                                        ALU.add).then_inc(s["lo_sig"], 1)
                dve.wait_ge(s["kk_squared"], ONE + t + 1)
                nc.vector.reduce_sum(hs[0:R, 0, :], heads(sq[0:R]), axis=AX_X).then_inc(s["kk_sum"], 1)
                dve.wait_ge(s["lora_done"], ONE + t + 1)
                nc.vector.tensor_tensor(z[0:R], PS[0:R, 0, :], vec["w0"][0:R], ALU.add).then_inc(s["z_ready"], 1)
                nc.vector.tensor_tensor(a[0:R], PS[0:R, 1, :], vec["a0"][0:R], ALU.add).then_inc(s["za_ready"], 1)
                dve.wait_ge(s["z_exp"], ONE + t + 1)
                chain(nc.vector.tensor_scalar(z[0:R], z[0:R], 1.0, None, ALU.add))
                chain(nc.vector.reciprocal(z[0:R], z[0:R]))
                nc.vector.tensor_scalar(lw[0:R], z[0:R], -float(np.exp(-0.5)), None, ALU.mult).then_inc(s["lw_ready"], 1)
                dve.wait_ge(s["a_tanh"], ONE + t + 1)
                chain(nc.vector.tensor_scalar(a[0:R], a[0:R], 0.5, 0.5, ALU.mult, ALU.add))
                chain(nc.vector.scalar_tensor_tensor(k2[0:R], a[0:R], 1.0, vec["k_a"][0:R], ALU.subtract, ALU.mult))
                nc.vector.scalar_tensor_tensor(k2[0:R], k2[0:R], 1.0, ps[0:R, W:2 * W], ALU.add,
                                               ALU.mult).then_inc(s["rk_ready"], 1)
                dve.wait_ge(s["e_ready"], ONE + t + 1)
                dve.wait_ge(s["lw_ready"], ONE + t + 1)
                nc.vector.tensor_tensor(e_bef[0:R], PS[0:R, 3, :], lw[0:R], ALU.subtract).then_inc(s["bef_ready"], 1)
                dve.wait_ge(s["kk_root"], ONE + t + 1)
                chain(nc.vector.tensor_scalar(hs[0:R, 1, :], hs[0:R, 1, :], 1e-12, None, ALU.max))
                chain(nc.vector.reciprocal(hs[0:R, 2, :], hs[0:R, 1, :]))
                chain(nc.vector.tensor_tensor(heads(kk[0:R]), heads(kk[0:R]), spread(hs[0:R, 2, :], R), ALU.mult))
                chain(nc.vector.tensor_tensor(bb[0:R], kk[0:R], a[0:R], ALU.mult))
                dve.wait_ge(s["bef_exp"], ONE + t + 1)
                nc.vector.tensor_tensor(kq[0:R], kk[0:R], e_bef[0:R], ALU.mult)
                nc.vector.tensor_tensor(rt[0:R], ps[0:R, 0:W], e_in[0:R], ALU.mult)
                nc.vector.tensor_tensor(bt[0:R], bb[0:R], e_out[0:R], ALU.mult)
                dve.wait_ge(s["rk_ready"], ONE + t + 1)
                nc.vector.tensor_tensor(kt[0:R], k2[0:R], e_out[0:R], ALU.mult).then_inc(s["scaled_ready"], 1)
                for n, dst in enumerate((AB, AK)):
                    dve.wait_ge(s["pair_done"], ONE + 2 * t + n + 1)
                    for i in range(2):
                        last = nc.vector.tensor_tensor(
                            dst[0:R, i::2].rearrange("p h k t -> p h (k t)"),
                            PS[0:R, 4 + 2 * n + i, :].rearrange("p (h k) -> p h k", h=4),
                            tri[smp][0:R].rearrange("p k t -> p (k t)").unsqueeze(1).broadcast_to([R, 4, 2 * CH]),
                            ALU.mult)
                    last.then_inc(s["masked"], 1)
                eyeb = eye[0:R].unsqueeze(1).broadcast_to([R, RH, CH])
                NL = SLEVELS if smp else LEVELS
                dve.wait_ge(s["level_masks"], ONE + 2 * t + 1)
                nc.vector.tensor_tensor(Tt[0:R], eyeb, heads(ML[0:R, 0, :]), ALU.subtract)
                dve.wait_ge(s["x_done"], ONE + t * LEVELS + 1)
                nc.vector.tensor_tensor(Tn[0:R], eyeb, heads(PS[0:R, 0, :]), ALU.subtract).then_inc(s["t_ready"], 1)
                for n in range(1, NL):
                    dve.wait_ge(s["t_ready"], ONE + t * LEVELS + n)
                    dve.wait_ge(s["y_done"], ONE + t * (LEVELS - 1) + n)
                    if n < NL - 1:
                        nc.vector.tensor_tensor(Tn[0:R], Tn[0:R], heads(PS[0:R, 1, :]), ALU.subtract)
                    nc.vector.tensor_tensor(Tt[0:R], Tt[0:R], heads(PS[0:R, 2, :]), ALU.subtract).then_inc(s["t_ready"], 1)
                if not smp:
                    for c in range(G):
                        u = 2 * t + c
                        for i in range(2):
                            half = slice(64 * i, 64 * i + 64)
                            last = nc.vector.tensor_tensor(
                                Sp[half, :, i, :], state[half], ep[half, :, 2 * c:2 * c + 1].broadcast_to(
                                    [64, NPAIR, RD]), ALU.mult)
                        last.then_inc(s["sp_ready"], 1)
                        dve.wait_ge(s["sp_ready"], ONE + u + 1)
                        dve.wait_ge(s["st_done"], ONE + u + 1)
                        for i in range(2):
                            half = slice(64 * i, 64 * i + 64)
                            last = nc.vector.tensor_tensor(state[half], Sp[half, :, i, :],
                                                           PS[half, 6, 0:NPAIR * RD].rearrange(
                                                               "p (n i) -> p n i", n=NPAIR), ALU.add)
                        chain(last)
                        nc.vector.tensor_tensor(state[:], state[:], ep[:, :, 2 * c + 1:2 * c + 2].broadcast_to(
                            [P, NPAIR, RD]), ALU.mult).then_inc(s["state_ready"], 1)
                        dve.wait_ge(s["state_ready"], ONE + u + 1)
                else:
                    dve.wait_ge(s["turned_copied"], ONE + 4 * t + 4)
                    dve.wait_ge(s["sstate_in"], ONE + 32)
                    for n in range(2):
                        for pr in range(NPAIR):
                            last = nc.vector.tensor_tensor(
                                big[:, n * NPAIR + pr], qrT[:, n, pr, 0:R].unsqueeze(1).broadcast_to([P, SB, CH]),
                                seq_of[:], ALU.mult)
                    last.then_inc(s["sp_ready"], 1)
                    for n in range(2):
                        if n == 0:
                            dve.wait_ge(s["sa_copied"], ONE + 2 * t + 1)
                            dve.wait_ge(s["yy_done"], ONE + 2 * t + 1)
                            dve.wait_ge(s["sp_ready"], ONE + 2 * t + 1)
                        else:
                            dve.wait_ge(s["st_done"], ONE + 2 * t + 1)
                        src = SA[0:R] if n == 0 else v
                        for h in range(RH):
                            last = nc.vector.tensor_tensor(
                                big[0:R, h], src[:, h * RD:(h + 1) * RD].unsqueeze(1).broadcast_to([R, SB, RD]),
                                seq_row[0:R].unsqueeze(2).broadcast_to([R, SB, RD]), ALU.mult)
                        last.then_inc(s["big_ready"], 1)
                        dve.wait_ge(s["big_ready"], ONE + 1 + n)
                    dve.wait_ge(s["st_done"], ONE + 2 * t + 2)
                    for pr in range(NPAIR):
                        last = nc.vector.tensor_tensor(sstate[:, pr], sstate[:, pr], PS[:, SBANK[pr], :].rearrange(
                            "p (b i) -> p b i", b=SB), ALU.add)
                    chain(last)
                    for pr in range(NPAIR):
                        last = nc.vector.tensor_tensor(sstate[:, pr], sstate[:, pr],
                                                       ep[:, pr, :].unsqueeze(2).broadcast_to([P, SB, RD]), ALU.mult)
                    last.then_inc(s["state_ready"], 1)
                dve.wait_ge(s["yy_done"], ONE + 2 * t + G)
                yp = heads(PS[0:R, 5, :])
                chain(nc.vector.reduce_sum(hs[0:R, 5, :], yp, axis=AX_X))
                chain(nc.vector.tensor_scalar(hs[0:R, 5, :], hs[0:R, 5, :], 1.0 / RD, None, ALU.mult))
                nc.vector.tensor_tensor(heads(yc[0:R]), yp, spread(hs[0:R, 5, :], R), ALU.subtract).then_inc(s["y_centered"], 1)
                dve.wait_ge(s["y_squared"], ONE + t + 1)
                nc.vector.reduce_sum(hs[0:R, 3, :], heads(sq[0:R]), axis=AX_X).then_inc(s["y_sum"], 1)
                dve.wait_ge(s["bonus_in"], ONE + t + 1)
                chain(nc.vector.reduce_sum(hs[0:R, 6, :], heads(bon[0:R]), axis=AX_X))
                dve.wait_ge(s["out_stored"], ONE + 16 * t)
                chain(nc.vector.tensor_tensor(heads(out[0:R]), heads(v), spread(hs[0:R, 6, :], R), ALU.mult))
                chain(nc.vector.tensor_tensor(out[0:R], out[0:R], vec["ln_b"][0:R], ALU.add))
                dve.wait_ge(s["y_root"], ONE + t + 1)
                chain(nc.vector.reciprocal(hs[0:R, 5, :], hs[0:R, 4, :]))
                chain(nc.vector.tensor_tensor(heads(yc[0:R]), heads(yc[0:R]), spread(hs[0:R, 5, :], R), ALU.mult))
                chain(nc.vector.tensor_tensor(yc[0:R], yc[0:R], vec["ln_w"][0:R], ALU.mult))
                chain(nc.vector.tensor_tensor(out[0:R], out[0:R], yc[0:R], ALU.add))
                nc.vector.tensor_tensor(out[0:R], out[0:R], g[0:R], ALU.mult).then_inc(s["out_ready"], 1)
                chain.end(smp)

            times(body)(dve)

def out_projection(nc, T):
    with ExitStack() as ctx:
        m = Mem(nc, ctx, "op")
        w = m.sb("w", [P, KD, D])
        ident = m.sb("ident", [P, P])
        mx = [m.sb(f"mixed{i}", [P, D]) for i in range(2)]
        x = [m.sb(f"x{i}", [P, D]) for i in range(2)]
        mT = m.sb("mT", [P, KD, P])
        h = [m.sb(f"h{i}", [P, D]) for i in range(2)]
        zero = m.sb("zero", [P, D])
        psT = m.ps("psT", [P, KD, P])
        psO = [m.ps(f"psO{i}", [P, D]) for i in range(2)]
        ident_in = m.sem("ident_in")
        w_in = m.sem("w_in")
        tile_in = [m.sem(f"tile_in{i}") for i in range(2)]
        zeroed = m.sem("zeroed")
        zero_stored = m.sem("zero_stored")
        turned = m.sem("turned")
        copied = m.sem("copied")
        summed = m.sem("summed")
        added = m.sem("added")
        stored = m.sem("stored")
        block = ctx.enter_context(nc.Block())

        def tiles(body):
            for t in range(NT):
                body(t, t % 2, P if t < PT else SROWS)

        @block.sync
        def _(sp):
            sp.dma_start(ident[:], T["ident"]).then_inc(ident_in, 16)

            def load(t, i, R):
                if t >= 2:
                    sp.wait_ge(turned, t - 1)
                    sp.wait_ge(added, t - 1)
                sp.dma_start(mx[i][0:R], T["mixed"][t * P:t * P + R, :]).then_inc(tile_in[i], 16)
                sp.dma_start(x[i][0:R], T["x"][t * P:t * P + R, :]).then_inc(tile_in[i], 16)
                if t == 0:
                    for k in range(KD):
                        sp.dma_start(w[:, k, :], T["w_out"][k * P:(k + 1) * P, :]).then_inc(w_in, 16)
                if t:
                    store(t - 1, 1 - i, P)

            def store(t, i, R):
                sp.wait_ge(added, t + 1)
                sp.dma_start(T["h"][t * P:t * P + R, :], h[i][0:R]).then_inc(stored, 16)

            tiles(load)
            store(PT, 0, SROWS)
            sp.wait_ge(zeroed, 1)
            sp.dma_start(T["h"][SEQ + SROWS:ROWS, :], zero[0:P - SROWS]).then_inc(zero_stored, 16)
            sp.wait_ge(stored, 16 * NT)
            sp.wait_ge(zero_stored, 16)

        @block.gpsimd
        def _(pool):
            nc.gpsimd.memset(zero[:], 0.0).then_inc(zeroed, 1)

        @block.tensor
        def _(pe):
            pe.wait_ge(ident_in, 16)

            def turn(t, i, R):
                pe.wait_ge(tile_in[i], 32 * (t // 2 + 1))
                pe.wait_ge(copied, t)
                for k in range(KD):
                    last = nc.tensor.transpose(psT[:, k, 0:R], mx[i][0:R, k * P:(k + 1) * P], ident[0:R, 0:R])
                last.then_inc(turned, 1)

            def product(t, i, R):
                pe.wait_ge(copied, t + 1)
                if t >= 2:
                    pe.wait_ge(added, t - 1)
                if t == 0:
                    pe.wait_ge(w_in, 16 * KD)
                for j in range(2):
                    for k in range(KD):
                        last = nc.tensor.matmul(psO[i][0:R, j * 512:(j + 1) * 512], mT[:, k, 0:R],
                                                w[:, k, j * 512:(j + 1) * 512], start=(k == 0), stop=(k == KD - 1))
                last.then_inc(summed, 1)

            tiles(lambda t, i, R: (turn(t, i, R), product(t, i, R)))

        @block.scalar
        def _(act):
            def copy(t, i, R):
                act.wait_ge(turned, t + 1)
                act.wait_ge(summed, t)
                nc.scalar.activation(mT[:, :, 0:R], psT[:, :, 0:R], ACT.Copy).then_inc(copied, 1)

            tiles(copy)

        @block.vector
        def _(dve):
            def add(t, i, R):
                dve.wait_ge(summed, t + 1)
                if t >= 2:
                    dve.wait_ge(stored, 16 * (t - 1))
                dve.wait_ge(tile_in[i], 32 * (t // 2 + 1))
                nc.vector.tensor_tensor(h[i][0:R], psO[i][0:R], x[i][0:R], ALU.add).then_inc(added, 1)

            tiles(add)

def peer(nc, T):
    NBUF = 8
    QW = 2 * NK
    with ExitStack() as ctx:
        m = Mem(nc, ctx, "pe")
        wq = m.sb("wq", [P, KD, PH * QW])
        keys = m.sb("keys", [P, PH, 2, NK])
        buf = [m.sb(f"buf{b}", [P, 2 * D]) for b in range(NBUF)]
        hb = [m.sb(f"h{i}", [P, D]) for i in range(2)]
        hn = [m.sb(f"hn{i}", [P, D]) for i in range(2)]
        hnT = m.sb("hnT", [P, KD, P])
        gf = m.sb("gf", [P, D])
        gy = m.sb("gy", [P, D])
        y = m.sb("y", [P, D])
        y_sq = m.sb("y_sq", [P, D])
        ident = m.sb("ident", [P, P])
        iota = m.sb("iota", [P, TOPK])
        diag = m.sb("diag", [P, NBUF, P])
        q = m.sb("q", [P, QW])
        qT = m.sb("qT", [P, 2, P])
        top = m.sb("top", [P, 2, TOPK])
        topi = m.sb("topi", [P, 2, TOPK], U32)
        topf = m.sb("topf", [P, 2, TOPK])
        left = m.sb("left", [P, 2, NK])
        cand = m.sb("cand", [P, TOPK, TOPK])
        cleft = m.sb("cleft", [P, TOPK * TOPK])
        best = m.sb("best", [P, TOPK])
        besti = m.sb("besti", [P, TOPK], U32)
        part = m.sb("part", [P, 2, TOPK], U32)
        partf = m.sb("partf", [P, 2, TOPK])
        hit = m.sb("hit", [P, TOPK, 2 * TOPK])
        row = m.sb("row", [P, 2, TOPK])
        ex = m.sb("ex", [P, TOPK])
        sm = m.sb("sm", [P, 4])
        gate = [m.sb(f"gate{i}", [P, PH * TOPK]) for i in range(2)]
        expert = [m.sb(f"expert{i}", [P, PH * TOPK], U32) for i in range(2)]
        expert_h = [m.sb(f"expert_h{i}", [P, TOPK], U32) for i in range(2)]
        dot = m.sb("dot", [P, 2, TOPK])
        act_v = m.sb("act", [P, 2, TOPK])
        wgt = m.sb("wgt", [P, 2, TOPK])
        st = m.sb("st", [P, 8])
        psO = m.ps("psO", [P, D])
        psT = m.ps("psT", [P, KD, P])
        psQ = m.ps("psQ", [P, 512])
        psQT = m.ps("psQT", [P, 512])
        psS = m.ps("psS", [P, 512])

        wq_in = m.sem("wq_in")
        const_in = m.sem("const_in")
        h_in = [m.sem(f"h_in{i}") for i in range(2)]
        eps_set = m.sem("eps_set")
        h_summed = m.sem("h_summed")
        h_root = m.sem("h_root")
        tile_chain = m.sem("tile_chain")
        hn_ready = m.sem("hn_ready")
        hn_turned = m.sem("hn_turned")
        hnT_ready = m.sem("hnT_ready")
        q_done = m.sem("q_done")
        q_copied = m.sem("q_copied")
        qT_done = m.sem("qT_done")
        qT_copied = m.sem("qT_copied")
        scores_done = m.sem("scores_done")
        scores_read = m.sem("scores_read")
        topk_chain = m.sem("topk_chain")
        best_ready = m.sem("best_ready")
        exp_done = m.sem("exp_done")
        chosen = m.sem("chosen")
        staged = m.sem("staged")
        pool_carrier = m.sem("pool_carrier")
        dve_carrier = m.sem("dve_carrier")
        pe_carrier = m.sem("pe_carrier")
        gathered = [m.sem(f"gathered{b}", from_zero=True) for b in range(NBUF)]
        dotted = m.sem("dotted")
        gelu_done = m.sem("gelu_done")
        wgt_ready = m.sem("wgt_ready")
        diag_ready = m.sem("diag_ready")
        buffer_free = m.sem("buffer_free")
        started = m.sem("started")
        out_done = m.sem("out_done")
        out_copied = m.sem("out_copied")
        y_root = m.sem("y_root")
        y_summed = m.sem("y_summed")
        y_chain = m.sem("y_chain")
        y_ready = m.sem("y_ready")
        y_stored = m.sem("y_stored")
        m.prime()
        block = ctx.enter_context(nc.Block())

        KT, KU, KY = 1, 18, 1

        def h_count(t, par):
            return 16 * ((t - par) // 2 + 1) if isinstance(t, int) else 8 * (t - par) + 16

        def tiles(eng, tile_start, unit, tile_end, prologue):
            prologue()
            with eng.Fori(0, PT // 2) as pair:
                for par in range(2):
                    t = 2 * pair + par
                    tile_start(t, par, P, True)
                    with eng.Fori(0, PH // 2) as hp:
                        for hh in range(2):
                            unit(t * PH + 2 * hp + hh, 2 * hp + hh, par, hh, P, True)
                    tile_end(t, par, P)
            tile_start(PT, 0, SROWS, False)
            with eng.Fori(0, PH // 2) as hp:
                for hh in range(2):
                    unit(PT * PH + 2 * hp + hh, 2 * hp + hh, 0, hh, SROWS, False)
            tile_end(PT, 0, SROWS)

        @block.sync
        def _(sp):
            sp.dma_start(hb[0][:], T["h"][0:P, :]).then_inc(h_in[0], 16)
            sp.dma_start(ident[:], T["ident"]).then_inc(const_in, 16)
            sp.dma_start(iota[:], T["iota16"].partition_broadcast(P)).then_inc(const_in, 16)
            sp.dma_start(gf[:], T["ffn_norm"].partition_broadcast(P)).then_inc(const_in, 16)
            sp.dma_start(gy[:], T["final_norm"].partition_broadcast(P)).then_inc(const_in, 16)
            sp.dma_start(keys[:], T["sub_keys"]).then_inc(const_in, 16)
            for k in range(KD):
                sp.dma_start(wq[:, k, :], T["peer_wq"][k * P:(k + 1) * P, :]).then_inc(wq_in, 16)

            def tile_start(t, par, R, nxt):
                if nxt:
                    sp.wait_ge(started, ONE + t)
                    sp.dma_start(hb[1 - par][:], T["h"][rows(t + 1), :]).then_inc(h_in[1 - par], 16)

            def unit(it, h, par, hh, R, nxt):
                pass

            def tile_end(t, par, R):
                sp.wait_ge(y_ready, ONE + t + 1)
                sp.dma_start(T["y_all"][rows(t, R), :], y[0:R, :]).then_inc(y_stored, 16)

            with sp.Fori(0, PT // 2) as pair:
                for par in range(2):
                    tile_start(2 * pair + par, par, P, True)
                    tile_end(2 * pair + par, par, P)
            tile_end(PT, 0, SROWS)
            sp.wait_ge(y_stored, ONE + 16 * NT)

        @block.gpsimd
        def _(pool):
            nc.gpsimd.memset(st[:, 7:8], EPS).then_inc(eps_set, 1)

            def unit(it, h, par, hh, R, nxt):
                pool.wait_ge(chosen, ONE + it + 1)
                nc.gpsimd.tensor_copy(expert_h[hh][:], expert[par][:, bass.ds(h * TOPK, TOPK)]).then_inc(staged, 1)
                pool.wait_ge(staged, ONE + it + 1)
                for s in range(TOPK):
                    b = s % NBUF
                    pool.wait_ge(buffer_free, ONE + it * TOPK + s + 1)
                    carry(pool, pool_carrier)
                    pool.indirect_dma_start(buf[b][0:R, :], None, T["experts"],
                                            bass.IndirectOffsetOnAxis(ap=expert_h[hh][0:R, s:s + 1], axis=0)
                                            ).then_inc(gathered[b], 16)

            tiles(pool, lambda *a: None, unit, lambda *a: None, lambda: None)

        @block.tensor
        def _(pe):
            pe.sem_inc(buffer_free, NBUF)
            pe.wait_ge(const_in, ONE + 80)

            def front_tile(t, par):
                pe.wait_ge(hn_ready, ONE + t + 1)
                pe.wait_ge(hnT_ready, ONE + t)
                src = hn[par]
                for k in range(KD):
                    last = nc.tensor.transpose(psT[:, k, :], src[:, k * P:(k + 1) * P], ident[:])
                last.then_inc(hn_turned, 1)

            def query(fu, h):
                pe.wait_ge(q_copied, ONE + fu)
                for k in range(KD):
                    last = nc.tensor.matmul(psQ[:, 0:QW], hnT[:, k, :], wq[:, k, bass.ds(h * QW, QW)],
                                            start=(k == 0), stop=(k == KD - 1))
                last.then_inc(q_done, 1)

            def turn(fu):
                pe.wait_ge(q_copied, ONE + fu + 1)
                pe.wait_ge(qT_copied, ONE + fu)
                for c in range(2):
                    last = nc.tensor.transpose(psQT[:, c * P:(c + 1) * P], q[:, c * P:(c + 1) * P], ident[:])
                last.then_inc(qT_done, 1)

            def scores(fu, h):
                pe.wait_ge(qT_copied, ONE + fu + 1)
                pe.wait_ge(scores_read, ONE + fu)
                for c in range(2):
                    last = nc.tensor.matmul(psS[:, c * NK:(c + 1) * NK], qT[:, c, :],
                                            keys[:, bass.ds(h, 1), c, :].rearrange("p a n -> p (a n)"),
                                            start=True, stop=True)
                last.then_inc(scores_done, 1)

            def prologue():
                front_tile(0, 0)
                pe.wait_ge(wq_in, ONE + 16 * KD)
                pe.wait_ge(hnT_ready, ONE + 1)
                with pe.Fori(0, PH) as h:
                    query(h, h)
                    turn(h)
                    scores(h, h)

            def tile_start(t, par, R, nxt):
                if nxt:
                    front_tile(t + 1, 1 - par)
                    pe.wait_ge(hnT_ready, ONE + t + 2)
                pe.wait_ge(h_in[par], ONE + h_count(t, par))
                pe.wait_ge(out_copied, ONE + t)
                for j in range(2):
                    last = nc.tensor.matmul(psO[0:R, j * 512:(j + 1) * 512], ident[0:R, 0:R],
                                            hb[par][0:R, j * 512:(j + 1) * 512], start=True, stop=False,
                                            skip_group_check=True)
                last.then_inc(started, 1)

            def unit(it, h, par, hh, R, nxt):
                fu = it + PH
                for s in range(TOPK):
                    if nxt and s == 0:
                        query(fu, h)
                    if nxt and s == 2:
                        turn(fu)
                    if nxt and s == 4:
                        scores(fu, h)
                    b = s % NBUF
                    pe.wait_ge(diag_ready, ONE + it * TOPK + s + 1)
                    if R < P:
                        carry(pe, pe_carrier)
                    for j in range(2):
                        last = nc.tensor.matmul(psO[0:R, j * 512:(j + 1) * 512], diag[0:R, b, 0:R],
                                                buf[b][0:R, D + j * 512:D + (j + 1) * 512],
                                                start=False, stop=False, skip_group_check=True)
                    last.then_inc(buffer_free, 1)

            def tile_end(t, par, R):
                pass

            tiles(pe, tile_start, unit, tile_end, prologue)

        @block.scalar
        def _(act):
            act.wait_ge(eps_set, ONE + 1)

            def front_tile(t, par):
                act.wait_ge(h_in[par], ONE + h_count(t, par))
                act.wait_ge(hn_ready, ONE + t)
                nc.scalar.activation(y_sq[:], hb[par][:], ACT.Square, accum_out=st[:, 0:1]).then_inc(h_summed, 1)
                act.wait_ge(h_summed, ONE + t + 1)
                nc.scalar.activation(st[:, 1:2], st[:, 0:1], ACT.Sqrt, bias=st[:, 7:8],
                                     scale=1.0 / D).then_inc(h_root, 1)

            def copy_q(fu):
                act.wait_ge(q_done, ONE + fu + 1)
                act.wait_ge(qT_done, ONE + fu)
                nc.scalar.activation(q[:], psQ[:, 0:QW], ACT.Copy).then_inc(q_copied, 1)

            def copy_qT(fu):
                act.wait_ge(qT_done, ONE + fu + 1)
                act.wait_ge(scores_done, ONE + fu)
                nc.scalar.activation(qT[:].rearrange("p c t -> p (c t)"), psQT[:, 0:QW], ACT.Copy).then_inc(qT_copied, 1)

            def exp_best(fu):
                act.wait_ge(best_ready, ONE + fu + 1)
                nc.scalar.activation(ex[:], best[:], ACT.Exp, bias=sm[:, 0:1],
                                     accum_out=sm[:, 1:2]).then_inc(exp_done, 1)

            def prologue():
                front_tile(0, 0)
                with act.Fori(0, PH) as h:
                    copy_q(h)
                    copy_qT(h)
                    exp_best(h)

            def tile_start(t, par, R, nxt):
                if nxt:
                    front_tile(t + 1, 1 - par)

            def unit(it, h, par, hh, R, nxt):
                fu = it + PH
                for s in range(0, TOPK, 2):
                    if nxt and s == 0:
                        copy_q(fu)
                    if nxt and s == 2:
                        copy_qT(fu)
                    act.wait_ge(dotted, ONE + it * TOPK + s + 2)
                    nc.scalar.activation(act_v[0:R, hh, s:s + 2], dot[0:R, hh, s:s + 2],
                                         ACT.Gelu_apprx_tanh).then_inc(gelu_done, 1)
                    act.wait_ge(wgt_ready, ONE + it * (TOPK // 2) + s // 2 + 1)
                    for i in range(2):
                        nc.scalar.activation(diag[0:R, (s + i) % NBUF, 0:R], ident[0:R, 0:R], ACT.Copy,
                                             scale=wgt[0:R, hh, s + i:s + i + 1]).then_inc(diag_ready, 1)
                if nxt:
                    exp_best(fu)

            def tile_end(t, par, R):
                act.wait_ge(buffer_free, ONE + NBUF + (t + 1) * PH * TOPK)
                act.wait_ge(y_stored, ONE + 16 * t)
                nc.scalar.activation(y[0:R, :], psO[0:R, :], ACT.Copy).then_inc(out_copied, 1)
                act.wait_ge(out_copied, ONE + t + 1)
                nc.scalar.activation(y_sq[0:R, :], y[0:R, :], ACT.Square, accum_out=st[0:R, 3:4]).then_inc(y_summed, 1)
                act.wait_ge(y_summed, ONE + t + 1)
                nc.scalar.activation(st[0:R, 4:5], st[0:R, 3:4], ACT.Sqrt, bias=st[0:R, 7:8],
                                     scale=1.0 / D).then_inc(y_root, 1)

            tiles(act, tile_start, unit, tile_end, prologue)

        @block.vector
        def _(dve):
            dve.wait_ge(const_in, ONE + 80)

            def front_tile(t, par):
                chain = Chain(dve, tile_chain, t * KT, first=ONE)
                dve.wait_ge(h_root, ONE + t + 1)
                chain(nc.vector.reciprocal(st[:, 2:3], st[:, 1:2]))
                nc.vector.scalar_tensor_tensor(hn[par][:], hb[par][:], st[:, 2:3], gf[:], ALU.mult,
                                               ALU.mult).then_inc(hn_ready, 1)

            def front_turn(t):
                dve.wait_ge(hn_turned, ONE + t + 1)
                dve.wait_ge(q_done, ONE + t * PH)
                nc.vector.tensor_copy(hnT[:], psT[:]).then_inc(hnT_ready, 1)

            def choose(fu, h, par):
                chain = Chain(dve, topk_chain, fu * KU, dve_carrier, ONE)

                def first(c):
                    src = psS[:, c * NK:(c + 1) * NK]
                    if c == 0:
                        dve.wait_ge(scores_done, ONE + fu + 1)
                        carry(dve, dve_carrier)
                    chain(nc.vector.max(top[:, c, 0:8], src))
                    nc.vector.max_index(topi[:, c, 0:8], top[:, c, 0:8], src)
                    chain(nc.vector.match_replace(left[:, c, :], top[:, c, 0:8], src, -3e38))
                    chain(nc.vector.max(top[:, c, 8:16], left[:, c, :]))
                    last = nc.vector.max_index(topi[:, c, 8:16], top[:, c, 8:16], left[:, c, :])
                    if c == 1:
                        last.then_inc(scores_read, 1)
                        dve.wait_ge(scores_read, ONE + fu + 1)

                def second():
                    chain(nc.vector.tensor_copy(topf[:], topi[:]))
                    chain(nc.vector.tensor_tensor(cand[:], top[:, 0, :].unsqueeze(2).broadcast_to([P, TOPK, TOPK]),
                                                  top[:, 1, :].unsqueeze(1).broadcast_to([P, TOPK, TOPK]), ALU.add))
                    flat = cand[:].rearrange("p a b -> p (a b)")
                    chain(nc.vector.max(best[:, 0:8], flat))
                    nc.vector.max_index(besti[:, 0:8], best[:, 0:8], flat)
                    chain(nc.vector.match_replace(cleft[:], best[:, 0:8], flat, -3e38))
                    chain(nc.vector.max(best[:, 8:16], cleft[:]))
                    chain(nc.vector.max_index(besti[:, 8:16], best[:, 8:16], cleft[:]))
                    nc.vector.tensor_scalar(sm[:, 0:1], best[:, 0:1], -1.0, None, ALU.mult).then_inc(best_ready, 1)

                def places():
                    nc.vector.tensor_scalar(part[:, 0, :], besti[:], 4, None, ALU.logical_shift_right)
                    chain(nc.vector.tensor_scalar(part[:, 1, :], besti[:], 15, None, ALU.bitwise_and))
                    chain(nc.vector.tensor_copy(partf[:], part[:]))
                    for c in range(2):
                        last = nc.vector.tensor_tensor(hit[:, :, c * TOPK:(c + 1) * TOPK],
                                                partf[:, c, :].unsqueeze(2).broadcast_to([P, TOPK, TOPK]),
                                                iota[:].unsqueeze(1).broadcast_to([P, TOPK, TOPK]), ALU.is_equal)
                    chain(last)
                    for c in range(2):
                        last = nc.vector.tensor_tensor(hit[:, :, c * TOPK:(c + 1) * TOPK],
                                                hit[:, :, c * TOPK:(c + 1) * TOPK],
                                                topf[:, c, :].unsqueeze(1).broadcast_to([P, TOPK, TOPK]), ALU.mult)
                    chain(last)
                    for c in range(2):
                        last = nc.vector.reduce_sum(row[:, c, :], hit[:, :, c * TOPK:(c + 1) * TOPK], axis=AX_X)
                    chain(last)

                def finish():
                    dve.wait_ge(exp_done, ONE + fu + 1)
                    chain(nc.vector.reciprocal(sm[:, 2:3], sm[:, 1:2]))
                    nc.vector.scalar_tensor_tensor(expert[par][:, bass.ds(h * TOPK, TOPK)], row[:, 0, :], float(NK),
                                                   row[:, 1, :], ALU.mult, ALU.add)
                    nc.vector.tensor_scalar(gate[par][:, bass.ds(h * TOPK, TOPK)], ex[:], sm[:, 2:3], None,
                                            ALU.mult).then_inc(chosen, 1)
                    dve.wait_ge(chosen, ONE + fu + 1)

                return first, second, places, finish

            def prologue():
                front_tile(0, 0)
                front_turn(0)
                with dve.Fori(0, PH) as h:
                    first, second, places, finish = choose(h, h, 0)
                    first(0)
                    first(1)
                    second()
                    places()
                    finish()

            def tile_start(t, par, R, nxt):
                if nxt:
                    front_tile(t + 1, 1 - par)
                    front_turn(t + 1)

            def weigh(it, h, par, hh, R, s):
                dve.wait_ge(gelu_done, ONE + it * (TOPK // 2) + s // 2 + 1)
                nc.vector.tensor_tensor(wgt[0:R, hh, s:s + 2], act_v[0:R, hh, s:s + 2],
                                        gate[par][0:R, bass.ds(h * TOPK + s, 2)], ALU.mult).then_inc(wgt_ready, 1)

            def unit(it, h, par, hh, R, nxt):
                if nxt:
                    first, second, places, finish = choose(it + PH, h, 1 - par)
                for s in range(TOPK):
                    b = s % NBUF
                    dve.wait_ge(gathered[b], 32 * it + 16 * (s // NBUF + 1))
                    nc.vector.tensor_tensor_reduce(buf[b][0:R, 0:D], buf[b][0:R, 0:D], hn[par][0:R, :], 1.0, 0.0,
                                                   ALU.mult, ALU.add, dot[0:R, hh, s:s + 1]).then_inc(dotted, 1)
                    if s % 2 == 0 and s >= 2:
                        weigh(it, h, par, hh, R, s - 2)
                    if nxt:
                        if s == 6:
                            first(0)
                        if s == 8:
                            first(1)
                        if s == 10:
                            second()
                        if s == 12:
                            places()
                weigh(it, h, par, hh, R, TOPK - 2)
                if nxt:
                    finish()

            def tile_end(t, par, R):
                chain = Chain(dve, y_chain, t * KY, first=ONE)
                dve.wait_ge(y_root, ONE + t + 1)
                chain(nc.vector.reciprocal(st[0:R, 5:6], st[0:R, 4:5]))
                nc.vector.scalar_tensor_tensor(y[0:R, :], y[0:R, :], st[0:R, 5:6], gy[0:R, :], ALU.mult,
                                               ALU.mult).then_inc(y_ready, 1)

            tiles(dve, tile_start, unit, tile_end, prologue)

def host_arrays(inputs):
    x = np.zeros((ROWS, D), np.float32)
    x[:SEQ] = np.asarray(inputs["x_prompt"]).reshape(SEQ, D)
    x[SEQ:SEQ + SROWS] = np.asarray(inputs["x_sample"]).reshape(SROWS, D)
    a = {"x": x}
    for name in ("cache_k", "cache_v"):
        c = np.asarray(inputs[name])
        a[name] = np.ascontiguousarray(c.reshape(-1, H * VD))
    for name in ("attn_norm", "w_in", "w_out", "da_lambda_q1", "da_lambda_k1", "da_lambda_q2", "da_lambda_k2",
                 "da_subln", "rw_mu", "rw_w0", "rw_w_up", "rw_a0", "rw_a_up", "rw_g_up", "rw_k_k", "rw_k_a",
                 "rw_ln_w", "rw_ln_b", "ffn_norm", "peer_wq"):
        a[name] = np.ascontiguousarray(np.asarray(inputs[name])[0])
    for name in ("attn_norm",):
        a[name] = np.ascontiguousarray(a[name].reshape(KD, P).T)
    a["final_norm"] = np.ascontiguousarray(inputs["final_norm"])
    a["rw_r_k"] = np.ascontiguousarray(np.asarray(inputs["rw_r_k"]).reshape(RW))
    a["sub_keys"] = np.ascontiguousarray(np.asarray(inputs["peer_sub_keys"])[0].transpose(3, 0, 1, 2))
    a["experts"] = np.concatenate([np.asarray(inputs["peer_u"])[0], np.asarray(inputs["peer_v"])[0]], axis=1)
    a["page_table"] = np.ascontiguousarray(np.asarray(inputs["page_table"]).reshape(1, SB * NPAGE).astype(np.int32))
    s = np.asarray(inputs["state_wkv"])[0]
    a["state"] = np.ascontiguousarray(s.reshape(SB, RH // 2, 2, RD, RD).transpose(2, 4, 1, 0, 3).reshape(P, RH // 2, SB, RD))
    diag = np.zeros((P, RH // 2, SB, 2, RD), np.float32)
    for i in range(2):
        diag[i * RD:(i + 1) * RD, :, :, i] = a["state"][i * RD:(i + 1) * RD]
    a["state_diag"] = diag
    a["shift"] = np.ascontiguousarray(np.asarray(inputs["state_shift"])[0])
    a["ident"] = np.eye(P, dtype=np.float32)
    a["iota16"] = np.arange(TOPK, dtype=np.float32)
    at = np.arange(P)
    a["causal"] = np.where(at[None, :] <= at[:, None], 0.0, NEG).astype(np.float32)
    step, use = at % ST, at % 32 < 16
    a["new_mask"] = np.where(np.arange(ST)[None, :] <= step[:, None], 0.0, NEG).astype(np.float32)
    a["coef"] = np.stack([at % 32 < 8, use & (at % 32 >= 8)], axis=1).astype(np.float32)
    a["pick"] = (use[:, None] & ((at // 32 * ST + step)[:, None] == np.arange(4 * ST)[None, :])).astype(np.float32)
    a["prow"] = at[:, None].astype(np.float32)
    s_, t_ = at[:, None], at[None, :]
    same = s_ // CH == t_ // CH
    a["eye"] = np.concatenate([np.eye(CH)] * 2).astype(np.float32)
    a["cum_p"] = (same * ((s_ <= t_).astype(np.float32) - (s_ % CH < CH // 2))).astype(np.float32)
    a["cum_s"] = ((s_ // ST == t_ // ST) & (s_ <= t_)).astype(np.float32)
    quarter = at // (CH // 2)
    a["tot_p"] = (quarter[:, None] == np.arange(4)[None, :]).astype(np.float32)
    a["tot_s"] = (at[:, None] // ST == np.arange(SB)[None, :]).astype(np.float32)
    sc, tc = at[:, None] % CH, np.arange(CH)[None, :]
    a["tri_p"] = np.stack([sc < tc, sc <= tc], axis=1).astype(np.float32)
    one = sc // ST == tc // ST
    a["tri_s"] = np.stack([one & (sc < tc), one & (sc <= tc)], axis=1).astype(np.float32)
    a["levels"] = np.stack([(sc >> (n + 1) == tc >> (n + 1)) & (sc >> n & 1 == 0) & (tc >> n & 1 == 1)
                            for n in range(6)], axis=1).astype(np.float32)
    a["seq_of"] = np.broadcast_to((np.arange(CH)[None, :] // ST == np.arange(SB)[:, None])[None], (P, SB, CH)).astype(np.float32)
    a["seq_row"] = a["tot_s"]
    pos = np.zeros(ROWS, np.float32)
    pos[:SEQ] = np.arange(SEQ)
    pos[SEQ:SEQ + SROWS] = PAST + np.tile(np.arange(ST), SB)
    inv = np.float32(10000.0) ** (-np.arange(32, dtype=np.float32) / np.float32(32))
    ang = pos[:, None] * inv[None, :].astype(np.float32)
    cos, sin = np.cos(ang).astype(np.float32), np.sin(ang).astype(np.float32)
    a["rope"] = np.stack([cos, cos, -sin, sin], axis=1)
    return a

CONSTS = ("ident", "rope", "causal", "new_mask", "coef", "pick", "prow", "iota16", "eye", "cum_p", "cum_s", "tot_p",
          "tot_s", "tri_p", "tri_s", "levels", "seq_of", "seq_row")


def layer(nc, T):
    for stage in (in_projection, attention, time_mixing, out_projection, peer):
        with nc.cleanup_on_exit():
            stage(nc, T)


OUTS = {"y_all": (ROWS, D), "k_all": (ROWS, QK), "v_all": (ROWS, H * VD), "p_all": (ROWS, RP),
        "wkv_p": (P, RH // 2, RD), "wkv_s": (P, RH // 2, SB, RD)}
SCRATCH = {"q": (ROWS, QK), "mixed": (ROWS, D), "h": (ROWS, D)}


def kernel(**inputs):
    import concourse.bacc as bacc
    from concourse.bass_utils import run_bass_kernel_spmd

    nc = bacc.Bacc("TRN2", target_bir_lowering=False, num_devices=1)
    a = host_arrays(inputs)
    T, arrays = {}, {}
    for name, v in a.items():
        arrays[f"in_{name}"] = v
        T[name] = nc.dram_tensor(f"in_{name}", v.shape, mybir.dt.from_np(v.dtype), kind="ExternalInput").ap()
    for name, shape in OUTS.items():
        T[name] = nc.dram_tensor(f"out_{name}", shape, F32, kind="ExternalOutput").ap()
    for name, shape in SCRATCH.items():
        T[name] = nc.dram_tensor(f"scratch_{name}", shape, F32, kind="Internal").ap()
    layer(nc, T)
    r = run_bass_kernel_spmd(nc, [arrays], core_ids=[0]).results[0]
    y, k, v, p, wp, ws = (r[f"out_{n}"] for n in OUTS)
    end = SEQ + SROWS
    state = ws.reshape(2, RD, RH // 2, SB, RD).transpose(3, 2, 0, 4, 1).reshape(1, SB, RH, RD, RD)
    return (y[:SEQ].reshape(1, SEQ, D), y[SEQ:end].reshape(SB, ST, D),
            k[:SEQ].reshape(1, 1, SEQ, H, 2 * HD), v[:SEQ].reshape(1, 1, SEQ, H, VD),
            wp.reshape(2, RD, RH // 2, RD).transpose(2, 0, 3, 1).reshape(1, 1, RH, RD, RD),
            p[SEQ - 1].reshape(1, 1, RP),
            k[SEQ:end].reshape(1, SB, ST, H, 2 * HD), v[SEQ:end].reshape(1, SB, ST, H, VD),
            state, p[SEQ + ST - 1:end:ST].reshape(1, SB, RP))
```

```python
from contextlib import ExitStack

import numpy as np

import concourse.bass as bass
from concourse import mybir

F32 = mybir.dt.float32
U32 = mybir.dt.uint32
I32 = mybir.dt.int32
ALU = mybir.AluOpType
ACT = mybir.ActivationFunctionType
AX_X = mybir.AxisListType.X

P = 128
D = 1024
KD = D // P
SEQ = 1024
PT = SEQ // P
NT = PT + 1
ROWS = NT * P
SB, ST = 8, 8
SROWS = SB * ST
PAST = 512
PAGE = 128
NPAGE = PAST // PAGE
H = 4
HD = 64
VD = 128
QK = H * 2 * HD
RH = 8
RD = 64
RW = RH * RD
RP = 3 * RW + 64 + 64 + 128
IN = 2 * QK + H * VD + RP
CH = 64
GN_EPS = 64e-5
EPS = 1e-6
NEG = -1e30
LAM0 = 0.2
PH = 8
NK = 128
TOPK = 16


ONE = 1


class Chain:

    def __init__(self, eng, sem, start=0, carrier=None, first=0):
        self.eng, self.sem, self.n, self.carrier = eng, sem, start + first, carrier

    def __call__(self, ins):
        ins.then_inc(self.sem, 1)
        self.n = self.n + 1
        self.eng.wait_ge(self.sem, self.n)
        if self.carrier is not None:
            carry(self.eng, self.carrier)


class Mem:

    def __init__(self, nc, ctx, tag):
        self.nc, self.ctx, self.tag, self.sems = nc, ctx, tag, []

    def sb(self, name, shape, dt=F32):
        return self.ctx.enter_context(self.nc.sbuf_tensor(f"{self.tag}_{name}", shape, dt))

    def ps(self, name, shape, dt=F32):
        return self.ctx.enter_context(self.nc.psum_tensor(f"{self.tag}_{name}", shape, dt))

    def sem(self, name, from_zero=False):
        sem = self.nc.alloc_semaphore(f"{self.tag}_{name}")
        if not from_zero:
            self.sems.append(sem)
        return sem

    def prime(self):
        engines = (self.nc.sync, self.nc.gpsimd, self.nc.tensor, self.nc.scalar, self.nc.vector)
        for n, s in enumerate(self.sems):
            engines[n % 5].sem_inc(s, ONE)
        self.nc.all_engine_barrier()


def carry(eng, carrier):
    eng.sem_inc(carrier, 1)


def rows(t, n=P):
    return bass.ds(t * P, n)


def in_projection(nc, T):
    NG = (IN + 511) // 512
    cols = [(n * 512, min(512, IN - n * 512)) for n in range(NG)]
    NB = 6
    with ExitStack() as ctx:
        m = Mem(nc, ctx, "ip")
        w = m.sb("w", [P, KD, IN])
        x = m.sb("x", [P, D])
        sq = m.sb("sq", [P, D])
        xs = m.sb("xs", [P, D])
        xT = m.sb("xT", [P, KD, P])
        g = m.sb("g", [P, KD])
        ident = m.sb("ident", [P, P])
        stat = m.sb("stat", [P, 4])
        rope = m.sb("rope", [P, 4, 32])
        prod = m.sb("prod", [P, 2, QK])
        swap = m.sb("swap", [P, 2, QK])
        qk = m.sb("qk", [P, 2, QK])
        v = m.sb("v", [P, QK])
        rw = m.sb("rw", [P, RP])
        psT = m.ps("psT", [P, KD, P])
        psG = m.ps("psG", [P, NB, 512])

        const_in = m.sem("const_in")
        w_in = [m.sem(f"w_in{n}") for n in range(NG)]
        x_in = m.sem("x_in")
        eps_set = m.sem("eps_set")
        summed = m.sem("summed")
        squared = m.sem("squared")
        scaled = m.sem("scaled")
        turned = m.sem("turned")
        xT_ready = m.sem("xT_ready")
        group_done = m.sem("group_done")
        rotated = m.sem("rotated")
        copied = m.sem("copied")
        stored = m.sem("stored")
        dve_chain = m.sem("dve_chain")
        m.prime()
        block = ctx.enter_context(nc.Block())

        def store(sp, t):
            sp.wait_ge(rotated, ONE + 2 * t + 2)
            sp.dma_start(T["q"][rows(t), :], qk[:, 0, :]).then_inc(stored, 16)
            sp.dma_start(T["k_all"][rows(t), :], qk[:, 1, :]).then_inc(stored, 16)
            sp.wait_ge(copied, ONE + (NG - 2) * (t + 1))
            sp.dma_start(T["v_all"][rows(t), :], v[:]).then_inc(stored, 16)
            sp.dma_start(T["p_all"][rows(t), :], rw[:]).then_inc(stored, 16)

        @block.sync
        def _(sp):
            sp.dma_start(x[:], T["x"][0:P, :]).then_inc(x_in, 16)
            sp.dma_start(rope[:], T["rope"][0:P, :, :]).then_inc(x_in, 16)
            sp.dma_start(g[:], T["attn_norm"]).then_inc(const_in, 16)
            sp.dma_start(ident[:], T["ident"]).then_inc(const_in, 16)
            for n, (c0, cn) in enumerate(cols):
                sp.dma_start(w[:, :, c0:c0 + cn],
                             T["w_in"].rearrange("(k p) n -> p k n", p=P)[:, :, c0:c0 + cn]).then_inc(w_in[n], 16)
            with sp.Fori(0, NT - 1) as t:
                sp.wait_ge(scaled, ONE + t + 1)
                sp.dma_start(x[:], T["x"][rows(t + 1), :]).then_inc(x_in, 16)
                sp.wait_ge(rotated, ONE + 2 * t + 2)
                sp.dma_start(rope[:], T["rope"][rows(t + 1), :, :]).then_inc(x_in, 16)
                store(sp, t)
            store(sp, NT - 1)
            sp.wait_ge(stored, ONE + 64 * NT)

        @block.scalar
        def _(act):
            act.wait_ge(eps_set, ONE + 1)
            with act.Fori(0, NT) as t:
                act.wait_ge(x_in, ONE + 32 * t + 32)
                act.wait_ge(scaled, ONE + t)
                nc.scalar.activation(sq[:], x[:], ACT.Square, accum_out=stat[:, 0:1]).then_inc(summed, 1)
                act.wait_ge(summed, ONE + t + 1)
                nc.scalar.activation(stat[:, 1:2], stat[:, 0:1], ACT.Sqrt, bias=stat[:, 3:4],
                                     scale=1.0 / D).then_inc(squared, 1)
                act.wait_ge(stored, ONE + 64 * t)
                for n in range(2, NG):
                    c0, cn = cols[n]
                    act.wait_ge(group_done, ONE + NG * t + n + 1)
                    dst = v[:] if n == 2 else rw[:, c0 - 3 * QK:c0 - 3 * QK + cn]
                    nc.scalar.activation(dst, psG[:, n % NB, 0:cn], ACT.Copy).then_inc(copied, 1)

        @block.vector
        def _(dve):
            nc.vector.memset(stat[:, 3:4], EPS).then_inc(eps_set, 1)
            K = 3
            with dve.Fori(0, NT) as t:
                chain = Chain(dve, dve_chain, K * t, first=ONE)
                dve.wait_ge(squared, ONE + t + 1)
                chain(nc.vector.reciprocal(stat[:, 2:3], stat[:, 1:2]))
                dve.wait_ge(turned, ONE + t)
                nc.vector.tensor_scalar(xs[:], x[:], stat[:, 2:3], None, ALU.mult).then_inc(scaled, 1)
                dve.wait_ge(group_done, ONE + NG * t)
                dve.wait_ge(const_in, ONE + 32)
                dve.wait_ge(turned, ONE + t + 1)
                nc.vector.tensor_tensor(xT[:], psT[:], g[:].unsqueeze(2).broadcast_to([P, KD, P]),
                                        ALU.mult).then_inc(xT_ready, 1)
                cos = rope[:, 0:2, :].unsqueeze(1).broadcast_to([P, 2 * H, 2, 32])
                for n in range(2):
                    dve.wait_ge(group_done, ONE + NG * t + n + 1)
                    src = psG[:, n, :].rearrange("p (h s d) -> p h s d", h=2 * H, s=2)
                    pr = prod[:, n, :].rearrange("p (h s d) -> p h s d", h=2 * H, s=2)
                    sw = swap[:, n, :].rearrange("p (h s d) -> p h s d", h=2 * H, s=2)
                    nc.vector.tensor_tensor(pr, src, cos, ALU.mult)
                    for s in range(2):
                        sin = rope[:, 2 + s, :].unsqueeze(1).broadcast_to([P, 2 * H, 32])
                        last = nc.vector.tensor_tensor(sw[:, :, s, :], src[:, :, 1 - s, :], sin, ALU.mult)
                    chain(last)
                    dve.wait_ge(stored, ONE + 64 * t)
                    nc.vector.tensor_tensor(qk[:, n, :], prod[:, n, :], swap[:, n, :], ALU.add).then_inc(rotated, 1)
                dve.wait_ge(rotated, ONE + 2 * t + 2)

        @block.tensor
        def _(pe):
            pe.wait_ge(const_in, ONE + 32)
            with pe.Fori(0, NT) as t:
                pe.wait_ge(scaled, ONE + t + 1)
                pe.wait_ge(xT_ready, ONE + t)
                for k in range(KD):
                    last = nc.tensor.transpose(psT[:, k, :], xs[:, k * P:(k + 1) * P], ident[:])
                last.then_inc(turned, 1)
                pe.wait_ge(xT_ready, ONE + t + 1)
                for n, (c0, cn) in enumerate(cols):
                    if n < 2:
                        pe.wait_ge(rotated, ONE + 2 * t)
                        pe.wait_ge(copied, ONE + (NG - 2) * t)
                    elif n >= NB:
                        pe.wait_ge(rotated, ONE + 2 * t + n - NB + 1)
                    else:
                        pe.wait_ge(copied, ONE + (NG - 2) * t)
                    pe.wait_ge(w_in[n], ONE + 16)
                    for k in range(KD):
                        last = nc.tensor.matmul(psG[:, n % NB, 0:cn], xT[:, k, :], w[:, k, c0:c0 + cn],
                                                start=(k == 0), stop=(k == KD - 1))
                    last.then_inc(group_done, 1)

def attention(nc, T):
    SC = HD ** -0.5
    NU = PT * H
    KEYS = PAST + ST
    with ExitStack() as ctx:
        m = Mem(nc, ctx, "at")
        ident = m.sb("ident", [P, P])
        causal = m.sb("causal", [P, P])
        lam_in = m.sb("lam_in", [P, 4, HD])
        lam_pr = m.sb("lam_pr", [P, 2, HD])
        lam = m.sb("lam", [P, 4])
        subln = m.sb("subln", [P, VD])
        stat = m.sb("stat", [P, 1])
        qs = m.sb("q", [P, QK])
        ks = m.sb("k", [P, QK])
        qT = m.sb("qT", [P, H, P])
        kT = m.sb("kT", [P, H, SEQ])
        vs = m.sb("v", [P, PT, H * VD])
        prob = m.sb("prob", [P, 2, SEQ])
        A = m.sb("A", [P, SEQ])
        AT = m.sb("AT", [P, SEQ])
        mx = m.sb("mx", [P, 2])
        sums = m.sb("sums", [P, 2])
        inv = m.sb("inv", [P, 4])
        sq = m.sb("sq", [P, H, VD])
        hst = m.sb("hst", [P, 4, H])
        o = m.sb("o", [P, H, VD])
        pages = m.sb("pages", [P, SB * NPAGE], I32)
        pagef = m.sb("pagef", [P, SB * NPAGE])
        prow = m.sb("prow", [P, 1])
        pidx = m.sb("pidx", [P, SB * NPAGE], U32)
        kp = [m.sb(f"kp{i}", [P, NPAGE, QK]) for i in range(2)]
        vp = [m.sb(f"vp{i}", [P, NPAGE, H * VD]) for i in range(2)]
        vnew = m.sb("vnew", [ST, SB, H * VD])
        QB = m.sb("QB", [P, SB, H, 4, ST])
        kpT = m.sb("kpT", [P, H, PAST])
        knT = m.sb("knT", [P, H, SROWS])
        new_mask = m.sb("new_mask", [P, ST])
        coef = m.sb("coef", [P, 2])
        pick = m.sb("pick", [P, 4 * ST])
        pickw = m.sb("pickw", [P, 4 * ST])
        ATs = m.sb("ATs", [P, NPAGE + 1, 4 * ST])
        wrow = m.sb("wrow", [P, 2])
        coefl = m.sb("coefl", [P, 1])
        oT = m.sb("oT", [P, H, SROWS])
        psA = m.ps("psA", [P, 2, SEQ])
        psX = m.ps("psX", [P, SEQ])
        psO = m.ps("psO", [P, H, VD])
        psK = m.ps("psK", [P, H, P])

        const_in = m.sem("const_in")
        page_in = m.sem("page_in")
        pidx_ready = m.sem("pidx_ready")
        q_in = m.sem("q_in")
        k_in = m.sem("k_in")
        v_in = [m.sem(f"v_in{i}") for i in range(PT + 1)]
        kp_in = [m.sem(f"kp_in{i}") for i in range(2)]
        vp_in = [m.sem(f"vp_in{i}") for i in range(2)]
        lam_chain = m.sem("lam_chain")
        lam_exp = m.sem("lam_exp")
        lam_ready = m.sem("lam_ready")
        turned = m.sem("turned")
        turn_copied = m.sem("turn_copied")
        scored = m.sem("scored")
        chain_s = m.sem("chain")
        max_ready = m.sem("max_ready")
        exp_done = m.sem("exp_done")
        A_ready = m.sem("A_ready")
        A_turned = m.sem("A_turned")
        AT_ready = m.sem("AT_ready")
        pv_done = m.sem("pv_done")
        o_squared = m.sem("o_squared")
        o_sums = m.sem("o_sums")
        o_root = m.sem("o_root")
        o_ready = m.sem("o_ready")
        o_stored = m.sem("o_stored")
        QB_zero = m.sem("QB_zero")
        kp_turned = m.sem("kp_turned")
        kp_copied = m.sem("kp_copied")
        pickw_ready = m.sem("pickw_ready")
        pages_used = m.sem("pages_used")
        ATs_done = m.sem("ATs_done")
        ATs_copied = m.sem("ATs_copied")
        oT_copied = m.sem("oT_copied")
        block = ctx.enter_context(nc.Block())
        NCONST = 11

        def store(sp, t):
            n = P if t < PT else SROWS
            sp.wait_ge(o_ready, t + 1)
            sp.dma_start(T["mixed"][t * P:t * P + n, 0:H * VD], o[0:n].rearrange("p h d -> p (h d)")
                         ).then_inc(o_stored, 16)

        @block.sync
        def _(sp):
            for n, name in enumerate(("da_lambda_q1", "da_lambda_k1", "da_lambda_q2", "da_lambda_k2")):
                sp.dma_start(lam_in[:, n, :], T[name].partition_broadcast(P)).then_inc(const_in, 16)
            for dst, name in ((ident, "ident"), (causal, "causal"), (new_mask, "new_mask"), (coef, "coef"),
                              (pick, "pick"), (prow, "prow")):
                sp.dma_start(dst[:], T[name]).then_inc(const_in, 16)
            sp.dma_start(subln[:], T["da_subln"].partition_broadcast(P)).then_inc(const_in, 16)
            sp.dma_start(pages[:], T["page_table"].broadcast_to([P, SB * NPAGE])).then_inc(page_in, 16)
            for t in range(NT):
                if t:
                    sp.wait_ge(turned, 2 * t)
                sp.dma_start(ks[:], T["k_all"][t * P:(t + 1) * P, :]).then_inc(k_in, 16)
                sp.dma_start(qs[:], T["q"][t * P:(t + 1) * P, :]).then_inc(q_in, 16)
                if t < PT:
                    sp.dma_start(vs[:, t, :], T["v_all"][t * P:(t + 1) * P, :]).then_inc(v_in[t], 16)
                else:
                    sp.dma_start(vnew[:], T["v_all"][SEQ:SEQ + SROWS, :].rearrange("(b s) n -> s b n", s=ST)
                                 ).then_inc(v_in[t], 16)
                if t:
                    store(sp, t - 1)
            store(sp, PT)
            sp.wait_ge(o_stored, 16 * NT)

        @block.gpsimd
        def _(pool):
            nc.gpsimd.memset(QB[:], 0.0).then_inc(QB_zero, 1)
            pool.wait_ge(pidx_ready, 1)
            for b in range(SB):
                if b >= 2:
                    pool.wait_ge(pages_used, b - 1)
                for dst, src, s in ((kp, "cache_k", kp_in), (vp, "cache_v", vp_in)):
                    for g in range(NPAGE):
                        pool.indirect_dma_start(dst[b % 2][:, g, :], None, T[src], bass.IndirectOffsetOnAxis(
                            ap=pidx[:, b * NPAGE + g:b * NPAGE + g + 1], axis=0)).then_inc(s[b % 2], 16)

        @block.tensor
        def _(pe):
            pe.wait_ge(const_in, 16 * NCONST)

            def turn(t):
                for n, (src, s) in enumerate(((ks, k_in), (qs, q_in))):
                    pe.wait_ge(s, 16 * (t + 1))
                    pe.wait_ge(turn_copied, 2 * t + n)
                    for h in range(H):
                        last = nc.tensor.transpose(psK[:, h, :], src[:, h * P:(h + 1) * P], ident[:])
                    last.then_inc(turned, 1)

            def score(u):
                t, h = u // H, u % H
                pe.wait_ge(turn_copied, 2 * t + 2)
                if u:
                    pe.wait_ge(exp_done, 2 * u)
                n = (t + 1) * P
                for c in range(2):
                    for k0 in range(0, n, 512):
                        kn = min(512, n - k0)
                        last = nc.tensor.matmul(psA[:, c, k0:k0 + kn], qT[c * HD:(c + 1) * HD, h, :],
                                                kT[c * HD:(c + 1) * HD, h, k0:k0 + kn], start=True, stop=True)
                    last.then_inc(scored, 1)

            def value(u):
                t, h = u // H, u % H
                pe.wait_ge(A_ready, u + 1)
                if u:
                    pe.wait_ge(AT_ready, u)
                for b in range(t + 1):
                    last = nc.tensor.transpose(psX[:, b * P:(b + 1) * P], A[:, b * P:(b + 1) * P], ident[:])
                last.then_inc(A_turned, 1)
                pe.wait_ge(AT_ready, u + 1)
                if h == 0 and t:
                    pe.wait_ge(o_ready, t)
                if h == 0:
                    pe.wait_ge(v_in[t], 16)
                for b in range(t + 1):
                    last = nc.tensor.matmul(psO[:, h, :], AT[:, b * P:(b + 1) * P], vs[:, b, h * VD:(h + 1) * VD],
                                            start=(b == 0), stop=(b == t))
                last.then_inc(pv_done, 1)

            turn(0)
            score(0)
            for u in range(NU):
                if (u + 1) % H == 0 and u + 1 <= NU:
                    turn((u + 1) // H)
                if u + 1 < NU:
                    score(u + 1)
                value(u)
            pe.wait_ge(turn_copied, 2 * NT)
            pe.wait_ge(v_in[PT], 16)
            for b in range(SB):
                pe.wait_ge(kp_in[b % 2], 16 * NPAGE * (b // 2 + 1))
                for hp in range(2):
                    pe.wait_ge(kp_copied, 2 * b + hp)
                    if b == 0 and hp == 0:
                        pe.wait_ge(AT_ready, NU)
                    for h in range(2):
                        for g in range(NPAGE):
                            hh = 2 * hp + h
                            last = nc.tensor.transpose(psX[:, (h * NPAGE + g) * P:(h * NPAGE + g + 1) * P],
                                                       kp[b % 2][:, g, hh * P:(hh + 1) * P], ident[:])
                    last.then_inc(kp_turned, 1)
                pe.wait_ge(kp_copied, 2 * b + 2)
                pe.wait_ge(exp_done, 2 * NU + b)
                for h in range(H):
                    lhs = QB[:, b, h, :, :].rearrange("p c t -> p (c t)")
                    nc.tensor.matmul(psA[32 * h:32 * h + 32, 0, 0:PAST], lhs, kpT[:, h, :], start=True, stop=True)
                for h in range(H):
                    lhs = QB[:, b, h, :, :].rearrange("p c t -> p (c t)")
                    last = nc.tensor.matmul(psA[32 * h:32 * h + 32, 0, PAST:KEYS], lhs,
                                            knT[:, h, b * ST:(b + 1) * ST], start=True, stop=True)
                last.then_inc(scored, 1)
                pe.wait_ge(pickw_ready, b + 1)
                pe.wait_ge(ATs_copied, b)
                for g in range(NPAGE):
                    nc.tensor.matmul(psK[:, 0, g * 32:(g + 1) * 32], prob[:, 0, g * P:(g + 1) * P], pickw[:],
                                     start=True, stop=True)
                nc.tensor.matmul(psK[0:ST, 1, 0:32], prob[:, 0, PAST:KEYS], pickw[:],
                                 start=True, stop=True).then_inc(ATs_done, 1)
                pe.wait_ge(ATs_copied, b + 1)
                pe.wait_ge(vp_in[b % 2], 16 * NPAGE * (b // 2 + 1))
                if b == 0:
                    pe.wait_ge(o_ready, PT)
                for h in range(H):
                    out = psO[:, h, b * ST:(b + 1) * ST]
                    for g in range(NPAGE):
                        nc.tensor.matmul(out, vp[b % 2][:, g, h * VD:(h + 1) * VD], ATs[:, g, h * ST:(h + 1) * ST],
                                         start=(g == 0), stop=False)
                    last = nc.tensor.matmul(out, vnew[:, b, h * VD:(h + 1) * VD],
                                            ATs[0:ST, NPAGE, h * ST:(h + 1) * ST], start=False, stop=True)
                last.then_inc(pages_used, 1)
            pe.wait_ge(oT_copied, 1)
            for h in range(H):
                last = nc.tensor.transpose(psK[0:SROWS, h, :], oT[:, h, :], ident[:])
            last.then_inc(pv_done, 1)

        @block.scalar
        def _(act):
            act.wait_ge(lam_chain, 1)
            nc.scalar.activation(lam[:, 0:2], lam[:, 2:4], ACT.Exp).then_inc(lam_exp, 1)

            def expo(u):
                n = (u // H + 1) * P
                for c in range(2):
                    act.wait_ge(max_ready, 2 * u + c + 1)
                    if u:
                        act.wait_ge(A_ready, u)
                    nc.scalar.activation(prob[:, c, 0:n], psA[:, c, 0:n], ACT.Exp, bias=mx[:, c:c + 1],
                                         accum_out=sums[:, c:c + 1]).then_inc(exp_done, 1)

            def copy_AT(u):
                n = (u // H + 1) * P
                act.wait_ge(A_turned, u + 1)
                if u:
                    act.wait_ge(pv_done, u)
                nc.scalar.activation(AT[:, 0:n], psX[:, 0:n], ACT.Copy).then_inc(AT_ready, 1)

            def square(t, src, R):
                nc.scalar.activation(sq[0:R], src, ACT.Square).then_inc(o_squared, 1)
                act.wait_ge(o_sums, t + 1)
                nc.scalar.activation(hst[0:R, 1, :], hst[0:R, 0, :], ACT.Sqrt, bias=stat[0:R],
                                     scale=1.0 / VD).then_inc(o_root, 1)

            for u in range(NU):
                expo(u)
                copy_AT(u)
                if u % H == H - 1:
                    act.wait_ge(pv_done, u + 1)
                    square(u // H, psO[:], P)
            for b in range(SB):
                for hp in range(2):
                    act.wait_ge(kp_turned, 2 * b + hp + 1)
                    if b:
                        act.wait_ge(scored, 2 * NU + b)
                    nc.scalar.activation(kpT[:, 2 * hp:2 * hp + 2, :].rearrange("p h k -> p (h k)"), psX[:],
                                         ACT.Copy).then_inc(kp_copied, 1)
                act.wait_ge(max_ready, 2 * NU + b + 1)
                act.wait_ge(ATs_done, b)
                act.wait_ge(A_ready, NU)
                nc.scalar.activation(prob[:, 0, 0:KEYS], psA[:, 0, 0:KEYS], ACT.Exp, bias=mx[:, 0:1],
                                     accum_out=sums[:, 0:1]).then_inc(exp_done, 1)
            act.wait_ge(pv_done, NU + 1)
            square(PT, psK[0:SROWS], SROWS)

        @block.vector
        def _(dve):
            chain = Chain(dve, chain_s)
            chain(nc.vector.memset(stat[:], EPS))
            dve.wait_ge(const_in, 16 * NCONST)
            for n in range(2):
                nc.vector.tensor_tensor_reduce(lam_pr[:, n, :], lam_in[:, 2 * n, :], lam_in[:, 2 * n + 1, :], 1.0, 0.0,
                                               ALU.mult, ALU.add, lam[:, 2 + n:3 + n])
            nc.vector.memset(hst[:], 0.0).then_inc(lam_chain, 1)
            dve.wait_ge(lam_exp, 1)
            chain(nc.vector.tensor_tensor(lam[:, 2:3], lam[:, 1:2], lam[:, 0:1], ALU.subtract))
            chain(nc.vector.tensor_scalar(lam[:, 3:4], lam[:, 2:3], LAM0, None, ALU.subtract))
            nc.vector.scalar_tensor_tensor(coefl[:], coef[:, 1:2], lam[:, 3:4], coef[:, 0:1], ALU.mult,
                                           ALU.add).then_inc(lam_ready, 1)
            dve.wait_ge(page_in, 16)
            chain(nc.vector.tensor_copy(pagef[:], pages[:]))
            nc.vector.tensor_scalar(pidx[:], pagef[:], float(PAGE), prow[:, 0:1], ALU.mult,
                                    ALU.add).then_inc(pidx_ready, 1)

            def copy_turn(t):
                dve.wait_ge(turned, 2 * t + 1)
                if t < PT:
                    nc.vector.tensor_copy(kT[:, :, t * P:(t + 1) * P], psK[:]).then_inc(turn_copied, 1)
                    dve.wait_ge(turned, 2 * t + 2)
                    if t:
                        dve.wait_ge(scored, 2 * H * t)
                    nc.vector.tensor_scalar(qT[:], psK[:], SC, None, ALU.mult).then_inc(turn_copied, 1)
                else:
                    nc.vector.tensor_copy(knT[:], psK[:, :, 0:SROWS]).then_inc(turn_copied, 1)
                    dve.wait_ge(turned, 2 * t + 2)
                    dve.wait_ge(QB_zero, 1)
                    for c in range(2):
                        for h in range(H):
                            part = slice(c * HD, (c + 1) * HD)
                            last = nc.vector.tensor_scalar(
                                QB[part, :, h, c, :], psK[part, h, 0:SROWS].rearrange("p (b t) -> p b t", t=ST), SC, None,
                                ALU.mult)
                    last.then_inc(turn_copied, 1)

            def maxima(u):
                n = (u // H + 1) * P
                for c in range(2):
                    dve.wait_ge(scored, 2 * u + c + 1)
                    chain(nc.vector.tensor_tensor(psA[:, c, n - P:n], psA[:, c, n - P:n], causal[:], ALU.add))
                    dve.wait_ge(exp_done, 2 * u)
                    chain(nc.vector.reduce_max(inv[:, 2:3], psA[:, c, 0:n], axis=AX_X))
                    nc.vector.tensor_scalar(mx[:, c:c + 1], inv[:, 2:3], -1.0, None, ALU.mult).then_inc(max_ready, 1)
                    dve.wait_ge(max_ready, 2 * u + c + 1)

            def combine(u):
                n = (u // H + 1) * P
                dve.wait_ge(exp_done, 2 * u + 2)
                chain(nc.vector.reciprocal(inv[:, 0:2], sums[:]))
                chain(nc.vector.tensor_tensor(inv[:, 3:4], inv[:, 1:2], lam[:, 3:4], ALU.mult))
                chain(nc.vector.tensor_scalar(prob[:, 1, 0:n], prob[:, 1, 0:n], inv[:, 3:4], None, ALU.mult))
                if u:
                    dve.wait_ge(A_turned, u)
                nc.vector.scalar_tensor_tensor(A[:, 0:n], prob[:, 0, 0:n], inv[:, 0:1], prob[:, 1, 0:n], ALU.mult,
                                               ALU.add).then_inc(A_ready, 1)

            def norm(t, src, R):
                dve.wait_ge(o_squared, t + 1)
                nc.vector.reduce_sum(hst[0:R, 0, :], sq[0:R], axis=AX_X).then_inc(o_sums, 1)
                dve.wait_ge(o_root, t + 1)
                chain(nc.vector.reciprocal(hst[0:R, 2, :], hst[0:R, 1, :]))
                dve.wait_ge(o_stored, 16 * t)
                chain(nc.vector.tensor_tensor(o[0:R], src, hst[0:R, 2, :].unsqueeze(2).broadcast_to([R, H, VD]),
                                              ALU.mult))
                nc.vector.scalar_tensor_tensor(o[0:R], o[0:R], 1.0 - LAM0,
                                               subln[0:R].unsqueeze(1).broadcast_to([R, H, VD]), ALU.mult,
                                               ALU.mult).then_inc(o_ready, 1)

            dve.wait_ge(lam_ready, 1)
            copy_turn(0)
            maxima(0)
            for u in range(NU):
                combine(u)
                if (u + 1) % H == 0:
                    copy_turn((u + 1) // H)
                if u + 1 < NU:
                    maxima(u + 1)
                if u % H == H - 1:
                    norm(u // H, psO[:], P)
            for b in range(SB):
                dve.wait_ge(scored, 2 * NU + b + 1)
                chain(nc.vector.tensor_tensor(psA[:, 0, PAST:KEYS], psA[:, 0, PAST:KEYS], new_mask[:], ALU.add))
                dve.wait_ge(exp_done, 2 * NU + b)
                chain(nc.vector.reduce_max(inv[:, 2:3], psA[:, 0, 0:KEYS], axis=AX_X))
                nc.vector.tensor_scalar(mx[:, 0:1], inv[:, 2:3], -1.0, None, ALU.mult).then_inc(max_ready, 1)
                dve.wait_ge(exp_done, 2 * NU + b + 1)
                chain(nc.vector.reciprocal(wrow[:, 0:1], sums[:, 0:1]))
                chain(nc.vector.tensor_tensor(wrow[:, 1:2], wrow[:, 0:1], coefl[:], ALU.mult))
                dve.wait_ge(ATs_done, b)
                nc.vector.tensor_scalar(pickw[:], pick[:], wrow[:, 1:2], None, ALU.mult).then_inc(pickw_ready, 1)
                dve.wait_ge(ATs_done, b + 1)
                dve.wait_ge(pages_used, b)
                nc.vector.tensor_copy(ATs[:, 0:NPAGE, :], psK[:, 0, :].rearrange("p (g t) -> p g t", g=NPAGE))
                nc.vector.tensor_copy(ATs[0:ST, NPAGE, :], psK[0:ST, 1, 0:32]).then_inc(ATs_copied, 1)
            dve.wait_ge(pages_used, SB)
            nc.vector.tensor_copy(oT[:], psO[:, :, 0:SROWS]).then_inc(oT_copied, 1)
            norm(PT, psK[0:SROWS], SROWS)

class CountedChain(Chain):

    def __init__(self, eng, sem, times, per):
        super().__init__(eng, sem, times * per, first=ONE)
        self.per, self.calls = per, 0

    def __call__(self, ins):
        super().__call__(ins)
        self.calls += 1

    def end(self, last=False):
        if not last and self.calls != self.per:
            raise ValueError(f"the chain has {self.calls} instructions a turn, not {self.per}")


def time_mixing(nc, T):
    W = RW
    LEVELS = 6
    SLEVELS = 3
    NPAIR = RH // 2
    with ExitStack() as ctx:
        m = Mem(nc, ctx, "tm")
        ident = m.sb("ident", [P, P])
        eye = m.sb("eye", [P, CH])
        vec = {n: m.sb(n, [P, W]) for n in ("w0", "a0", "k_k", "k_a", "r_k", "ln_w", "ln_b")}
        mu = m.sb("mu", [P, RP])
        wa_up = m.sb("wa_up", [P, W])
        g_up = m.sb("g_up", [P, W])
        cum_l = [m.sb("cum_p", [P, P]), m.sb("cum_s", [P, P])]
        tot = [m.sb("tot_p", [P, 4]), m.sb("tot_s", [P, SB])]
        tri = [m.sb("tri_p", [P, 2, CH]), m.sb("tri_s", [P, 2, CH])]
        lev = m.sb("lev", [P, LEVELS, CH])
        seq_of = m.sb("seq_of", [P, SB, CH])
        seq_row = m.sb("seq_row", [P, SB])
        stat = m.sb("stat", [P, 1])
        p = m.sb("p", [P, RP])
        prev = m.sb("prev", [P, RP])
        ps = m.sb("ps", [P, RP])
        lo = m.sb("lo", [P, 2 * P])
        loT = m.sb("loT", [P, 2, P])
        z = m.sb("z", [P, W])
        lw = m.sb("lw", [P, W])
        a = m.sb("a", [P, W])
        g = m.sb("g", [P, W])
        kk = m.sb("kk", [P, W])
        k2 = m.sb("k2", [P, W])
        bb = m.sb("bb", [P, W])
        e_in = m.sb("e_in", [P, W])
        e_out = m.sb("e_out", [P, W])
        e_bef = m.sb("e_bef", [P, W])
        sq = m.sb("sq", [P, W])
        rt = m.sb("rt", [P, W])
        kq = m.sb("kq", [P, W])
        bt = m.sb("bt", [P, W])
        kt = m.sb("kt", [P, W])
        ep = m.sb("ep", [P, NPAIR, SB])
        hs = m.sb("hs", [P, 8, RH])
        qrT = m.sb("qrT", [P, 2, NPAIR, P])
        bkT = m.sb("bkT", [P, 2, NPAIR, P])
        AB = m.sb("AB", [P, RH, 2, CH])
        AK = m.sb("AK", [P, RH, 2, CH])
        ML = m.sb("ML", [P, LEVELS, RH * CH])
        Tn = m.sb("Tn", [P, RH, CH])
        Tt = m.sb("Tt", [P, RH, CH])
        X = m.sb("X", [P, RH, CH])
        state = m.sb("state", [P, NPAIR, RD])
        Sp = m.sb("Sp", [P, NPAIR, 2, RD])
        R_ = m.sb("R", [P, W])
        SA = m.sb("SA", [P, W])
        yc = m.sb("yc", [P, W])
        bon = m.sb("bon", [P, W])
        out = m.sb("out", [P, W])
        sstate = m.sb("sstate", [P, NPAIR, SB, RD])
        sdiag = m.sb("sdiag", [P, NPAIR, SB, 2, RD])
        big = m.sb("big", [P, 2 * NPAIR, SB, CH])
        PS = m.ps("PS", [P, 8, 512])

        names = """const_in p_in prev_in sstate_in eps_set prev_set mixed kk_scaled lo_ready lo_sig lo_turned lo_copied
            lora_done z_ready z_exp lw_ready za_ready a_tanh g_copied cum_done e_ready bef_ready bef_exp
            kk_squared kk_sum kk_root scaled_ready turned_ready turned_copied pair_done masked level_masks
            x_done x_copied y_done t_ready sp_ready r_done r_copied sa_done sa_copied yy_done st_done
            state_ready y_centered y_squared y_sum y_root y_scaled bonus_in out_ready out_stored state_stored chain pool_chain
            big_ready rk_ready carrier""".split()
        s = {n: m.sem(n) for n in names}
        NCONST = 1 + len(vec) + 3 + 11
        m.prime()
        block = ctx.enter_context(nc.Block())

        SBANK = (0, 1, 2, 7)

        def heads(ap, n=RH):
            return ap.rearrange("p (h d) -> p h d", h=n)

        @block.sync
        def _(sp):
            sp.dma_start(p[:], T["p_all"][0:P, :]).then_inc(s["p_in"], 16)
            sp.wait_ge(s["prev_set"], ONE + 1)
            sp.dma_start(prev[1:P, :], T["p_all"][0:P - 1, :]).then_inc(s["prev_in"], 16)
            sp.dma_start(mu[:], T["rw_mu"].partition_broadcast(P)).then_inc(s["const_in"], 16)
            for n in vec:
                sp.dma_start(vec[n][:], T["rw_" + n].partition_broadcast(P)).then_inc(s["const_in"], 16)
            sp.dma_start(wa_up[0:64, :], T["rw_w_up"]).then_inc(s["const_in"], 16)
            sp.dma_start(wa_up[64:128, :], T["rw_a_up"]).then_inc(s["const_in"], 16)
            sp.dma_start(g_up[:], T["rw_g_up"]).then_inc(s["const_in"], 16)
            for dst, n in ((ident, "ident"), (eye, "eye"), (cum_l[0], "cum_p"), (cum_l[1], "cum_s"), (tot[0], "tot_p"),
                           (tot[1], "tot_s"), (tri[0], "tri_p"), (tri[1], "tri_s"), (lev, "levels"),
                           (seq_of, "seq_of"), (seq_row, "seq_row")):
                sp.dma_start(dst[:], T[n]).then_inc(s["const_in"], 16)
            sp.dma_start(sstate[:], T["state"]).then_inc(s["sstate_in"], 16)
            sp.dma_start(sdiag[:], T["state_diag"]).then_inc(s["sstate_in"], 16)

            def store(t, n):
                sp.wait_ge(s["out_ready"], ONE + t + 1)
                sp.dma_start(T["mixed"][rows(t, n), RW:2 * RW], out[0:n, :]).then_inc(s["out_stored"], 16)

            with sp.Fori(0, PT - 1) as t:
                sp.wait_ge(s["mixed"], ONE + t + 1)
                sp.dma_start(p[:], T["p_all"][rows(t + 1), :]).then_inc(s["p_in"], 16)
                sp.dma_start(prev[:], T["p_all"][bass.ds((t + 1) * P - 1, P), :]).then_inc(s["prev_in"], 16)
                store(t, P)
            sp.wait_ge(s["mixed"], ONE + PT)
            sp.dma_start(p[0:SROWS], T["p_all"][SEQ:SEQ + SROWS, :]).then_inc(s["p_in"], 16)
            sp.dma_start(prev[0:SROWS], T["p_all"][SEQ - 1:SEQ + SROWS - 1, :]).then_inc(s["prev_in"], 16)
            sp.wait_ge(s["prev_in"], ONE + 16 * NT)
            sp.dma_start(prev[0:SROWS:ST, :], T["shift"]).then_inc(s["prev_in"], 16)
            store(PT - 1, P)
            sp.wait_ge(s["state_ready"], ONE + 2 * PT)
            sp.dma_start(T["wkv_p"], state[:]).then_inc(s["state_stored"], 16)
            store(PT, SROWS)
            sp.wait_ge(s["state_ready"], ONE + 2 * PT + 1)
            sp.dma_start(T["wkv_s"], sstate[:]).then_inc(s["state_stored"], 16)
            sp.wait_ge(s["out_stored"], ONE + 16 * NT)
            sp.wait_ge(s["state_stored"], ONE + 32)

        def times(body):
            def run(eng):
                with eng.Fori(0, PT) as t:
                    body(t, P, 0)
                body(PT, SROWS, 1)
            return run

        @block.gpsimd
        def _(pool):
            nc.gpsimd.memset(prev[0:1, :], 0.0).then_inc(s["prev_set"], 1)
            nc.gpsimd.memset(stat[:], EPS).then_inc(s["eps_set"], 1)
            pool.wait_ge(s["const_in"], ONE + 16 * NCONST)

            def body(t, R, smp):
                chain = CountedChain(pool, s["pool_chain"], t, 3)
                pool.wait_ge(s["p_in"], ONE + 16 * (t + 1))
                pool.wait_ge(s["prev_in"], ONE + 16 * (t + 1) + 16 * smp)
                chain(nc.gpsimd.tensor_tensor(prev[0:R], prev[0:R], p[0:R], ALU.subtract))
                chain(nc.gpsimd.tensor_tensor(prev[0:R], prev[0:R], mu[0:R], ALU.mult))
                pool.wait_ge(s["out_ready"], ONE + t)
                nc.gpsimd.tensor_tensor(ps[0:R], prev[0:R], p[0:R], ALU.add).then_inc(s["mixed"], 1)
                pool.wait_ge(s["mixed"], ONE + t + 1)
                nc.gpsimd.tensor_tensor(kk[0:R], ps[0:R, W:2 * W], vec["k_k"][0:R], ALU.mult).then_inc(s["kk_scaled"], 1)
                pool.wait_ge(s["masked"], ONE + 2 * t + 1)
                for n in range(SLEVELS if smp else LEVELS):
                    last = nc.gpsimd.tensor_tensor(
                        heads(ML[0:R, n, :]), AB[0:R, :, 0, :],
                        lev[0:R, n, :].unsqueeze(1).broadcast_to([R, RH, CH]), ALU.mult)
                    if n == 0:
                        last.then_inc(s["level_masks"], 1)
                last.then_inc(s["level_masks"], 1)
                pool.wait_ge(s["rk_ready"], ONE + t + 1)
                chain(nc.gpsimd.tensor_tensor(bon[0:R], ps[0:R, 0:W], k2[0:R], ALU.mult))
                nc.gpsimd.tensor_tensor(bon[0:R], bon[0:R], vec["r_k"][0:R], ALU.mult).then_inc(s["bonus_in"], 1)
                chain.end()

            times(body)(pool)

        @block.tensor
        def _(pe):
            pe.wait_ge(s["const_in"], ONE + 16 * NCONST)

            def body(t, R, smp):
                G = 1 if smp else 2
                pe.wait_ge(s["state_ready"], ONE + 2 * t)
                pe.wait_ge(s["y_centered"], ONE + t)
                pe.wait_ge(s["lo_sig"], ONE + t + 1)
                for n in range(2):
                    last = nc.tensor.transpose(PS[:, 4, n * P:n * P + R], lo[0:R, n * P:(n + 1) * P], ident[0:R, 0:R])
                last.then_inc(s["lo_turned"], 1)
                pe.wait_ge(s["lo_copied"], ONE + t + 1)
                nc.tensor.matmul(PS[0:R, 0, :], loT[0:64, 0, 0:R], wa_up[0:64, :], start=True, stop=True)
                nc.tensor.matmul(PS[0:R, 1, :], loT[64:128, 0, 0:R], wa_up[64:128, :], start=True, stop=True)
                nc.tensor.matmul(PS[0:R, 2, :], loT[:, 1, 0:R], g_up[:], start=True, stop=True).then_inc(s["lora_done"], 1)
                pe.wait_ge(s["lw_ready"], ONE + t + 1)
                nc.tensor.matmul(PS[0:R, 3, :], cum_l[smp][0:R, 0:R], lw[0:R, :], start=True, stop=True)
                NS = SB if smp else 4
                for n in range(NPAIR):
                    last = nc.tensor.matmul(PS[:, 4, 256 + n * NS:256 + (n + 1) * NS], lw[0:R, n * P:(n + 1) * P],
                                            tot[smp][0:R, :], start=True, stop=True)
                last.then_inc(s["cum_done"], 1)
                pe.wait_ge(s["scaled_ready"], ONE + t + 1)
                pe.wait_ge(s["bef_exp"], ONE + t + 1)
                pe.wait_ge(s["za_ready"], ONE + t + 1)
                pe.wait_ge(s["g_copied"], ONE + t + 1)
                for n, src in enumerate((kq, rt, bt, kt)):
                    for pr in range(NPAIR):
                        last = nc.tensor.transpose(PS[:, n, pr * P:pr * P + R], src[0:R, pr * P:(pr + 1) * P],
                                                   ident[0:R, 0:R])
                    last.then_inc(s["turned_ready"], 1)
                pe.wait_ge(s["turned_copied"], ONE + 4 * t + 4)
                carry(pe, s["carrier"])
                for n in range(2):
                    for h in range(RH):
                        hp = slice(64 * (h % 2), 64 * (h % 2) + 64)
                        for c in range(G):
                            tok = slice(c * CH, (c + 1) * CH)
                            dst = PS[c * CH:(c + 1) * CH, 4 + 2 * n + h % 2, (h // 2) * P:(h // 2 + 1) * P]
                            last = nc.tensor.matmul(dst.rearrange("p (k t) -> p k t", k=2), bkT[hp, n, h // 2, tok],
                                                    qrT[hp, :, h // 2, tok], start=True, stop=True)
                    last.then_inc(s["pair_done"], 1)
                NL = SLEVELS if smp else LEVELS
                tl = t * (LEVELS)
                for n in range(NL):
                    if n == 0:
                        pe.wait_ge(s["level_masks"], ONE + 2 * t + 1)
                    else:
                        pe.wait_ge(s["level_masks"], ONE + 2 * t + 2)
                        pe.wait_ge(s["t_ready"], ONE + tl + n)
                    carry(pe, s["carrier"])
                    for h in range(RH):
                        for c in range(G):
                            cp = slice(c * CH, (c + 1) * CH)
                            rhs = eye[cp, :] if n == 0 else Tn[cp, h, :]
                            last = nc.tensor.matmul(PS[cp, 0, h * CH:(h + 1) * CH], heads(ML[:, n, :])[cp, h, :], rhs,
                                                    start=True, stop=True)
                    last.then_inc(s["x_done"], 1)
                    if n == 0:
                        continue
                    pe.wait_ge(s["x_copied"], ONE + t * (LEVELS - 1) + n)
                    carry(pe, s["carrier"])
                    for h in range(RH):
                        for c in range(G):
                            cp = slice(c * CH, (c + 1) * CH)
                            if n < NL - 1:
                                nc.tensor.matmul(PS[cp, 1, h * CH:(h + 1) * CH], Tt[cp, h, :], X[cp, h, :],
                                                 start=True, stop=True)
                            last = nc.tensor.matmul(PS[cp, 2, h * CH:(h + 1) * CH], X[cp, h, :], Tt[cp, h, :],
                                                    start=True, stop=True)
                    last.then_inc(s["y_done"], 1)
                pe.wait_ge(s["t_ready"], ONE + tl + NL)
                pe.wait_ge(s["masked"], ONE + 2 * t + 2)
                for c in range(G):
                    u = 2 * t + c
                    cp = slice(c * CH, (c + 1) * CH)
                    pe.wait_ge(s["sp_ready"], ONE + u + 1)
                    for h in range(RH):
                        hc = slice(h * CH, (h + 1) * CH)
                        if h % 2 == 0:
                            from_state(0, h // 2, cp, PS[cp, 3, h * CH:(h + 2) * CH], smp)
                        last = nc.tensor.matmul(PS[cp, 3, hc], AK[cp, h, 0, :], ps[cp, 2 * W + h * RD:2 * W + (h + 1) * RD],
                                                start=False, stop=True, skip_group_check=True)
                    last.then_inc(s["r_done"], 1)
                    for h in range(RH):
                        hc = slice(h * CH, (h + 1) * CH)
                        vh = ps[cp, 2 * W + h * RD:2 * W + (h + 1) * RD]
                        if h == 0:
                            pe.wait_ge(s["r_copied"], ONE + u + 1)
                            carry(pe, s["carrier"])
                            for i in range(RH):
                                last = nc.tensor.matmul(PS[cp, 4, i * CH:(i + 1) * CH], Tt[cp, i, :],
                                                        R_[cp, i * CH:(i + 1) * CH], start=True, stop=True)
                            last.then_inc(s["sa_done"], 1)
                            pe.wait_ge(s["sa_copied"], ONE + u + 1)
                        if h % 2 == 0:
                            from_state(1, h // 2, cp, PS[cp, 5, h * CH:(h + 2) * CH], smp)
                        nc.tensor.matmul(PS[cp, 5, hc], AK[cp, h, 1, :], vh, start=False, stop=False,
                                         skip_group_check=True)
                        last = nc.tensor.matmul(PS[cp, 5, hc], AB[cp, h, 1, :], SA[cp, hc], start=False, stop=True,
                                                skip_group_check=True)
                    last.then_inc(s["yy_done"], 1)
                    if not smp:
                        for h in range(RH):
                            hp = slice(64 * (h % 2), 64 * (h % 2) + 64)
                            hc = slice(h * CH, (h + 1) * CH)
                            dst = PS[hp, 6, (h // 2) * RD:(h // 2 + 1) * RD]
                            nc.tensor.matmul(dst, bt[cp, hc], SA[cp, hc], start=True, stop=False)
                            last = nc.tensor.matmul(dst, kt[cp, hc], ps[cp, 2 * W + h * RD:2 * W + (h + 1) * RD],
                                                    start=False, stop=True)
                        last.then_inc(s["st_done"], 1)
                        continue
                    for n, src in enumerate((bt, kt)):
                        pe.wait_ge(s["big_ready"], ONE + 1 + n)
                        for h in range(RH):
                            hp = slice(64 * (h % 2), 64 * (h % 2) + 64)
                            last = nc.tensor.matmul(PS[hp, SBANK[h // 2], :], src[cp, h * RD:(h + 1) * RD],
                                                    big[cp, h, :, :].rearrange("p b i -> p (b i)"),
                                                    start=(n == 0), stop=(n == 1), skip_group_check=True)
                        last.then_inc(s["st_done"], 1)

            def from_state(n, pr, cp, dst, smp):
                if not smp:
                    nc.tensor.matmul(dst, qrT[:, n, pr, cp], Sp[:, pr].rearrange("p k i -> p (k i)"), start=True,
                                     stop=False, skip_group_check=True)
                    return
                for b in range(SB):
                    nc.tensor.matmul(dst, big[:, n * NPAIR + pr, b, :], sdiag[:, pr, b].rearrange("p k i -> p (k i)"),
                                     start=(b == 0), stop=False, skip_group_check=True)

            times(body)(pe)

        @block.scalar
        def _(act):
            act.wait_ge(s["eps_set"], ONE + 1)
            gn_eps = hs[:, 7, 0:1]
            act.wait_ge(s["chain"], ONE + 1)

            def body(t, R, smp):
                G = 1 if smp else 2
                act.wait_ge(s["mixed"], ONE + t + 1)
                nc.scalar.activation(lo[0:R, 0:64], ps[0:R, 3 * W:3 * W + 64], ACT.Tanh)
                nc.scalar.activation(lo[0:R, 64:128], ps[0:R, 3 * W + 64:3 * W + 128], ACT.Copy)
                nc.scalar.activation(lo[0:R, 128:256], ps[0:R, 3 * W + 128:3 * W + 256], ACT.Tanh,
                                     scale=0.5).then_inc(s["lo_ready"], 1)
                act.wait_ge(s["kk_scaled"], ONE + t + 1)
                nc.scalar.activation(sq[0:R], kk[0:R], ACT.Square).then_inc(s["kk_squared"], 1)
                act.wait_ge(s["lo_turned"], ONE + t + 1)
                nc.scalar.activation(loT[:, :, 0:R], PS[:, 4, 0:256].rearrange("p (n t) -> p n t", n=2)[:, :, 0:R],
                                     ACT.Copy).then_inc(s["lo_copied"], 1)
                act.wait_ge(s["z_ready"], ONE + t + 1)
                nc.scalar.activation(z[0:R], z[0:R], ACT.Exp, scale=-1.0).then_inc(s["z_exp"], 1)
                act.wait_ge(s["za_ready"], ONE + t + 1)
                nc.scalar.activation(a[0:R], a[0:R], ACT.Tanh, scale=0.5).then_inc(s["a_tanh"], 1)
                nc.scalar.activation(g[0:R], PS[0:R, 2, :], ACT.Copy).then_inc(s["g_copied"], 1)
                act.wait_ge(s["cum_done"], ONE + t + 1)
                nc.scalar.activation(e_in[0:R], PS[0:R, 3, :], ACT.Exp)
                nc.scalar.activation(e_out[0:R], PS[0:R, 3, :], ACT.Exp, scale=-1.0)
                NS = SB if smp else 4
                nc.scalar.activation(ep[:, :, 0:NS], PS[:, 4, 256:256 + NPAIR * NS].rearrange("p (n k) -> p n k", n=NPAIR),
                                     ACT.Exp).then_inc(s["e_ready"], 1)
                act.wait_ge(s["bef_ready"], ONE + t + 1)
                nc.scalar.activation(e_bef[0:R], e_bef[0:R], ACT.Exp).then_inc(s["bef_exp"], 1)
                act.wait_ge(s["kk_sum"], ONE + t + 1)
                nc.scalar.activation(hs[0:R, 1, :], hs[0:R, 0, :], ACT.Sqrt).then_inc(s["kk_root"], 1)
                for n in range(4):
                    dst = (qrT, bkT)[n // 2][:, n % 2, :, 0:R]
                    act.wait_ge(s["turned_ready"], ONE + 4 * t + n + 1)
                    nc.scalar.activation(dst, PS[:, n, :].rearrange("p (n t) -> p n t", n=NPAIR)[:, :, 0:R],
                                         ACT.Copy).then_inc(s["turned_copied"], 1)
                for n in range(1, SLEVELS if smp else LEVELS):
                    act.wait_ge(s["x_done"], ONE + t * LEVELS + n + 1)
                    nc.scalar.activation(X[0:R], heads(PS[0:R, 0, :]), ACT.Copy).then_inc(s["x_copied"], 1)
                for c in range(G):
                    u = 2 * t + c
                    cp = slice(c * CH, (c + 1) * CH)
                    act.wait_ge(s["r_done"], ONE + u + 1)
                    nc.scalar.activation(R_[cp], PS[cp, 3, :], ACT.Copy, scale=-1.0).then_inc(s["r_copied"], 1)
                    act.wait_ge(s["sa_done"], ONE + u + 1)
                    nc.scalar.activation(SA[cp], PS[cp, 4, :], ACT.Copy).then_inc(s["sa_copied"], 1)
                act.wait_ge(s["y_centered"], ONE + t + 1)
                nc.scalar.activation(sq[0:R], yc[0:R], ACT.Square).then_inc(s["y_squared"], 1)
                act.wait_ge(s["y_sum"], ONE + t + 1)
                nc.scalar.activation(hs[0:R, 4, :], hs[0:R, 3, :], ACT.Sqrt, bias=gn_eps[0:R],
                                     scale=1.0 / RD).then_inc(s["y_root"], 1)

            times(body)(act)

        @block.vector
        def _(dve):
            nc.vector.memset(hs[:, 7, :], GN_EPS).then_inc(s["chain"], 1)
            nc.vector.memset(Sp[:], 0.0)
            nc.vector.memset(state[:], 0.0).then_inc(s["chain"], 1)
            dve.wait_ge(s["chain"], ONE + 2)
            dve.wait_ge(s["const_in"], ONE + 16 * NCONST)
            K = 19

            def spread(ap, R):
                return ap.unsqueeze(2).broadcast_to([R, RH, RD])

            def body(t, R, smp):
                G = 1 if smp else 2
                chain = CountedChain(dve, s["chain"], t, K)
                chain.n = chain.n + 2
                v = ps[0:R, 2 * W:3 * W]
                dve.wait_ge(s["lo_ready"], ONE + t + 1)
                nc.vector.tensor_scalar(lo[0:R, 128:256], lo[0:R, 128:256], 0.5, 0.5, ALU.mult,
                                        ALU.add).then_inc(s["lo_sig"], 1)
                dve.wait_ge(s["kk_squared"], ONE + t + 1)
                nc.vector.reduce_sum(hs[0:R, 0, :], heads(sq[0:R]), axis=AX_X).then_inc(s["kk_sum"], 1)
                dve.wait_ge(s["lora_done"], ONE + t + 1)
                nc.vector.tensor_tensor(z[0:R], PS[0:R, 0, :], vec["w0"][0:R], ALU.add).then_inc(s["z_ready"], 1)
                nc.vector.tensor_tensor(a[0:R], PS[0:R, 1, :], vec["a0"][0:R], ALU.add).then_inc(s["za_ready"], 1)
                dve.wait_ge(s["z_exp"], ONE + t + 1)
                chain(nc.vector.tensor_scalar(z[0:R], z[0:R], 1.0, None, ALU.add))
                chain(nc.vector.reciprocal(z[0:R], z[0:R]))
                nc.vector.tensor_scalar(lw[0:R], z[0:R], -float(np.exp(-0.5)), None, ALU.mult).then_inc(s["lw_ready"], 1)
                dve.wait_ge(s["a_tanh"], ONE + t + 1)
                chain(nc.vector.tensor_scalar(a[0:R], a[0:R], 0.5, 0.5, ALU.mult, ALU.add))
                chain(nc.vector.scalar_tensor_tensor(k2[0:R], a[0:R], 1.0, vec["k_a"][0:R], ALU.subtract, ALU.mult))
                nc.vector.scalar_tensor_tensor(k2[0:R], k2[0:R], 1.0, ps[0:R, W:2 * W], ALU.add,
                                               ALU.mult).then_inc(s["rk_ready"], 1)
                dve.wait_ge(s["e_ready"], ONE + t + 1)
                dve.wait_ge(s["lw_ready"], ONE + t + 1)
                nc.vector.tensor_tensor(e_bef[0:R], PS[0:R, 3, :], lw[0:R], ALU.subtract).then_inc(s["bef_ready"], 1)
                dve.wait_ge(s["kk_root"], ONE + t + 1)
                chain(nc.vector.tensor_scalar(hs[0:R, 1, :], hs[0:R, 1, :], 1e-12, None, ALU.max))
                chain(nc.vector.reciprocal(hs[0:R, 2, :], hs[0:R, 1, :]))
                chain(nc.vector.tensor_tensor(heads(kk[0:R]), heads(kk[0:R]), spread(hs[0:R, 2, :], R), ALU.mult))
                chain(nc.vector.tensor_tensor(bb[0:R], kk[0:R], a[0:R], ALU.mult))
                dve.wait_ge(s["bef_exp"], ONE + t + 1)
                nc.vector.tensor_tensor(kq[0:R], kk[0:R], e_bef[0:R], ALU.mult)
                nc.vector.tensor_tensor(rt[0:R], ps[0:R, 0:W], e_in[0:R], ALU.mult)
                nc.vector.tensor_tensor(bt[0:R], bb[0:R], e_out[0:R], ALU.mult)
                dve.wait_ge(s["rk_ready"], ONE + t + 1)
                nc.vector.tensor_tensor(kt[0:R], k2[0:R], e_out[0:R], ALU.mult).then_inc(s["scaled_ready"], 1)
                for n, dst in enumerate((AB, AK)):
                    dve.wait_ge(s["pair_done"], ONE + 2 * t + n + 1)
                    for i in range(2):
                        last = nc.vector.tensor_tensor(
                            dst[0:R, i::2].rearrange("p h k t -> p h (k t)"),
                            PS[0:R, 4 + 2 * n + i, :].rearrange("p (h k) -> p h k", h=4),
                            tri[smp][0:R].rearrange("p k t -> p (k t)").unsqueeze(1).broadcast_to([R, 4, 2 * CH]),
                            ALU.mult)
                    last.then_inc(s["masked"], 1)
                eyeb = eye[0:R].unsqueeze(1).broadcast_to([R, RH, CH])
                NL = SLEVELS if smp else LEVELS
                dve.wait_ge(s["level_masks"], ONE + 2 * t + 1)
                nc.vector.tensor_tensor(Tt[0:R], eyeb, heads(ML[0:R, 0, :]), ALU.subtract)
                dve.wait_ge(s["x_done"], ONE + t * LEVELS + 1)
                nc.vector.tensor_tensor(Tn[0:R], eyeb, heads(PS[0:R, 0, :]), ALU.subtract).then_inc(s["t_ready"], 1)
                for n in range(1, NL):
                    dve.wait_ge(s["t_ready"], ONE + t * LEVELS + n)
                    dve.wait_ge(s["y_done"], ONE + t * (LEVELS - 1) + n)
                    if n < NL - 1:
                        nc.vector.tensor_tensor(Tn[0:R], Tn[0:R], heads(PS[0:R, 1, :]), ALU.subtract)
                    nc.vector.tensor_tensor(Tt[0:R], Tt[0:R], heads(PS[0:R, 2, :]), ALU.subtract).then_inc(s["t_ready"], 1)
                if not smp:
                    for c in range(G):
                        u = 2 * t + c
                        for i in range(2):
                            half = slice(64 * i, 64 * i + 64)
                            last = nc.vector.tensor_tensor(
                                Sp[half, :, i, :], state[half], ep[half, :, 2 * c:2 * c + 1].broadcast_to(
                                    [64, NPAIR, RD]), ALU.mult)
                        last.then_inc(s["sp_ready"], 1)
                        dve.wait_ge(s["sp_ready"], ONE + u + 1)
                        dve.wait_ge(s["st_done"], ONE + u + 1)
                        for i in range(2):
                            half = slice(64 * i, 64 * i + 64)
                            last = nc.vector.tensor_tensor(state[half], Sp[half, :, i, :],
                                                           PS[half, 6, 0:NPAIR * RD].rearrange(
                                                               "p (n i) -> p n i", n=NPAIR), ALU.add)
                        chain(last)
                        nc.vector.tensor_tensor(state[:], state[:], ep[:, :, 2 * c + 1:2 * c + 2].broadcast_to(
                            [P, NPAIR, RD]), ALU.mult).then_inc(s["state_ready"], 1)
                        dve.wait_ge(s["state_ready"], ONE + u + 1)
                else:
                    dve.wait_ge(s["turned_copied"], ONE + 4 * t + 4)
                    dve.wait_ge(s["sstate_in"], ONE + 32)
                    for n in range(2):
                        for pr in range(NPAIR):
                            last = nc.vector.tensor_tensor(
                                big[:, n * NPAIR + pr], qrT[:, n, pr, 0:R].unsqueeze(1).broadcast_to([P, SB, CH]),
                                seq_of[:], ALU.mult)
                    last.then_inc(s["sp_ready"], 1)
                    for n in range(2):
                        if n == 0:
                            dve.wait_ge(s["sa_copied"], ONE + 2 * t + 1)
                            dve.wait_ge(s["yy_done"], ONE + 2 * t + 1)
                            dve.wait_ge(s["sp_ready"], ONE + 2 * t + 1)
                        else:
                            dve.wait_ge(s["st_done"], ONE + 2 * t + 1)
                        src = SA[0:R] if n == 0 else v
                        for h in range(RH):
                            last = nc.vector.tensor_tensor(
                                big[0:R, h], src[:, h * RD:(h + 1) * RD].unsqueeze(1).broadcast_to([R, SB, RD]),
                                seq_row[0:R].unsqueeze(2).broadcast_to([R, SB, RD]), ALU.mult)
                        last.then_inc(s["big_ready"], 1)
                        dve.wait_ge(s["big_ready"], ONE + 1 + n)
                    dve.wait_ge(s["st_done"], ONE + 2 * t + 2)
                    for pr in range(NPAIR):
                        last = nc.vector.tensor_tensor(sstate[:, pr], sstate[:, pr], PS[:, SBANK[pr], :].rearrange(
                            "p (b i) -> p b i", b=SB), ALU.add)
                    chain(last)
                    for pr in range(NPAIR):
                        last = nc.vector.tensor_tensor(sstate[:, pr], sstate[:, pr],
                                                       ep[:, pr, :].unsqueeze(2).broadcast_to([P, SB, RD]), ALU.mult)
                    last.then_inc(s["state_ready"], 1)
                dve.wait_ge(s["yy_done"], ONE + 2 * t + G)
                yp = heads(PS[0:R, 5, :])
                chain(nc.vector.reduce_sum(hs[0:R, 5, :], yp, axis=AX_X))
                chain(nc.vector.tensor_scalar(hs[0:R, 5, :], hs[0:R, 5, :], 1.0 / RD, None, ALU.mult))
                nc.vector.tensor_tensor(heads(yc[0:R]), yp, spread(hs[0:R, 5, :], R), ALU.subtract).then_inc(s["y_centered"], 1)
                dve.wait_ge(s["y_squared"], ONE + t + 1)
                nc.vector.reduce_sum(hs[0:R, 3, :], heads(sq[0:R]), axis=AX_X).then_inc(s["y_sum"], 1)
                dve.wait_ge(s["bonus_in"], ONE + t + 1)
                chain(nc.vector.reduce_sum(hs[0:R, 6, :], heads(bon[0:R]), axis=AX_X))
                dve.wait_ge(s["out_stored"], ONE + 16 * t)
                chain(nc.vector.tensor_tensor(heads(out[0:R]), heads(v), spread(hs[0:R, 6, :], R), ALU.mult))
                chain(nc.vector.tensor_tensor(out[0:R], out[0:R], vec["ln_b"][0:R], ALU.add))
                dve.wait_ge(s["y_root"], ONE + t + 1)
                chain(nc.vector.reciprocal(hs[0:R, 5, :], hs[0:R, 4, :]))
                chain(nc.vector.tensor_tensor(heads(yc[0:R]), heads(yc[0:R]), spread(hs[0:R, 5, :], R), ALU.mult))
                chain(nc.vector.tensor_tensor(yc[0:R], yc[0:R], vec["ln_w"][0:R], ALU.mult))
                chain(nc.vector.tensor_tensor(out[0:R], out[0:R], yc[0:R], ALU.add))
                nc.vector.tensor_tensor(out[0:R], out[0:R], g[0:R], ALU.mult).then_inc(s["out_ready"], 1)
                chain.end(smp)

            times(body)(dve)

def out_projection(nc, T):
    with ExitStack() as ctx:
        m = Mem(nc, ctx, "op")
        w = m.sb("w", [P, KD, D])
        ident = m.sb("ident", [P, P])
        mx = [m.sb(f"mixed{i}", [P, D]) for i in range(2)]
        x = [m.sb(f"x{i}", [P, D]) for i in range(2)]
        mT = m.sb("mT", [P, KD, P])
        h = [m.sb(f"h{i}", [P, D]) for i in range(2)]
        zero = m.sb("zero", [P, D])
        psT = m.ps("psT", [P, KD, P])
        psO = [m.ps(f"psO{i}", [P, D]) for i in range(2)]
        ident_in = m.sem("ident_in")
        w_in = m.sem("w_in")
        tile_in = [m.sem(f"tile_in{i}") for i in range(2)]
        zeroed = m.sem("zeroed")
        zero_stored = m.sem("zero_stored")
        turned = m.sem("turned")
        copied = m.sem("copied")
        summed = m.sem("summed")
        added = m.sem("added")
        stored = m.sem("stored")
        block = ctx.enter_context(nc.Block())

        def tiles(body):
            for t in range(NT):
                body(t, t % 2, P if t < PT else SROWS)

        @block.sync
        def _(sp):
            sp.dma_start(ident[:], T["ident"]).then_inc(ident_in, 16)

            def load(t, i, R):
                if t >= 2:
                    sp.wait_ge(turned, t - 1)
                    sp.wait_ge(added, t - 1)
                sp.dma_start(mx[i][0:R], T["mixed"][t * P:t * P + R, :]).then_inc(tile_in[i], 16)
                sp.dma_start(x[i][0:R], T["x"][t * P:t * P + R, :]).then_inc(tile_in[i], 16)
                if t == 0:
                    for k in range(KD):
                        sp.dma_start(w[:, k, :], T["w_out"][k * P:(k + 1) * P, :]).then_inc(w_in, 16)
                if t:
                    store(t - 1, 1 - i, P)

            def store(t, i, R):
                sp.wait_ge(added, t + 1)
                sp.dma_start(T["h"][t * P:t * P + R, :], h[i][0:R]).then_inc(stored, 16)

            tiles(load)
            store(PT, 0, SROWS)
            sp.wait_ge(zeroed, 1)
            sp.dma_start(T["h"][SEQ + SROWS:ROWS, :], zero[0:P - SROWS]).then_inc(zero_stored, 16)
            sp.wait_ge(stored, 16 * NT)
            sp.wait_ge(zero_stored, 16)

        @block.gpsimd
        def _(pool):
            nc.gpsimd.memset(zero[:], 0.0).then_inc(zeroed, 1)

        @block.tensor
        def _(pe):
            pe.wait_ge(ident_in, 16)

            def turn(t, i, R):
                pe.wait_ge(tile_in[i], 32 * (t // 2 + 1))
                pe.wait_ge(copied, t)
                for k in range(KD):
                    last = nc.tensor.transpose(psT[:, k, 0:R], mx[i][0:R, k * P:(k + 1) * P], ident[0:R, 0:R])
                last.then_inc(turned, 1)

            def product(t, i, R):
                pe.wait_ge(copied, t + 1)
                if t >= 2:
                    pe.wait_ge(added, t - 1)
                if t == 0:
                    pe.wait_ge(w_in, 16 * KD)
                for j in range(2):
                    for k in range(KD):
                        last = nc.tensor.matmul(psO[i][0:R, j * 512:(j + 1) * 512], mT[:, k, 0:R],
                                                w[:, k, j * 512:(j + 1) * 512], start=(k == 0), stop=(k == KD - 1))
                last.then_inc(summed, 1)

            tiles(lambda t, i, R: (turn(t, i, R), product(t, i, R)))

        @block.scalar
        def _(act):
            def copy(t, i, R):
                act.wait_ge(turned, t + 1)
                act.wait_ge(summed, t)
                nc.scalar.activation(mT[:, :, 0:R], psT[:, :, 0:R], ACT.Copy).then_inc(copied, 1)

            tiles(copy)

        @block.vector
        def _(dve):
            def add(t, i, R):
                dve.wait_ge(summed, t + 1)
                if t >= 2:
                    dve.wait_ge(stored, 16 * (t - 1))
                dve.wait_ge(tile_in[i], 32 * (t // 2 + 1))
                nc.vector.tensor_tensor(h[i][0:R], psO[i][0:R], x[i][0:R], ALU.add).then_inc(added, 1)

            tiles(add)

def peer(nc, T):
    NBUF = 8
    AHEAD = 2
    RING = 4
    LAST = NT - 1
    QW = 2 * NK
    with ExitStack() as ctx:
        m = Mem(nc, ctx, "pe")
        wq = m.sb("wq", [P, KD, PH * QW])
        keys = m.sb("keys", [P, PH, 2, NK])
        buf = [m.sb(f"buf{b}", [P, 2 * D]) for b in range(NBUF)]
        hb = [m.sb(f"h{i}", [P, D]) for i in range(2)]
        hn = [m.sb(f"hn{i}", [P, D]) for i in range(2)]
        hnT = m.sb("hnT", [P, KD, P])
        gf = m.sb("gf", [P, D])
        gy = m.sb("gy", [P, D])
        y = m.sb("y", [P, D])
        y_sq = m.sb("y_sq", [P, D])
        ident = m.sb("ident", [P, P])
        iota = m.sb("iota", [P, TOPK])
        diag = m.sb("diag", [P, NBUF, P])
        q = m.sb("q", [P, QW])
        qT = m.sb("qT", [P, 2, P])
        top = m.sb("top", [P, 2, TOPK])
        topi = m.sb("topi", [P, 2, TOPK], U32)
        topf = m.sb("topf", [P, 2, TOPK])
        left = m.sb("left", [P, 2, NK])
        cand = m.sb("cand", [P, TOPK, TOPK])
        cleft = m.sb("cleft", [P, TOPK * TOPK])
        best = m.sb("best", [P, TOPK])
        besti = m.sb("besti", [P, TOPK], U32)
        part = m.sb("part", [P, 2, TOPK], U32)
        partf = m.sb("partf", [P, 2, TOPK])
        hit = m.sb("hit", [P, TOPK, 2 * TOPK])
        row = m.sb("row", [P, 2, TOPK])
        ex = m.sb("ex", [P, TOPK])
        sm = m.sb("sm", [P, 4])
        gate = m.sb("gate", [P, RING, TOPK])
        expert = m.sb("expert", [P, RING, TOPK], U32)
        dot = m.sb("dot", [P, 2, TOPK])
        act_v = m.sb("act", [P, 2, TOPK])
        wgt = m.sb("wgt", [P, 2, TOPK])
        st = m.sb("st", [P, 8])
        psO = m.ps("psO", [P, D])
        psT = m.ps("psT", [P, KD, P])
        psQ = m.ps("psQ", [P, 512])
        psQT = m.ps("psQT", [P, 512])
        psS = m.ps("psS", [P, 512])

        wq_in = m.sem("wq_in")
        const_in = m.sem("const_in")
        h_in = [m.sem(f"h_in{i}") for i in range(2)]
        eps_set = m.sem("eps_set")
        h_summed = m.sem("h_summed")
        h_root = m.sem("h_root")
        tile_chain = m.sem("tile_chain")
        hn_ready = m.sem("hn_ready")
        hn_turned = m.sem("hn_turned")
        hnT_ready = m.sem("hnT_ready")
        q_done = m.sem("q_done")
        q_copied = m.sem("q_copied")
        qT_done = m.sem("qT_done")
        qT_copied = m.sem("qT_copied")
        scores_done = m.sem("scores_done")
        scores_read = m.sem("scores_read")
        topk_chain = m.sem("topk_chain")
        best_ready = m.sem("best_ready")
        exp_done = m.sem("exp_done")
        chosen = m.sem("chosen")
        gathered = [m.sem(f"gathered{b}") for b in range(NBUF)]
        dotted = m.sem("dotted")
        gelu_done = m.sem("gelu_done")
        wgt_ready = m.sem("wgt_ready")
        diag_ready = m.sem("diag_ready")
        buffer_free = m.sem("buffer_free")
        started = m.sem("started")
        out_done = m.sem("out_done")
        out_copied = m.sem("out_copied")
        y_root = m.sem("y_root")
        y_summed = m.sem("y_summed")
        y_chain = m.sem("y_chain")
        y_ready = m.sem("y_ready")
        y_stored = m.sem("y_stored")
        block = ctx.enter_context(nc.Block())

        KT, KU, KY = 1, 18, 1
        SLOTS = PH * TOPK

        def h_count(t, par):
            return 16 * (t // 2 + 1)

        def tiles(tile):
            for t in range(NT):
                tile(t, t % 2, P if t < LAST else SROWS)

        def slots(t):
            return [(n // TOPK, n % TOPK, n) for n in range(SLOTS)]

        def chooses(t, h):
            return not (t == LAST and h + AHEAD >= PH)

        def has_next(t):
            return t < LAST

        def has_last(t):
            return t > 0

        @block.sync
        def _(sp):
            sp.dma_start(hb[0][:], T["h"][0:P, :]).then_inc(h_in[0], 16)
            sp.dma_start(ident[:], T["ident"]).then_inc(const_in, 16)
            sp.dma_start(gf[:], T["ffn_norm"].partition_broadcast(P)).then_inc(const_in, 16)
            for k in range(KD):
                sp.dma_start(wq[:, k, :], T["peer_wq"][k * P:(k + 1) * P, :]).then_inc(wq_in, 16)
            sp.dma_start(iota[:], T["iota16"].partition_broadcast(P)).then_inc(const_in, 16)
            sp.dma_start(keys[:], T["sub_keys"]).then_inc(const_in, 16)
            sp.dma_start(gy[:], T["final_norm"].partition_broadcast(P)).then_inc(const_in, 16)

            def tile(t, par, R):
                if has_next(t):
                    sp.wait_ge(started, t + 1)
                    sp.dma_start(hb[1 - par][:], T["h"][rows(t + 1), :]).then_inc(h_in[1 - par], 16)
                if has_last(t):
                    store(t - 1, P)

            def store(t, R):
                sp.wait_ge(y_ready, t + 1)
                sp.dma_start(T["y_all"][rows(t, R), :], y[0:R, :]).then_inc(y_stored, 16)

            tiles(tile)
            store(LAST, SROWS)
            sp.wait_ge(y_stored, 16 * NT)

        @block.gpsimd
        def _(pool):
            nc.gpsimd.memset(st[:, 7:8], EPS).then_inc(eps_set, 1)

            def tile(t, par, R):
                for h, s, n in slots(t):
                    if s == 0:
                        pool.wait_ge(chosen, t * PH + h + 1)
                    b = n % NBUF
                    pool.wait_ge(buffer_free, t * SLOTS + n + 1)
                    pool.indirect_dma_start(buf[b][0:R, :], None, T["experts"],
                                            bass.IndirectOffsetOnAxis(ap=expert[0:R, h % RING, s:s + 1], axis=0)
                                            ).then_inc(gathered[b], 16)

            tiles(tile)

        @block.tensor
        def _(pe):
            pe.sem_inc(buffer_free, NBUF)
            pe.wait_ge(const_in, 80)

            def turn_hn(t, par):
                pe.wait_ge(hn_ready, t + 1)
                for k in range(KD):
                    last = nc.tensor.transpose(psT[:, k, :], hn[par][:, k * P:(k + 1) * P], ident[:])
                last.then_inc(hn_turned, 1)

            def query(u, h):
                if h == 0:
                    pe.wait_ge(hnT_ready, u // PH + 1)
                pe.wait_ge(q_copied, u)
                for k in range(KD):
                    last = nc.tensor.matmul(psQ[:, 0:QW], hnT[:, k, :], wq[:, k, h * QW:(h + 1) * QW],
                                            start=(k == 0), stop=(k == KD - 1))
                last.then_inc(q_done, 1)

            def turn_q(u):
                pe.wait_ge(q_copied, u + 1)
                pe.wait_ge(qT_copied, u)
                for c in range(2):
                    last = nc.tensor.transpose(psQT[:, c * P:(c + 1) * P], q[:, c * P:(c + 1) * P], ident[:])
                last.then_inc(qT_done, 1)

            def scores(u, h):
                pe.wait_ge(qT_copied, u + 1)
                pe.wait_ge(scores_read, u)
                for c in range(2):
                    last = nc.tensor.matmul(psS[:, c * NK:(c + 1) * NK], qT[:, c, :], keys[:, h, c, :],
                                            start=True, stop=True)
                last.then_inc(scores_done, 1)

            turn_hn(0, 0)
            pe.wait_ge(wq_in, 16 * KD)
            for u in range(AHEAD):
                query(u, u)
                turn_q(u)
                scores(u, u)

            def tile(t, par, R):
                pe.wait_ge(h_in[par], h_count(t, par))
                pe.wait_ge(out_copied, t)
                for j in range(2):
                    last = nc.tensor.matmul(psO[0:R, j * 512:(j + 1) * 512], ident[0:R, 0:R],
                                            hb[par][0:R, j * 512:(j + 1) * 512], start=True, stop=False,
                                            skip_group_check=True)
                last.then_inc(started, 1)
                for h, s, n in slots(t):
                    u, hu = t * PH + h + AHEAD, (h + AHEAD) % PH
                    if chooses(t, h) and s == 0:
                        query(u, hu)
                    if chooses(t, h) and s == 2:
                        turn_q(u)
                    if chooses(t, h) and s == 4:
                        scores(u, hu)
                    if has_next(t) and (h, s) == (PH - AHEAD - 1, 8):
                        turn_hn(t + 1, 1 - par)
                    b = n % NBUF
                    pe.wait_ge(diag_ready, t * SLOTS + n + 1)
                    for j in range(2):
                        last = nc.tensor.matmul(psO[0:R, j * 512:(j + 1) * 512], diag[0:R, b, 0:R],
                                                buf[b][0:R, D + j * 512:D + (j + 1) * 512],
                                                start=False, stop=False, skip_group_check=True)
                    last.then_inc(buffer_free, 1)

            tiles(tile)

        @block.scalar
        def _(act):
            act.wait_ge(eps_set, 1)

            def norm_h(t, par):
                act.wait_ge(h_in[par], h_count(t, par))
                act.wait_ge(hn_ready, t)
                nc.scalar.activation(y_sq[:], hb[par][:], ACT.Square, accum_out=st[:, 0:1]).then_inc(h_summed, 1)
                act.wait_ge(h_summed, t + 1)
                nc.scalar.activation(st[:, 1:2], st[:, 0:1], ACT.Sqrt, bias=st[:, 7:8],
                                     scale=1.0 / D).then_inc(h_root, 1)

            def copy_q(u):
                act.wait_ge(q_done, u + 1)
                act.wait_ge(qT_done, u)
                nc.scalar.activation(q[:], psQ[:, 0:QW], ACT.Copy).then_inc(q_copied, 1)

            def copy_qT(u):
                act.wait_ge(qT_done, u + 1)
                act.wait_ge(scores_done, u)
                nc.scalar.activation(qT[:].rearrange("p c t -> p (c t)"), psQT[:, 0:QW], ACT.Copy).then_inc(qT_copied, 1)

            def exp_best(u):
                act.wait_ge(best_ready, u + 1)
                nc.scalar.activation(ex[:], best[:], ACT.Exp, bias=sm[:, 0:1],
                                     accum_out=sm[:, 1:2]).then_inc(exp_done, 1)

            def copy_out(t, R):
                act.wait_ge(buffer_free, NBUF + (t + 1) * SLOTS)
                act.wait_ge(y_stored, 16 * t)
                nc.scalar.activation(y[0:R, :], psO[0:R, :], ACT.Copy).then_inc(out_copied, 1)

            def norm_y(t, R):
                act.wait_ge(out_copied, t + 1)
                nc.scalar.activation(y_sq[0:R, :], y[0:R, :], ACT.Square, accum_out=st[0:R, 3:4]).then_inc(y_summed, 1)
                act.wait_ge(y_summed, t + 1)
                nc.scalar.activation(st[0:R, 4:5], st[0:R, 3:4], ACT.Sqrt, bias=st[0:R, 7:8],
                                     scale=1.0 / D).then_inc(y_root, 1)

            norm_h(0, 0)
            for u in range(AHEAD):
                copy_q(u)
                copy_qT(u)
                exp_best(u)

            def tile(t, par, R):
                if has_last(t):
                    copy_out(t - 1, P)
                for h, s, n in slots(t)[::2]:
                    u = t * PH + h + AHEAD
                    r = h % 2
                    if chooses(t, h) and s == 0:
                        copy_q(u)
                    if chooses(t, h) and s == 2:
                        copy_qT(u)
                    if chooses(t, h) and s == TOPK - 2:
                        exp_best(u)
                    if has_last(t) and (h, s) == (1, 4):
                        norm_y(t - 1, P)
                    if has_next(t) and (h, s) == (PH - AHEAD - 3, 8):
                        norm_h(t + 1, 1 - par)
                    act.wait_ge(dotted, t * SLOTS + n + 2)
                    nc.scalar.activation(act_v[0:R, r, s:s + 2], dot[0:R, r, s:s + 2],
                                         ACT.Gelu_apprx_tanh).then_inc(gelu_done, 1)
                    act.wait_ge(wgt_ready, t * (SLOTS // 2) + n // 2 + 1)
                    for i in range(2):
                        nc.scalar.activation(diag[0:R, (n + i) % NBUF, 0:R], ident[0:R, 0:R], ACT.Copy,
                                             scale=wgt[0:R, r, s + i:s + i + 1]).then_inc(diag_ready, 1)
            tiles(tile)
            copy_out(LAST, SROWS)
            norm_y(LAST, SROWS)

        @block.vector
        def _(dve):
            dve.wait_ge(const_in, 80)

            def make_hn(t, par):
                chain = Chain(dve, tile_chain, t * KT)
                dve.wait_ge(h_root, t + 1)
                chain(nc.vector.reciprocal(st[:, 2:3], st[:, 1:2]))
                nc.vector.scalar_tensor_tensor(hn[par][:], hb[par][:], st[:, 2:3], gf[:], ALU.mult,
                                               ALU.mult).then_inc(hn_ready, 1)

            def copy_hnT(t):
                dve.wait_ge(hn_turned, t + 1)
                nc.vector.tensor_copy(hnT[:], psT[:]).then_inc(hnT_ready, 1)

            def choose(fu, h):
                chain = Chain(dve, topk_chain, fu * KU)

                def first(c):
                    src = psS[:, c * NK:(c + 1) * NK]
                    if c == 0:
                        dve.wait_ge(scores_done, fu + 1)
                    chain(nc.vector.max(top[:, c, 0:8], src))
                    nc.vector.max_index(topi[:, c, 0:8], top[:, c, 0:8], src)
                    chain(nc.vector.match_replace(left[:, c, :], top[:, c, 0:8], src, -3e38))
                    chain(nc.vector.max(top[:, c, 8:16], left[:, c, :]))
                    last = nc.vector.max_index(topi[:, c, 8:16], top[:, c, 8:16], left[:, c, :])
                    if c == 1:
                        last.then_inc(scores_read, 1)
                        dve.wait_ge(scores_read, fu + 1)

                def second():
                    chain(nc.vector.tensor_copy(topf[:], topi[:]))
                    chain(nc.vector.tensor_tensor(cand[:], top[:, 0, :].unsqueeze(2).broadcast_to([P, TOPK, TOPK]),
                                                  top[:, 1, :].unsqueeze(1).broadcast_to([P, TOPK, TOPK]), ALU.add))
                    flat = cand[:].rearrange("p a b -> p (a b)")
                    chain(nc.vector.max(best[:, 0:8], flat))
                    nc.vector.max_index(besti[:, 0:8], best[:, 0:8], flat)
                    chain(nc.vector.match_replace(cleft[:], best[:, 0:8], flat, -3e38))
                    chain(nc.vector.max(best[:, 8:16], cleft[:]))
                    chain(nc.vector.max_index(besti[:, 8:16], best[:, 8:16], cleft[:]))
                    nc.vector.tensor_scalar(sm[:, 0:1], best[:, 0:1], -1.0, None, ALU.mult).then_inc(best_ready, 1)

                def places():
                    nc.vector.tensor_scalar(part[:, 0, :], besti[:], 4, None, ALU.logical_shift_right)
                    chain(nc.vector.tensor_scalar(part[:, 1, :], besti[:], 15, None, ALU.bitwise_and))
                    chain(nc.vector.tensor_copy(partf[:], part[:]))
                    for c in range(2):
                        last = nc.vector.tensor_tensor(hit[:, :, c * TOPK:(c + 1) * TOPK],
                                                partf[:, c, :].unsqueeze(2).broadcast_to([P, TOPK, TOPK]),
                                                iota[:].unsqueeze(1).broadcast_to([P, TOPK, TOPK]), ALU.is_equal)
                    chain(last)
                    for c in range(2):
                        last = nc.vector.tensor_tensor(hit[:, :, c * TOPK:(c + 1) * TOPK],
                                                hit[:, :, c * TOPK:(c + 1) * TOPK],
                                                topf[:, c, :].unsqueeze(1).broadcast_to([P, TOPK, TOPK]), ALU.mult)
                    chain(last)
                    for c in range(2):
                        last = nc.vector.reduce_sum(row[:, c, :], hit[:, :, c * TOPK:(c + 1) * TOPK], axis=AX_X)
                    chain(last)

                def finish():
                    dve.wait_ge(exp_done, fu + 1)
                    chain(nc.vector.reciprocal(sm[:, 2:3], sm[:, 1:2]))
                    nc.vector.scalar_tensor_tensor(expert[:, h % RING, :], row[:, 0, :], float(NK),
                                                   row[:, 1, :], ALU.mult, ALU.add)
                    nc.vector.tensor_scalar(gate[:, h % RING, :], ex[:], sm[:, 2:3], None,
                                            ALU.mult).then_inc(chosen, 1)
                    dve.wait_ge(chosen, fu + 1)

                return first, second, places, finish

            make_hn(0, 0)
            copy_hnT(0)
            for u in range(AHEAD):
                first, second, places, finish = choose(u, u)
                first(0)
                first(1)
                second()
                places()
                finish()

            def weigh(t, h, s, n, R):
                r = h % 2
                dve.wait_ge(gelu_done, t * (SLOTS // 2) + n // 2 + 1)
                nc.vector.tensor_tensor(wgt[0:R, r, s:s + 2], act_v[0:R, r, s:s + 2],
                                        gate[0:R, h % RING, s:s + 2], ALU.mult).then_inc(wgt_ready, 1)

            def norm_y(t, R):
                chain = Chain(dve, y_chain, t * KY)
                dve.wait_ge(y_root, t + 1)
                chain(nc.vector.reciprocal(st[0:R, 5:6], st[0:R, 4:5]))
                nc.vector.scalar_tensor_tensor(y[0:R, :], y[0:R, :], st[0:R, 5:6], gy[0:R, :], ALU.mult,
                                               ALU.mult).then_inc(y_ready, 1)

            def tile(t, par, R):
                for h, s, n in slots(t):
                    if s == 0 and chooses(t, h):
                        first, second, places, finish = choose(t * PH + h + AHEAD, (h + AHEAD) % PH)
                    b = n % NBUF
                    dve.wait_ge(gathered[b], 16 * (t * (SLOTS // NBUF) + n // NBUF + 1))
                    nc.vector.tensor_tensor_reduce(buf[b][0:R, 0:D], buf[b][0:R, 0:D], hn[par][0:R, :], 1.0, 0.0,
                                                   ALU.mult, ALU.add, dot[0:R, h % 2, s:s + 1]).then_inc(dotted, 1)
                    if s % 2 == 0 and n >= 2:
                        weigh(t, (n - 2) // TOPK, (n - 2) % TOPK, n - 2, R)
                    if chooses(t, h):
                        if s == 6:
                            first(0)
                        if s == 8:
                            first(1)
                        if s == 10:
                            second()
                        if s == 12:
                            places()
                        if s == TOPK - 1:
                            if n == SLOTS - 1:
                                weigh(t, h, s - 1, n - 1, R)
                            finish()
                    elif n == SLOTS - 1:
                        weigh(t, h, s - 1, n - 1, R)
                    if has_last(t) and (h, s) == (1, 10):
                        norm_y(t - 1, P)
                    if has_next(t) and (h, s) == (PH - AHEAD - 3, 14):
                        make_hn(t + 1, 1 - par)
                    if has_next(t) and (h, s) == (PH - AHEAD - 1, 14):
                        copy_hnT(t + 1)

            tiles(tile)
            norm_y(LAST, SROWS)

def host_arrays(inputs):
    x = np.zeros((ROWS, D), np.float32)
    x[:SEQ] = np.asarray(inputs["x_prompt"]).reshape(SEQ, D)
    x[SEQ:SEQ + SROWS] = np.asarray(inputs["x_sample"]).reshape(SROWS, D)
    a = {"x": x}
    for name in ("cache_k", "cache_v"):
        c = np.asarray(inputs[name])
        a[name] = np.ascontiguousarray(c.reshape(-1, H * VD))
    for name in ("attn_norm", "w_in", "w_out", "da_lambda_q1", "da_lambda_k1", "da_lambda_q2", "da_lambda_k2",
                 "da_subln", "rw_mu", "rw_w0", "rw_w_up", "rw_a0", "rw_a_up", "rw_g_up", "rw_k_k", "rw_k_a",
                 "rw_ln_w", "rw_ln_b", "ffn_norm", "peer_wq"):
        a[name] = np.ascontiguousarray(np.asarray(inputs[name])[0])
    for name in ("attn_norm",):
        a[name] = np.ascontiguousarray(a[name].reshape(KD, P).T)
    a["final_norm"] = np.ascontiguousarray(inputs["final_norm"])
    a["rw_r_k"] = np.ascontiguousarray(np.asarray(inputs["rw_r_k"]).reshape(RW))
    a["sub_keys"] = np.ascontiguousarray(np.asarray(inputs["peer_sub_keys"])[0].transpose(3, 0, 1, 2))
    a["experts"] = np.concatenate([np.asarray(inputs["peer_u"])[0], np.asarray(inputs["peer_v"])[0]], axis=1)
    a["page_table"] = np.ascontiguousarray(np.asarray(inputs["page_table"]).reshape(1, SB * NPAGE).astype(np.int32))
    s = np.asarray(inputs["state_wkv"])[0]
    a["state"] = np.ascontiguousarray(s.reshape(SB, RH // 2, 2, RD, RD).transpose(2, 4, 1, 0, 3).reshape(P, RH // 2, SB, RD))
    diag = np.zeros((P, RH // 2, SB, 2, RD), np.float32)
    for i in range(2):
        diag[i * RD:(i + 1) * RD, :, :, i] = a["state"][i * RD:(i + 1) * RD]
    a["state_diag"] = diag
    a["shift"] = np.ascontiguousarray(np.asarray(inputs["state_shift"])[0])
    a["ident"] = np.eye(P, dtype=np.float32)
    a["iota16"] = np.arange(TOPK, dtype=np.float32)
    at = np.arange(P)
    a["causal"] = np.where(at[None, :] <= at[:, None], 0.0, NEG).astype(np.float32)
    step, use = at % ST, at % 32 < 16
    a["new_mask"] = np.where(np.arange(ST)[None, :] <= step[:, None], 0.0, NEG).astype(np.float32)
    a["coef"] = np.stack([at % 32 < 8, use & (at % 32 >= 8)], axis=1).astype(np.float32)
    a["pick"] = (use[:, None] & ((at // 32 * ST + step)[:, None] == np.arange(4 * ST)[None, :])).astype(np.float32)
    a["prow"] = at[:, None].astype(np.float32)
    s_, t_ = at[:, None], at[None, :]
    same = s_ // CH == t_ // CH
    a["eye"] = np.concatenate([np.eye(CH)] * 2).astype(np.float32)
    a["cum_p"] = (same * ((s_ <= t_).astype(np.float32) - (s_ % CH < CH // 2))).astype(np.float32)
    a["cum_s"] = ((s_ // ST == t_ // ST) & (s_ <= t_)).astype(np.float32)
    quarter = at // (CH // 2)
    a["tot_p"] = (quarter[:, None] == np.arange(4)[None, :]).astype(np.float32)
    a["tot_s"] = (at[:, None] // ST == np.arange(SB)[None, :]).astype(np.float32)
    sc, tc = at[:, None] % CH, np.arange(CH)[None, :]
    a["tri_p"] = np.stack([sc < tc, sc <= tc], axis=1).astype(np.float32)
    one = sc // ST == tc // ST
    a["tri_s"] = np.stack([one & (sc < tc), one & (sc <= tc)], axis=1).astype(np.float32)
    a["levels"] = np.stack([(sc >> (n + 1) == tc >> (n + 1)) & (sc >> n & 1 == 0) & (tc >> n & 1 == 1)
                            for n in range(6)], axis=1).astype(np.float32)
    a["seq_of"] = np.broadcast_to((np.arange(CH)[None, :] // ST == np.arange(SB)[:, None])[None], (P, SB, CH)).astype(np.float32)
    a["seq_row"] = a["tot_s"]
    pos = np.zeros(ROWS, np.float32)
    pos[:SEQ] = np.arange(SEQ)
    pos[SEQ:SEQ + SROWS] = PAST + np.tile(np.arange(ST), SB)
    inv = np.float32(10000.0) ** (-np.arange(32, dtype=np.float32) / np.float32(32))
    ang = pos[:, None] * inv[None, :].astype(np.float32)
    cos, sin = np.cos(ang).astype(np.float32), np.sin(ang).astype(np.float32)
    a["rope"] = np.stack([cos, cos, -sin, sin], axis=1)
    return a

CONSTS = ("ident", "rope", "causal", "new_mask", "coef", "pick", "prow", "iota16", "eye", "cum_p", "cum_s", "tot_p",
          "tot_s", "tri_p", "tri_s", "levels", "seq_of", "seq_row")


def layer(nc, T):
    for stage in (in_projection, attention, time_mixing, out_projection, peer):
        with nc.cleanup_on_exit():
            stage(nc, T)


OUTS = {"y_all": (ROWS, D), "k_all": (ROWS, QK), "v_all": (ROWS, H * VD), "p_all": (ROWS, RP),
        "wkv_p": (P, RH // 2, RD), "wkv_s": (P, RH // 2, SB, RD)}
SCRATCH = {"q": (ROWS, QK), "mixed": (ROWS, D), "h": (ROWS, D)}


def kernel(**inputs):
    import concourse.bacc as bacc
    from concourse.bass_utils import run_bass_kernel_spmd

    nc = bacc.Bacc("TRN2", target_bir_lowering=False, num_devices=1)
    a = host_arrays(inputs)
    T, arrays = {}, {}
    for name, v in a.items():
        arrays[f"in_{name}"] = v
        T[name] = nc.dram_tensor(f"in_{name}", v.shape, mybir.dt.from_np(v.dtype), kind="ExternalInput").ap()
    for name, shape in OUTS.items():
        T[name] = nc.dram_tensor(f"out_{name}", shape, F32, kind="ExternalOutput").ap()
    for name, shape in SCRATCH.items():
        T[name] = nc.dram_tensor(f"scratch_{name}", shape, F32, kind="Internal").ap()
    layer(nc, T)
    r = run_bass_kernel_spmd(nc, [arrays], core_ids=[0]).results[0]
    y, k, v, p, wp, ws = (r[f"out_{n}"] for n in OUTS)
    end = SEQ + SROWS
    state = ws.reshape(2, RD, RH // 2, SB, RD).transpose(3, 2, 0, 4, 1).reshape(1, SB, RH, RD, RD)
    return (y[:SEQ].reshape(1, SEQ, D), y[SEQ:end].reshape(SB, ST, D),
            k[:SEQ].reshape(1, 1, SEQ, H, 2 * HD), v[:SEQ].reshape(1, 1, SEQ, H, VD),
            wp.reshape(2, RD, RH // 2, RD).transpose(2, 0, 3, 1).reshape(1, 1, RH, RD, RD),
            p[SEQ - 1].reshape(1, 1, RP),
            k[SEQ:end].reshape(1, SB, ST, H, 2 * HD), v[SEQ:end].reshape(1, SB, ST, H, VD),
            state, p[SEQ + ST - 1:end:ST].reshape(1, SB, RP))
```
